# Optimizing a Trainium2 kernel written in Bass

```python
import jax, jax.numpy as jnp
from jax import lax
import numpy as np

D_MODEL = 1024
BATCH = 1
SEQ = 256
DEPTH = 1
DEC_BATCH = 8
DEC_SEQ = 1
PAST_LEN = 2048
PAGE_SIZE = 128

D_CONV = D_MODEL // 2
CONV_GROUPS = 4
CONV_WIDTH = 3
D_REC = D_MODEL // 2
N_REC_HEADS = 4
HEAD_K = D_REC // N_REC_HEADS
HEAD_V = D_REC // N_REC_HEADS
D_MIX = D_CONV + D_REC
CHUNK = 64
N_META = 16
N_EXPERTS = 32
TOP_K = 4
D_FF = D_MODEL
SWIGLU_LIMIT = 7.0
SWIGLU_ALPHA = 1.702
EPS = 1e-5
SPLIT_SIZES = (D_CONV, D_CONV, D_CONV, D_REC, D_REC, D_REC, D_REC)
SPLIT_POINTS = tuple(int(p) for p in np.cumsum(SPLIT_SIZES)[:-1])
D_IN = sum(SPLIT_SIZES)

kernel_name = "hymba_conv_hgrn2_moe_step"

def _rmsnorm(x, g):
    xf = x.astype(jnp.float32)
    out = xf * lax.rsqrt(jnp.mean(xf * xf, axis=-1, keepdims=True) + EPS)
    return (out * g.astype(jnp.float32)).astype(x.dtype)

def _gla_chunk(S0, q, k, v, logf):
    b = jnp.cumsum(logf.astype(jnp.float32), axis=2)
    C = q.shape[2]
    causal = jnp.tril(jnp.ones((C, C), dtype=bool))
    diff = b[:, :, :, None, :] - b[:, :, None, :, :]
    decay = jnp.exp(jnp.where(causal[:, :, None], diff, -jnp.inf))
    scores = jnp.einsum('bhtk,bhsk,bhtsk->bhts', q, k, decay)
    o = (jnp.einsum('bhts,bhsv->bhtv', scores, v)
         + jnp.einsum('bhtk,bhkv->bhtv', q * jnp.exp(b), S0))
    b_last = b[:, :, -1:, :]
    S_new = (jnp.exp(b_last[:, :, 0, :])[..., None] * S0
             + jnp.einsum('bhsk,bhsv->bhkv', k * jnp.exp(b_last - b), v))
    return S_new.astype(S0.dtype), o.astype(q.dtype)

def _gla_scan(S0, q, k, v, logf, chunk):
    Bn, H, T, _ = q.shape
    n = T // chunk

    def split(a):
        return jnp.moveaxis(a.reshape(Bn, H, n, chunk, a.shape[-1]), 2, 0)

    def step(S, xs):
        return _gla_chunk(S, *xs)

    S, o = lax.scan(step, S0, (split(q), split(k), split(v), split(logf)))
    return S, jnp.moveaxis(o, 0, 2).reshape(Bn, H, T, -1)

def _token_mixers(u, conv_buf, S0, conv_w, lb, rec_gain, segments):
    Bn, T, _ = u.shape
    bg, cg, hv, q, fx, iv, og = jnp.split(u, SPLIT_POINTS, axis=-1)
    bx = bg * hv
    xp = jnp.concatenate([conv_buf.astype(bx.dtype), bx], axis=1)
    conv = sum(conv_w[j] * xp[:, j:j + T] for j in range(CONV_WIDTH))
    y_conv = cg * conv
    new_buf = xp[:, T:]
    f = lb.astype(u.dtype) + (1 - lb.astype(u.dtype)) * jax.nn.sigmoid(fx)
    logf = jnp.log(f)
    kk = 1 - f

    def heads(a, d):
        return a.reshape(Bn, T, N_REC_HEADS, d).transpose(0, 2, 1, 3)

    qh, kh, vh, lfh = heads(q, HEAD_K), heads(kk, HEAD_K), heads(iv, HEAD_V), heads(logf, HEAD_K)
    S = S0
    outs = []
    start = 0
    for length, chunk in segments:
        sl = slice(start, start + length)
        S, o = _gla_scan(S, qh[:, :, sl], kh[:, :, sl], vh[:, :, sl], lfh[:, :, sl], chunk)
        outs.append(o)
        start += length
    o = jnp.concatenate(outs, axis=2)
    of = o.astype(jnp.float32)
    o = (of * lax.rsqrt(jnp.mean(of * of, axis=-1, keepdims=True) + EPS)).astype(u.dtype)
    o = o.transpose(0, 2, 1, 3).reshape(Bn, T, D_REC)
    y_rec = o * rec_gain * jax.nn.silu(og)
    return jnp.concatenate([y_conv, y_rec], axis=-1), new_buf, S

def _moe(x, router_w, router_b, w1, b1, w2, b2):
    logits = x.astype(jnp.float32) @ router_w.astype(jnp.float32) + router_b.astype(jnp.float32)
    top_logits, top_idx = lax.top_k(logits, TOP_K)
    gates = jax.nn.softmax(top_logits, axis=-1)
    combine = jnp.einsum('tk,tke->te', gates,
                         jax.nn.one_hot(top_idx, N_EXPERTS, dtype=jnp.float32)).astype(x.dtype)
    out = jnp.zeros_like(x)
    for e in range(N_EXPERTS):
        a = x @ w1[e] + b1[e]
        glu = jnp.minimum(a[:, ::2], SWIGLU_LIMIT)
        lin = jnp.clip(a[:, 1::2], -SWIGLU_LIMIT, SWIGLU_LIMIT)
        act = glu * jax.nn.sigmoid(SWIGLU_ALPHA * glu) * (lin + 1)
        out = out + combine[:, e:e + 1] * (act @ w2[e] + b2[e])
    return out

def setup_inputs(seed: int = 0) -> dict:
    key = jax.random.key(seed)
    ks = jax.random.split(key, 20)
    f32 = jnp.float32
    nrm = lambda k, shape, s: jax.random.normal(k, shape, f32) * s
    return {
        "x_prompt": nrm(ks[0], (BATCH, SEQ, D_MODEL), 1.0),
        "x_sample": nrm(ks[1], (DEC_BATCH, DEC_SEQ, D_MODEL), 1.0),
        "state_conv": nrm(ks[2], (DEPTH, DEC_BATCH, CONV_WIDTH - 1, D_CONV), 1.0),
        "state_rec": nrm(ks[3], (DEPTH, DEC_BATCH, N_REC_HEADS, HEAD_K, HEAD_V), 0.5),
        "meta_tokens": nrm(ks[4], (N_META, D_MODEL), 1.0),
        "norm_mix": 1.0 + nrm(ks[5], (DEPTH, D_MODEL), 0.02),
        "w_in": nrm(ks[6], (DEPTH, D_MODEL, D_IN), D_MODEL ** -0.5),
        "conv_w": nrm(ks[7], (DEPTH, CONV_WIDTH, D_CONV), CONV_WIDTH ** -0.5),
        "rec_lower_bound": nrm(ks[8], (DEPTH + 1, D_REC), 0.1),
        "rec_norm": 1.0 + nrm(ks[9], (DEPTH, D_REC), 0.02),
        "w_out": nrm(ks[10], (DEPTH, D_MIX, D_MODEL), D_MIX ** -0.5),
        "norm_ffn": 1.0 + nrm(ks[11], (DEPTH, D_MODEL), 0.02),
        "router_w": nrm(ks[12], (DEPTH, D_MODEL, N_EXPERTS), D_MODEL ** -0.5),
        "router_b": nrm(ks[13], (DEPTH, N_EXPERTS), 0.01),
        "expert_w1": nrm(ks[14], (DEPTH, N_EXPERTS, D_MODEL, 2 * D_FF), D_MODEL ** -0.5),
        "expert_b1": nrm(ks[15], (DEPTH, N_EXPERTS, 2 * D_FF), 0.01),
        "expert_w2": nrm(ks[16], (DEPTH, N_EXPERTS, D_FF, D_MODEL), D_FF ** -0.5),
        "expert_b2": nrm(ks[17], (DEPTH, N_EXPERTS, D_MODEL), 0.01),
        "norm_final": 1.0 + nrm(ks[18], (D_MODEL,), 0.02),
    }

def reference(x_prompt, x_sample, state_conv, state_rec, meta_tokens, norm_mix, w_in,
              conv_w, rec_lower_bound, rec_norm, w_out, norm_ffn, router_w, router_b,
              expert_w1, expert_b1, expert_w2, expert_b2, norm_final):
    Bp = x_prompt.shape[0]
    meta = jnp.broadcast_to(meta_tokens.astype(x_prompt.dtype), (Bp, N_META, D_MODEL))
    h_p = jnp.concatenate([meta, x_prompt], axis=1)
    h_s = x_sample
    lb_all = jnp.cumsum(jax.nn.softmax(rec_lower_bound.astype(jnp.float32), axis=0), axis=0)
    conv_p_l, rec_p_l, conv_s_l, rec_s_l = [], [], [], []
    for l in range(DEPTH):
        Lp = h_p.shape[1]
        Bs, Ls = h_s.shape[0], h_s.shape[1]
        n_p = Bp * Lp
        tok = jnp.concatenate([h_p.reshape(-1, D_MODEL), h_s.reshape(-1, D_MODEL)], axis=0)
        u = _rmsnorm(tok, norm_mix[l]) @ w_in[l]
        u_p = u[:n_p].reshape(Bp, Lp, D_IN)
        u_s = u[n_p:].reshape(Bs, Ls, D_IN)
        zero_buf = jnp.zeros((Bp, CONV_WIDTH - 1, D_CONV), u.dtype)
        zero_S = jnp.zeros((Bp, N_REC_HEADS, HEAD_K, HEAD_V), u.dtype)
        y_p, cb_p, S_p = _token_mixers(u_p, zero_buf, zero_S, conv_w[l], lb_all[l], rec_norm[l],
                                       ((N_META, N_META), (Lp - N_META, CHUNK)))
        y_s, cb_s, S_s = _token_mixers(u_s, state_conv[l], state_rec[l], conv_w[l], lb_all[l],
                                       rec_norm[l], ((Ls, Ls),))
        conv_p_l.append(cb_p)
        rec_p_l.append(S_p)
        conv_s_l.append(cb_s)
        rec_s_l.append(S_s)
        mix = jnp.concatenate([y_p.reshape(-1, D_MIX), y_s.reshape(-1, D_MIX)], axis=0) @ w_out[l]
        h_p = h_p + mix[:n_p].reshape(Bp, Lp, D_MODEL)
        h_s = h_s + mix[n_p:].reshape(Bs, Ls, D_MODEL)
        if l == DEPTH - 1:
            h_p = h_p[:, N_META:]
        n_p = h_p.shape[0] * h_p.shape[1]
        tok = jnp.concatenate([h_p.reshape(-1, D_MODEL), h_s.reshape(-1, D_MODEL)], axis=0)
        ff = _moe(_rmsnorm(tok, norm_ffn[l]), router_w[l], router_b[l],
                  expert_w1[l], expert_b1[l], expert_w2[l], expert_b2[l])
        h_p = h_p + ff[:n_p].reshape(h_p.shape)
        h_s = h_s + ff[n_p:].reshape(h_s.shape)
    y_prompt = _rmsnorm(h_p, norm_final)
    y_sample = _rmsnorm(h_s, norm_final)
    new_conv_prompt = jnp.stack(conv_p_l, axis=0)
    new_rec_prompt = jnp.stack(rec_p_l, axis=0)
    new_conv_sample = jnp.stack(conv_s_l, axis=0)
    new_rec_sample = jnp.stack(rec_s_l, axis=0)
    return (y_prompt, y_sample, new_conv_prompt, new_rec_prompt, new_conv_sample, new_rec_sample)


_drawn_inputs = setup_inputs


def setup_inputs(seed=0):
    import zlib

    import numpy as np

    out = dict(_drawn_inputs(seed))
    spreads = {}
    factors = {'rec_norm': 2.934,
     'expert_b1': 8.0,
     'expert_b2': 8.0,
     'norm_final': 8.447,
     'router_b': 3.802}
    for name, (base, spread) in spreads.items():
        noise = np.random.default_rng([zlib.crc32(name.encode()), seed]).standard_normal(out[name].shape)
        drawn = base * np.exp(spread * noise) if base else spread * noise
        out[name] = __import__('jax').numpy.asarray(drawn.astype(out[name].dtype))
    for name, factor in factors.items():
        out[name] = (out[name] * factor).astype(out[name].dtype)
    return out
```

```python
import concourse.bass as bass
from concourse import mybir
from contextlib import ExitStack

F32 = mybir.dt.float32
BF16 = mybir.dt.bfloat16
U32 = mybir.dt.uint32
I32 = mybir.dt.int32
ALU = mybir.AluOpType
ACT = mybir.ActivationFunctionType
AX = mybir.AxisListType

P = 128
D = 1024
KT = D // P
HALF = D // 2
NS, NM, NP = 8, 16, 256
S0C, P0C = 0, NS + NM
TOK = NS + NM + NP
NT = NP + NS
HEADS = 4
E = 32
TOPK = 4
CAP = 64
PASSES = -(-NT // CAP)
PAD_ROW = 2 * NT
ROWS = PAD_ROW + P
LEVELS = 7
ROUTE = 8
EPS = 1e-5
LIMIT = 7.0
ALPHA = 1.702
BG, CG, HV, QG, FX, IV, OG = range(7)
TILE_COL = [P0C, P0C + P, 0]
TILE_ROWS = [P, P, NS + NM]


def bcast(ap, shape):
    return ap.to_broadcast(shape)


def build_step(nc, x_prompt, x_sample, state_conv, state_rec, meta_tokens, norm_mix, w_in, conv_w,
               rec_lower_bound, rec_norm, w_out, norm_ffn, router_w, router_b, expert_w1, expert_b1,
               expert_w2, expert_b2, norm_final,
               y_prompt, y_sample, new_conv_prompt, new_rec_prompt, new_conv_sample, new_rec_sample):
    hn_table = nc.dram_tensor("hn_table", [ROWS, HALF], F32).ap()
    sum_table = nc.dram_tensor("sum_table", [ROWS, HALF], F32).ap()
    hn_rows = hn_table.rearrange("(t a) n -> t (a n)", a=2)
    sum_rows = sum_table.rearrange("(t a) n -> t (a n)", a=2)

    ctx = ExitStack()
    with ctx:
        def sem(name):
            return ctx.enter_context(nc.semaphore(name))

        w1r = ctx.enter_context(nc.sbuf_tensor("w1r", [P, 8, 2048], F32))
        w2r = ctx.enter_context(nc.sbuf_tensor("w2r", [P, 8, 2048], F32))
        ARENA = 20440
        mem = ctx.enter_context(nc.sbuf_tensor("mem", [P, ARENA], F32))
        top = [0]

        def take(n):
            a = top[0]
            top[0] += n
            assert top[0] <= ARENA, top[0]
            return mem[:, a:a + n]


        ident = take(P)
        prefix = take(P)
        strict = take(P)
        suffix = take(P)
        spans = take(LEVELS * P)
        blocks = take(LEVELS * P)
        gains = take(24)
        small = take(P)
        router_sb = take(KT * E)
        lb2 = take(2 * 512)
        xT = take(KT * TOK)
        kk = take(3 * 512)
        logf = take(3 * 512)
        vtok = take(3 * 512)
        sog = take(2 * 512)
        kk_meta = take(512)
        qC = take(2 * 512)
        kkC = take(2 * 512)
        qS = take(HEADS * 32)
        kS = take(HEADS * NS)
        qhat = take(2 * 512)
        srec = take(2 * 512)
        bx = take(4 * TOK)
        ctmp = take(TOK)
        cT = take(4 * 2 * NS)
        nconv = take(4 * (2 + 2 * NS))
        yT = take(KT * TOK)

        def cut(ap, n):
            return ap.rearrange("p (a n) -> p a n", n=n)

        def from_(ap, n, at=0):
            return mem[:, ap.offset + at:ap.offset + at + n]

        spans3, blocks3 = cut(spans, P), cut(blocks, P)
        lb3, xT3, kk3, logf3, vtok3, sog3 = cut(lb2, 512), cut(xT, TOK), cut(kk, 512), cut(logf, 512), cut(vtok, 512), cut(sog, 512)
        qC3, kkC3, qS3, kS3, qhat3, srec3 = cut(qC, 512), cut(kkC, 512), cut(qS, 32), cut(kS, NS), cut(qhat, 512), cut(srec, 512)
        bx3, yT3, router3 = cut(bx, TOK), cut(yT, TOK), cut(router_sb, E)
        cT4 = cT.rearrange("p (g b i) -> p g b i", g=4, i=2)
        nconv3 = cut(nconv, 2 + 2 * NS)
        gmix, gconv, grec = gains[:, 0:8], gains[:, 8:20], gains[:, 20:24]
        ssq, rstd = small[:, 0:3], small[:, 3:6]
        ossq, orstd = small[:, 6:15], small[:, 15:24]
        hssq, hrstd = small[:, 24:27], small[:, 27:30]
        fssq, frstd = small[:, 30:33], small[:, 33:36]
        eps_col = small[:, 36:37]
        meta_row = small[:, 37:38]
        rbrow = small[0:1, 40:72]
        maxcount = small[:, 72:73]
        maxcount_i = small[:, 73:74].bitcast(I32)
        pad_at = small[:, 74:75]
        unpad = small[:, 75:76]
        tok_col = small[:, 76:77]
        upper = small[:, 91:92]
        decay_all = small[:, 80:88]
        hi = w2r[:, 4:6, :].rearrange("p a n -> p (a n)")
        lo = w2r[:, 6:8, :].rearrange("p a n -> p (a n)")
        x3 = cut(hi[:, 0:3072], D)
        xn3 = cut(lo[:, 0:3072], D)
        gain_rows = lo[0:24, 3072:3200]
        ex3 = cut(hi[:, 0:1024], 512)
        wl3 = cut(hi[:, 1024:2048], 512)
        sc3 = cut(hi[:, 2048:3072], 512)
        vdiag = hi[0:NS, 3072:4096]
        s0 = lo.rearrange("p (h b v) -> p h b v", h=HEADS, b=NS)
        ftmp3 = cut(yT[:, 0:1536], 512)
        lbtmp = yT[:, 1536:2048]
        tail3 = cut(yT[:, 1120:2144], 512)
        fS3 = cut(lb2[:, 256:256 + HEADS * NS], NS)
        ssum = from_(srec, 1024)
        hs_tmp = from_(qC, 512)[0:NS, :]
        crow = qhat[0:2 * NS, 0:512]
        ncrow = lb2[0:2 + 2 * NS, 512:1024]
        sogS, oS = lb2[:, 0:128], lb2[:, 128:256]
        h3 = cut(from_(kk, 3 * D), D)
        hn3 = cut(from_(vtok, 3 * D), D)
        hnT3 = cut(xT[:, 0:KT * NT], NT)
        gffn = lb2
        b2_sb = bx[0:E, 0:D]
        route = from_(spans, 2 * LEVELS * P)
        logits3 = cut(route[:, 0:96], E)
        top8 = cut(route[:, 96:120], 8)
        idx8 = cut(route[:, 120:144].bitcast(U32), 8)
        idxf = cut(route[:, 144:168], 8)
        gate4 = cut(route[:, 168:180], TOPK)
        gsum = route[:, 180:183]
        comb3 = cut(route[:, 192:288], E)
        member3 = cut(route[:, 288:384], E)
        posm3 = cut(route[:, 384:480], E)
        iota32 = route[:, 480:512]
        iota64 = route[:, 512:576]
        slotf = cut(route[:, 576:576 + E * 2], 2)
        slot_gate = route[:, 640:672]
        slot_row = route[:, 672:704].bitcast(U32)
        gather_at = route[:, 704:706].bitcast(U32)
        scatter_at = route[:, 706:708].bitcast(U32)
        row_valid = route[:, 708:711]
        vals = cut(route[:, 720:720 + 288].bitcast(BF16), 6)
        gres = cut(route[:, 1008:1104], E)
        combT = route[0:E, 1104:1104 + NT]
        ones = route[:, 1392:1392 + P]
        slotv = cut(route[:, 1520:1520 + 6 * ROUTE], 6)
        eq_all = from_(qhat, 3 * TOPK * E).rearrange("p (i j e) -> p i j e", i=3, j=TOPK)
        onehot = from_(qhat, 2 * 3 * ROUTE * CAP // 2).bitcast(BF16).rearrange(
            "p (k i e s) -> p k i e s", k=2, i=3, e=ROUTE)
        xg3 = cut(from_(qC, 2 * HALF), HALF)
        xgT4 = from_(lb2, 2 * HALF).rearrange("p (k c s) -> p k c s", k=2, c=4)
        b1r3 = [from_(yT, 2048)[0:1, :], from_(xT, 2048)[0:1, :]]
        glu, sig, lin, act = [from_(vtok, 512, 512 * n) for n in range(4)]
        actT4 = from_(vtok, 2 * HALF, 2048).rearrange("p (k c s) -> p k c s", k=2, c=4)
        ysb3 = cut(from_(kk, 2 * HALF), HALF)
        fin3 = cut(w1r[:, 0:2, :].rearrange("p a n -> p (a n)")[:, 0:3072], D)
        gfin = w1r[:, 2, 0:D]
        fsq = w1r[:, 3, 0:D]

        ps = ctx.enter_context(nc.psum_tensor("ps", [P, 8, 512], F32))
        psA = ps[:, 0:2, :].rearrange("p a n -> p (a n)")

        x_in, gain_in, lb_in, crow_in, s0_in, const_in, xres_in, gffn_in, b2_in, gfin_in, fin_in = [
            sem(n) for n in ("x_in", "gain_in", "lb_in", "crow_in", "s0_in", "const_in", "xres_in",
                             "gffn_in", "b2_in", "gfin_in", "fin_in")]
        win_in = [sem(f"win_in{g}") for g in range(7)]
        wout_in = [sem(f"wout_in{g}") for g in range(2)]
        w1_in = [sem(f"w1_in{t}") for t in range(8)]
        w2_in = [sem(f"w2_in{t}") for t in range(8)]
        b1_in = [sem(f"b1_in{k}") for k in range(2)]
        gathered = [sem(f"gathered{k}") for k in range(2)]
        out_done, state_out, rec_out, conv_out, hn_out, sum_out, scattered = [
            sem(n) for n in ("out_done", "state_out", "rec_out", "conv_out", "hn_out", "sum_out", "scattered")]
        pool_const, pool_link, dve_link, act_link = [
            sem(n) for n in ("pool_const", "pool_link", "dve_link", "act_link")]
        gains_ps, gains_sb, x_sq, rstd_x, xn_sb, xT_ps, xT_act, xT_dve, crow_ps, cT_sb = [
            sem(n) for n in ("gains_ps", "gains_sb", "x_sq", "rstd_x", "xn_sb", "xT_ps", "xT_act", "xT_dve",
                             "crow_ps", "cT_sb")]
        lb_sub, lb_exp, lb_sb = [sem(n) for n in ("lb_sub", "lb_exp", "lb_sb")]
        fx_ps, fx_exp, f_sb, logf_sb, kk_sb, iv_ps, v_sb, q_ps, q_sb, og_ps, og_exp, sog_sb = [
            sem(n) for n in ("fx_ps", "fx_exp", "f_sb", "logf_sb", "kk_sb", "iv_ps", "v_sb", "q_ps", "q_sb",
                             "og_ps", "og_exp", "sog_sb")]
        kkT_ps, kkT_sb, span_ps, span_exp, ex_used, score_ps, score_sb, tail_ps, tail_exp, khat_sb = [
            sem(n) for n in ("kkT_ps", "kkT_sb", "span_ps", "span_exp", "ex_used", "score_ps", "score_sb",
                             "tail_ps", "tail_exp", "khat_sb")]
        bg_ps, bg_sb, hv_ps, bx_sb, cg_ps, conv_sb, yconv_sb, nconv_sb, ncrow_ps, ncrow_sb = [
            sem(n) for n in ("bg_ps", "bg_sb", "hv_ps", "bx_sb", "cg_ps", "conv_sb", "yconv_sb", "nconv_sb",
                             "ncrow_ps", "ncrow_sb")]
        state_ps, state_sb, o_ps, osq_sb, oss_sb, ortd_sb, yrec_sb, yT_ps, yTrec_sb, hs_sb = [
            sem(n) for n in ("state_ps", "state_sb", "o_ps", "osq_sb", "oss_sb", "ortd_sb", "yrec_sb", "yT_ps",
                             "yTrec_sb", "hs_sb")]
        vdiag_sb, outer_ps, snew_sb, os_ps, os_sb = [
            sem(n) for n in ("vdiag_sb", "outer_ps", "snew_sb", "os_ps", "os_sb")]
        mix_ps, h_sb, h_sq, hrstd_act, hn_sb, hnT_ps, hnT_act, hnT_dve, logit_ps, logit_sb = [
            sem(n) for n in ("mix_ps", "h_sb", "h_sq", "hrstd_act", "hn_sb", "hnT_ps", "hnT_act", "hnT_dve",
                             "logit_ps", "logit_sb")]
        gate_sub, gate_exp, member_sb, pos_ps, pos_sb, combT_ps, combT_sb, b2_ps, sum_sb, max_sb = [
            sem(n) for n in ("gate_sub", "gate_exp", "member_sb", "pos_ps", "pos_sb", "combT_ps", "combT_sb",
                             "b2_ps", "sum_sb", "max_sb")]
        onehot_sb, slot_ps, slot_sb, pass_sb, pos_moved = [
            sem(n) for n in ("onehot_sb", "slot_ps", "slot_sb", "pass_sb", "pos_moved")]
        at_sb, xgT_ps, xgT_sb, w1_used, w2_used, glu_sb, sig_sb, lin_sb, gl_sb, act_sb = [
            sem(n) for n in ("at_sb", "xgT_ps", "xgT_sb", "w1_used", "w2_used", "glu_sb", "sig_sb",
                             "lin_sb", "gl_sb", "act_sb")]
        actT_ps, actT_sb, y_sb, sums_done, fin_sq, frstd_act, fin_sb, route_const = [
            sem(n) for n in ("actT_ps", "actT_sb", "y_sb", "sums_done", "fin_sq", "frstd_act", "fin_sb",
                             "route_const")]

        STEPS = [(c, l) for c in range(2) for l in range(LEVELS + 1)]
        PIECES = []
        for s, (c, l) in enumerate(STEPS):
            PIECES.append(("span", s))
            if l == 0:
                PIECES.append(("diag", c))
            if s and STEPS[s - 1][1] < LEVELS:
                PIECES.append(("score", s - 1))
            if s < 3:
                PIECES.append(("tail", (2, 0, 1)[s]))
        PROJ = [(g, j) for j in range(4) for g in (BG, HV)] + [(CG, j) for j in range(4)]
        SCHEDULE = []
        for n, proj in enumerate(PROJ):
            SCHEDULE.append(("proj", proj))
            SCHEDULE += PIECES[3 * n:3 * n + 3]
        SCHEDULE += PIECES[3 * len(PROJ):]
        SCORES = [p for p in PIECES if p[0] in ("diag", "score")]

        def score_no(s):
            return SCORES.index(("score", s))

        def w_group(g):
            return w_in[0].rearrange("(t p) n -> p t n", p=P)[:, :, g * 512:(g + 1) * 512]

        def slots(ring, a):
            return ring[:, a:a + 2, :].rearrange("p a n -> p (a n)")

        w_sb = {g: cut(slots(ring, a), 512) for g, (ring, a) in {
            FX: (w1r, 4), IV: (w2r, 0), QG: (w1r, 6), OG: (w2r, 2), BG: (w1r, 0), HV: (w1r, 2),
            CG: (w1r, 4)}.items()}
        wout_sb = [cut(slots(w1r, 6), D), cut(slots(w2r, 0), D)]
        w1_v = expert_w1[0].rearrange("e (t p) n -> e t p n", p=P)
        w2_v = expert_w2[0].rearrange("e (r a p) n -> e r p a n", a=2, p=P)

        block = ctx.enter_context(nc.Block())

        def run_passes(eng, first, later):
            first(0)
            eng.wait_ge(max_sb, 1)
            most = eng.value_load(maxcount_i[0:1, 0:1], min_val=0, max_val=NT)
            with eng.Fori(1, PASSES) as c:
                with eng.If(most > c * CAP):
                    later(c)

        def pairs(eng, c, body, start=0, stop=E // 2):
            with eng.Fori(start, stop) as i:
                for k in range(2):
                    body(c, i, k)

        def num(c, i, k):
            return c * E + i * 2 + k

        def use(c, i):
            return c * (E // 2) + i

        @block.sync
        def _(sp):
            for i in range(2):
                sp.dma_start(x3[:, i, :], x_prompt[0, i * P:(i + 1) * P, :]).then_inc(x_in, 16)
            sp.dma_start(x3[0:NS, 2, :], x_sample[:, 0, :]).then_inc(x_in, 16)
            sp.dma_start(x3[NS:NS + NM, 2, :], meta_tokens).then_inc(x_in, 16)
            sp.dma_start(w_sb[FX], w_group(FX)).then_inc(win_in[FX], 16)
            sp.dma_start(w_sb[IV], w_group(IV)).then_inc(win_in[IV], 16)
            sp.dma_start(w_sb[QG], w_group(QG)).then_inc(win_in[QG], 16)
            sp.dma_start(w_sb[OG], w_group(OG)).then_inc(win_in[OG], 16)
            sp.dma_start(w_sb[BG], w_group(BG)).then_inc(win_in[BG], 16)
            sp.dma_start(w_sb[HV], w_group(HV)).then_inc(win_in[HV], 16)
            sp.wait_ge(xT_ps, KT)
            for h in range(HEADS):
                sp.dma_start(s0[:, h], state_rec[0, :, h].rearrange("b k v -> k b v")).then_inc(s0_in, 16)
            sp.wait_ge(fx_ps, 3)
            sp.dma_start(w_sb[CG], w_group(CG)).then_inc(win_in[CG], 16)
            wout_v = w_out[0].rearrange("(t p) n -> p t n", p=P)
            sp.wait_ge(q_ps, HEADS)
            sp.dma_start(wout_sb[0], wout_v[:, 0:4, :]).then_inc(wout_in[0], 16)
            sp.wait_ge(iv_ps, 3)
            sp.dma_start(wout_sb[1], wout_v[:, 4:8, :]).then_inc(wout_in[1], 16)

            def load_w1(t, e):
                sp.dma_start(w1r[:, t, :], w1_v[e, t]).then_inc(w1_in[t], 16)

            def load_w2(k, r, e):
                sp.dma_start(cut(w2r[:, 4 * k + r, :], D), w2_v[e, r]).then_inc(w2_in[4 * k + r], 16)

            def load_b1(k, e):
                sp.dma_start(b1r3[k], expert_b1[0, e:e + 1, :] if isinstance(e, int)
                             else expert_b1[0, bass.ds(e, 1), :]).then_inc(b1_in[k], 16)

            sp.wait_ge(og_ps, 3)
            load_w2(0, 2, 0)
            load_w2(0, 3, 0)
            sp.wait_ge(hv_ps, 4)
            for t in range(4):
                load_w1(t, 0)
            sp.wait_ge(cg_ps, 4)
            load_w1(4, 0)
            load_w1(5, 0)
            sp.wait_ge(snew_sb, HEADS)
            for h in range(HEADS):
                sp.dma_start(new_rec_sample[0, :, h].rearrange("b k v -> k b v"), s0[:, h]).then_inc(state_out, 16)
            sp.wait_ge(state_sb, 3)
            sp.dma_start(new_rec_prompt[0, 0].rearrange("h k v -> k h v"),
                         srec3[:, 0].rearrange("p (h v) -> p h v", h=HEADS)).then_inc(rec_out, 16)
            sp.wait_ge(yrec_sb, 3)
            sp.wait_ge(outer_ps, HEADS)
            load_w2(1, 0, 1)
            load_w2(1, 1, 1)
            sp.wait_ge(mix_ps, 3)
            load_w1(6, 0)
            load_w1(7, 0)
            load_w2(0, 0, 0)
            load_w2(0, 1, 0)
            load_b1(0, 0)
            sp.wait_ge(logit_ps, 3)
            load_b1(1, 1)
            sp.wait_ge(os_ps, HEADS)
            sp.wait_ge(state_out, 16 * HEADS)
            load_w2(1, 2, 1)
            load_w2(1, 3, 1)
            for t in range(8):
                sp.wait_ge(w1_used, t + 1)
                load_w1(t, 1)

            def load(c, i, k):
                n = num(c, i, k)
                e = i * 2 + k
                sp.wait_ge(w1_used, n * 8 - 15)
                load_b1(k, e)
                for t in range(8):
                    sp.wait_ge(w1_used, n * 8 - 7 + t)
                    load_w1(t, e)
                for r in range(4):
                    sp.wait_ge(w2_used, n * 4 - 7 + r)
                    load_w2(k, r, e)

            run_passes(sp, lambda c: pairs(sp, c, load, start=1), lambda c: pairs(sp, c, load))
            sp.wait_ge(sums_done, 1)
            sp.dma_start(gfin, norm_final.unsqueeze(0).to_broadcast([P, D])).then_inc(gfin_in, 16)
            for i in range(2):
                sp.dma_start(fin3[:, i], sum_rows[i * P:(i + 1) * P, :]).then_inc(fin_in, 16)
            sp.dma_start(fin3[0:NS, 2], sum_rows[NP:NT, :]).then_inc(fin_in, 16)
            for i in range(2):
                sp.wait_ge(fin_sb, i + 1)
                sp.dma_start(y_prompt[0, i * P:(i + 1) * P, :], fin3[:, i]).then_inc(out_done, 16)
            sp.wait_ge(fin_sb, 3)
            sp.dma_start(y_sample[:, 0, :], fin3[0:NS, 2]).then_inc(out_done, 16)
            sp.wait_ge(conv_out, 32)
            sp.wait_ge(rec_out, 16)
            sp.wait_ge(out_done, 16 * 3)


        @block.gpsimd
        def _(pool):
            linked = [0]

            def link(ins):
                linked[0] += 1
                ins.then_inc(pool_link, 1)
                pool.wait_ge(pool_link, linked[0])

            pool.memset(ident, 0.0)
            for m in (prefix, strict, suffix, spans, blocks):
                pool.memset(m, 1.0)
            pool.memset(small, 0.0)
            link(pool.memset(bx[:, 0:HALF], 0.0))
            pool.dma_start(hn_table[PAD_ROW:ROWS, :], bx[:, 0:HALF]).then_inc(scattered, 16)
            pool.dma_start(sum_table[PAD_ROW:ROWS, :], bx[:, 0:HALF]).then_inc(scattered, 16)
            pool.memset(eps_col, EPS)
            pool.iota(pad_at, pattern=[[0, 1]], base=PAD_ROW, channel_multiplier=1,
                      allow_small_or_imprecise_dtypes=True)
            pool.iota(tok_col, pattern=[[0, 1]], base=0, channel_multiplier=2,
                      allow_small_or_imprecise_dtypes=True)
            pool.iota(unpad, pattern=[[0, 1]], base=-PAD_ROW, channel_multiplier=-1,
                      allow_small_or_imprecise_dtypes=True)
            pool.memset(meta_row, 1.0)
            pool.memset(upper, 1.0)

            def keep(ap, op, base, chan, pattern, fill=0.0):
                return pool.affine_select(out=ap, in_=ap, compare_op=op, fill=fill, base=base,
                                          pattern=pattern, channel_multiplier=chan)

            keep(ident, ALU.not_equal, 0, 1, [[-1, P]], 1.0)
            keep(prefix, ALU.is_ge, 0, -1, [[1, P]])
            keep(strict, ALU.is_ge, -1, -1, [[1, P]])
            link(keep(suffix, ALU.is_ge, -1, 1, [[-1, P]]))
            keep(meta_row, ALU.is_ge, -NS, 1, [[0, 1]])
            link(keep(upper, ALU.is_ge, -CAP, 1, [[0, 1]]))
            link(pool.tensor_tensor(unpad, unpad, upper, ALU.add))
            halves = []
            for l in range(LEVELS):
                h = 1 << l
                nb = P // (2 * h)
                sp_l = spans3[:, l].rearrange("p (m a i) -> p m a i", a=2, i=h)
                bl_l = blocks3[:, l].rearrange("p (m a i) -> p m a i", a=2, i=h)
                halves.append((h, nb, sp_l, bl_l))
            for h, nb, sp_l, bl_l in halves:
                keep(sp_l[:, :, 1], ALU.is_ge, -h, 1, [[-2 * h, nb], [0, h]])
                keep(sp_l[:, :, 0], ALU.is_ge, -1, 1, [[-2 * h, nb], [-1, h]])
                keep(bl_l[:, :, 1], ALU.is_ge, 0, 1, [[-2 * h, nb], [0, h]])
                last = pool.memset(bl_l[:, :, 0], 0.0)
            link(last)
            for h, nb, sp_l, bl_l in halves:
                keep(sp_l[:, :, 1], ALU.is_ge, h, -1, [[2 * h, nb], [1, h]])
                keep(sp_l[:, :, 0], ALU.is_ge, h - 1, -1, [[2 * h, nb], [0, h]])
                last = keep(bl_l[:, :, 1], ALU.is_ge, h - 1, -1, [[2 * h, nb], [0, h]])
            last.then_inc(pool_const, 1)

            pool.wait_ge(v_sb, 3)
            for h in range(HEADS):
                if h:
                    pool.wait_ge(outer_ps, h)
                pool.tensor_tensor(vdiag.rearrange("p (b v) -> p b v", b=NS),
                                   bcast(vtok3[0:NS, 2, h * P:(h + 1) * P].unsqueeze(1), [NS, NS, P]),
                                   bcast(ident[0:NS, 0:NS].unsqueeze(2), [NS, NS, P]),
                                   ALU.mult).then_inc(vdiag_sb, 1)

            pool.wait_ge(state_ps, 3)
            pool.wait_ge(outer_ps, HEADS)
            for i in range(2):
                pool.dma_start(h3[:, i], x_prompt[0, i * P:(i + 1) * P, :]).then_inc(xres_in, 16)
            pool.dma_start(h3[0:NS, 2], x_sample[:, 0, :]).then_inc(xres_in, 16)
            pool.wait_ge(yT_ps, 3)
            pool.wait_ge(ncrow_sb, 1)
            pool.dma_start(new_conv_prompt[0, 0], ncrow[0:2, :]).then_inc(conv_out, 16)
            pool.dma_start(new_conv_sample[0].rearrange("b i n -> (b i) n"), ncrow[2:2 + 2 * NS, :])\
                .then_inc(conv_out, 16)
            pool.wait_ge(conv_out, 16 * 2)
            pool.dma_start(gffn, norm_ffn[0].unsqueeze(0).to_broadcast([P, D])).then_inc(gffn_in, 16)
            pool.wait_ge(nconv_sb, 1)
            pool.wait_ge(yconv_sb, 4)
            pool.dma_start(b2_sb, expert_b2[0]).then_inc(b2_in, 16)
            pool.wait_ge(score_sb, len(SCORES))
            pool.iota(iota32, pattern=[[1, E]], base=0, channel_multiplier=0,
                      allow_small_or_imprecise_dtypes=True)
            pool.iota(iota64, pattern=[[1, CAP]], base=0, channel_multiplier=0,
                      allow_small_or_imprecise_dtypes=True)
            pool.memset(ones, 1.0)
            pool.memset(logits3[:, 2], 0.0)
            pool.memset(row_valid, 1.0)
            link(pool.memset(vals[:, :, 2:3], 1.0))
            pool.tensor_copy(vals[:, :, 0:1], bcast(tok_col.unsqueeze(1), [P, 3 * E, 1]))
            for i in range(3):
                pool.memset(vals[:, i * E:(i + 1) * E, 1:2], 2.0 * P * i)
            pool.affine_select(out=row_valid[:, 2:3], in_=row_valid[:, 2:3], compare_op=ALU.is_ge, fill=0.0,
                               base=NS - 1, pattern=[[0, 1]], channel_multiplier=-1).then_inc(route_const, 1)
            for i in range(2):
                pool.wait_ge(hn_sb, i + 1)
                pool.dma_start(hn_rows[i * P:(i + 1) * P, :], hn3[:, i]).then_inc(hn_out, 16)
            pool.wait_ge(hn_sb, 3)
            pool.dma_start(hn_rows[NP:NT, :], hn3[0:NS, 2]).then_inc(hn_out, 16)
            for i in range(2):
                pool.wait_ge(sum_sb, i + 1)
                pool.dma_start(sum_rows[i * P:(i + 1) * P, :], h3[:, i]).then_inc(sum_out, 16)
            pool.wait_ge(sum_sb, 3)
            pool.dma_start(sum_rows[NP:NT, :], h3[0:NS, 2]).then_inc(sum_out, 16)

            def until(place, *waits):
                spare = small[0:1, 101 + place:102 + place]
                for signal, value in waits:
                    pool.wait_ge(signal, value)
                pool.tensor_tensor(spare, small[0:1, 100:101], small[0:1, 100:101], ALU.add)

            def gather(k, e, nth_copy):
                pool.tensor_copy(gather_at[:, k:k + 1], slot_row[:, bass.ds(e, 1)]).then_inc(at_sb, 1)
                until(1, (at_sb, nth_copy))
                pool.indirect_dma_start(xg3[:, k], None, hn_table[:, :],
                                        bass.IndirectOffsetOnAxis(gather_at[:, k:k + 1], 0))\
                    .then_inc(gathered[k], 16)

            def scatter(c, i, k, nth_copy):
                n = num(c, i, k)
                until(2, (scattered, (n + 2) * 16))
                pool.tensor_copy(scatter_at[:, k:k + 1], slot_row[:, bass.ds(i * 2 + k, 1)]).then_inc(at_sb, 1)
                until(3, (at_sb, nth_copy), (y_sb, n + 1))
                pool.indirect_dma_start(sum_table[:, :], bass.IndirectOffsetOnAxis(scatter_at[:, k:k + 1], 0),
                                        ysb3[:, k], None, bounds_check=ROWS - 1,
                                        compute_op=ALU.add).then_inc(scattered, 16)

            def one_pair(c, i, last):
                for k in range(2):
                    n = num(c, i, k)
                    nth = c * (2 * E) + (i * 2 + k) * 2
                    if not (last and k == 1):
                        until(0, (xgT_ps, n + 1))
                        gather(1 - k, i * 2 + k + 1, nth + 2)
                        scatter(c, i, k, nth + 3)
                    else:
                        scatter(c, i, k, nth + 2)

            def one_pass(c):
                until(4, (slot_sb, c * 4 + 4))
                gather(0, 0, c * (2 * E) + 1)
                with pool.Fori(0, E // 2 - 1) as i:
                    one_pair(c, i, False)
                one_pair(c, E // 2 - 1, True)
                until(5, (scattered, c * (16 * E) + 16 * E + 32))

            pool.wait_ge(hn_out, 48)
            pool.wait_ge(sum_out, 48)
            run_passes(pool, one_pass, one_pass)
            pool.memset(small[:, 90:91], 0.0).then_inc(sums_done, 1)

        @block.scalar
        def _(act):
            act.dma_start(gain_rows[0:8, :], norm_mix[0].rearrange("(t p) -> t p", p=P)).then_inc(gain_in, 16)
            act.dma_start(gain_rows[8:20, :], conv_w[0].rearrange("j (g p) -> (j g) p", p=P)).then_inc(gain_in, 16)
            act.dma_start(gain_rows[20:24, :], rec_norm[0].rearrange("(g p) -> g p", p=P)).then_inc(gain_in, 16)
            act.dma_start(lb2, rec_lower_bound.rearrange("a n -> (a n)").unsqueeze(0).to_broadcast([P, D]))\
                .then_inc(lb_in, 16)
            act.dma_start(crow, state_conv[0].rearrange("b i n -> (b i) n")).then_inc(crow_in, 16)
            act.dma_start(router3, router_w[0].rearrange("(t p) n -> p t n", p=P)).then_inc(const_in, 16)
            act.wait_ge(pool_const, 1)
            act.dma_start(rbrow, router_b).then_inc(const_in, 16)
            act.wait_ge(x_in, 64)
            for i in range(3):
                r = TILE_ROWS[i]
                last = act.activation(xn3[0:r, i], x3[0:r, i], ACT.Square, accum_out=ssq[0:r, i:i + 1])
                last.then_inc(x_sq, 1)
            act.wait_ge(x_sq, 3)
            for i in range(3):
                r = TILE_ROWS[i]
                act.activation(rstd[0:r, i:i + 1], ssq[0:r, i:i + 1], ACT.Sqrt, bias=eps_col[0:r],
                               scale=1.0 / D).then_inc(rstd_x, 1)
            act.wait_ge(gains_sb, 1)
            for t in range(0, KT, 2):
                act.wait_ge(xT_ps, t + 1)
                act.activation(xT3[:, t], ps[:, t % 2, 0:TOK], ACT.Copy, scale=gmix[:, t:t + 1]).then_inc(xT_act, 1)
            act.wait_ge(lb_sub, 1)
            act.activation(lb2, lb2, ACT.Exp).then_inc(lb_exp, 1)
            for i in range(3):
                r = TILE_ROWS[i]
                act.wait_ge(fx_ps, i + 1)
                act.activation(ftmp3[0:r, i], ps[0:r, 2 + i, :], ACT.Exp, scale=-1.0).then_inc(fx_exp, 1)
            for i in range(3):
                r = TILE_ROWS[i]
                act.wait_ge(f_sb, i + 1)
                act.activation(logf3[0:r, i], ftmp3[0:r, i], ACT.Ln).then_inc(logf_sb, 1)
            for i in range(3):
                r = TILE_ROWS[i]
                act.wait_ge(iv_ps, i + 1)
                act.activation(vtok3[0:r, i], ps[0:r, 5 + i, :], ACT.Copy).then_inc(v_sb, 1)
            for h in range(HEADS):
                act.wait_ge(q_ps, h + 1)
                act.activation(qC3.rearrange("p c (h t) -> p c h t", h=HEADS)[:, :, h],
                               ps[:, h % 2, P0C:TOK].rearrange("p (c t) -> p c t", c=2), ACT.Copy)
                act.activation(qS3[:, h], ps[:, h % 2, 0:32], ACT.Copy).then_inc(q_sb, 1)
            for i in range(2):
                act.wait_ge(og_ps, i + 1)
                act.activation(sog3[:, i], ps[:, 2 + i, :], ACT.Exp, scale=-1.0).then_inc(og_exp, 1)
            act.wait_ge(og_ps, 3)
            act.wait_ge(f_sb, 3)
            act.activation(sogS, ps[:, 4, 0:P], ACT.Exp, scale=-1.0).then_inc(og_exp, 1)
            for i in range(2):
                act.wait_ge(kkT_ps, i + 1)
                act.activation(kkC3[:, i], ps[:, i, :], ACT.Copy).then_inc(kkT_sb, 1)
            act.wait_ge(kkT_ps, 3)
            act.activation(kS3, ps[:, 5, 0:HEADS * NS].rearrange("p (h b) -> p h b", h=HEADS),
                           ACT.Copy).then_inc(kkT_sb, 1)
            tails = 0
            for what, a in SCHEDULE:
                if what == "proj" and a[0] == BG:
                    j = a[1]
                    act.wait_ge(bg_ps, j + 1)
                    if j:
                        act.wait_ge(bx_sb, j)
                    act.activation(ctmp, ps[:, 5, 0:TOK], ACT.Copy).then_inc(bg_sb, 1)
                if what == "span":
                    act.wait_ge(span_ps, a + 1)
                    if a >= 2:
                        act.wait_ge(ex_used, a - 1)
                    act.activation(ex3[:, a % 2], ps[:, a % 2, :], ACT.Exp).then_inc(span_exp, 1)
                if what == "tail":
                    r = TILE_ROWS[a]
                    tails += 1
                    act.wait_ge(tail_ps, tails)
                    if tails > 2:
                        act.wait_ge(khat_sb, tails - 2)
                    act.activation(tail3[0:r, tails % 2], ps[0:r, 4, :], ACT.Exp).then_inc(tail_exp, 1)
            for c in range(2):
                act.wait_ge(o_ps, c + 1)
                act.activation(ex3[:, c], ps[:, c, :], ACT.Square).then_inc(osq_sb, 1)
            act.wait_ge(os_sb, 1)
            act.activation(tail3[:, 0, 0:P], oS, ACT.Square, accum_out=ossq[:, 8:9]).then_inc(osq_sb, 1)
            act.wait_ge(oss_sb, 2)
            act.wait_ge(osq_sb, 3)
            act.activation(orstd, ossq, ACT.Sqrt, bias=eps_col, scale=1.0 / P).then_inc(ortd_sb, 1)
            act.wait_ge(mix_ps, 3)
            act.activation(hs_tmp, ps[32:32 + NS, 6, :], ACT.Copy).then_inc(hs_sb, 1)
            for i in range(3):
                r = [P, P, NS][i]
                act.wait_ge(h_sb, i + 1)
                act.activation(hn3[0:r, i], h3[0:r, i], ACT.Square, accum_out=hssq[0:r, i:i + 1]).then_inc(h_sq, 1)
                act.wait_ge(h_sq, i + 1)
                act.activation(hrstd[0:r, i:i + 1], hssq[0:r, i:i + 1], ACT.Sqrt, bias=eps_col[0:r],
                               scale=1.0 / D).then_inc(hrstd_act, 1)
            for t in range(0, KT, 2):
                act.wait_ge(hnT_ps, t + 1)
                act.activation(hnT3[:, t], ps[:, t % 2, 0:NT], ACT.Copy).then_inc(hnT_act, 1)
            act.wait_ge(gate_sub, 1)
            act.activation(gate4, gate4, ACT.Exp).then_inc(gate_exp, 1)
            act.wait_ge(combT_ps, 3)
            act.activation(combT, ps[0:E, 3, 0:NT], ACT.Copy).then_inc(combT_sb, 1)

            def expert(c, i, k):
                n = num(c, i, k)
                act.wait_ge(xgT_ps, n + 1)
                act.activation(xgT4[:, k], ps[:, 2, :].rearrange("p (c s) -> p c s", c=4), ACT.Copy)\
                    .then_inc(xgT_sb, 1)
                act.wait_ge(glu_sb, n + 1)
                act.activation(sig, glu, ACT.Sigmoid, scale=ALPHA).then_inc(sig_sb, 1)
                act.wait_ge(actT_ps, n + 1)
                act.activation(actT4[:, k], ps[:, 3, :].rearrange("p (c s) -> p c s", c=4), ACT.Copy)\
                    .then_inc(actT_sb, 1)

            def one_pass(c):
                pairs(act, c, expert)

            run_passes(act, one_pass, one_pass)
            act.wait_ge(fin_in, 48)
            for i in range(3):
                r = [P, P, NS][i]
                if i:
                    act.wait_ge(fin_sq, i)
                act.activation(fsq[0:r], fin3[0:r, i], ACT.Square, accum_out=fssq[0:r, i:i + 1]).then_inc(fin_sq, 1)
            act.wait_ge(fin_sq, 3)
            for i in range(3):
                r = [P, P, NS][i]
                act.activation(frstd[0:r, i:i + 1], fssq[0:r, i:i + 1], ACT.Sqrt, bias=eps_col[0:r],
                               scale=1.0 / D).then_inc(frstd_act, 1)

        @block.vector
        def _(dve):
            linked = [0]

            def link(ins):
                linked[0] += 1
                ins.then_inc(dve_link, 1)
                dve.wait_ge(dve_link, linked[0])

            dve.wait_ge(gains_ps, 1)
            dve.tensor_copy(gains, ps[:, 7, 0:24]).then_inc(gains_sb, 1)
            for i in range(3):
                r = TILE_ROWS[i]
                dve.wait_ge(rstd_x, i + 1)
                link(dve.reciprocal(rstd[0:r, i:i + 1], rstd[0:r, i:i + 1]))
                dve.tensor_scalar(xn3[0:r, i], x3[0:r, i], rstd[0:r, i:i + 1], None, ALU.mult).then_inc(xn_sb, 1)
            dve.wait_ge(lb_in, 16)
            link(dve.tensor_tensor(lbtmp, lb3[:, 0], lb3[:, 1], ALU.max))
            dve.tensor_tensor(lb3, lb3, bcast(lbtmp.unsqueeze(1), [P, 2, 512]), ALU.subtract).then_inc(lb_sub, 1)
            dve.wait_ge(gains_sb, 1)
            for t in range(1, KT, 2):
                dve.wait_ge(xT_ps, t + 1)
                dve.tensor_scalar(xT3[:, t], ps[:, t % 2, 0:TOK], gmix[:, t:t + 1], None, ALU.mult)\
                    .then_inc(xT_dve, 1)
            dve.wait_ge(crow_ps, 1)
            dve.tensor_copy(cT4, ps[:, 6, 0:64].rearrange("p (g b i) -> p g b i", g=4, i=2)).then_inc(cT_sb, 1)
            dve.wait_ge(lb_exp, 1)
            link(dve.tensor_tensor(lbtmp, lb3[:, 0], lb3[:, 1], ALU.add))
            link(dve.reciprocal(lbtmp, lbtmp))
            link(dve.tensor_tensor(lb3[:, 0], lb3[:, 0], lbtmp, ALU.mult))
            link(dve.tensor_scalar(lb3[:, 1], lb3[:, 0], -1.0, 1.0, ALU.mult, ALU.add))
            for i in range(3):
                r = TILE_ROWS[i]
                f = ftmp3[0:r, i]
                dve.wait_ge(fx_exp, i + 1)
                link(dve.tensor_scalar(f, f, 1.0, None, ALU.add))
                link(dve.reciprocal(f, f))
                link(dve.tensor_tensor(f, f, lb3[0:r, 1], ALU.mult))
                dve.tensor_tensor(f, f, lb3[0:r, 0], ALU.add).then_inc(f_sb, 1)
                dve.wait_ge(f_sb, i + 1)
                dve.tensor_scalar(kk3[0:r, i], f, -1.0, 1.0, ALU.mult, ALU.add).then_inc(kk_sb, 1)
            for i in range(3):
                g = sog3[:, i] if i < 2 else sogS
                o = ps[:, 2 + i, :] if i < 2 else ps[:, 4, 0:P]
                dve.wait_ge(og_exp, i + 1)
                link(dve.tensor_scalar(g, g, 1.0, None, ALU.add))
                link(dve.reciprocal(g, g))
                dve.tensor_tensor(g, g, o, ALU.mult).then_inc(sog_sb, 1)
            dve.wait_ge(kkT_sb, 3)
            dve.tensor_scalar(fS3, kS3, -1.0, 1.0, ALU.mult, ALU.add)

            tails = 0
            scores = 0
            dve.wait_ge(scattered, 32)
            for what, a in SCHEDULE:
                if what == "proj" and a[0] == HV:
                    j = a[1]
                    dve.wait_ge(hv_ps, j + 1)
                    dve.wait_ge(bg_sb, j + 1)
                    dve.tensor_tensor(bx3[:, j], ctmp, ps[:, 6, 0:TOK], ALU.mult).then_inc(bx_sb, 1)
                    dve.wait_ge(bx_sb, j + 1)
                    y = yT3[:, j, P0C:TOK]
                    ys = yT3[:, j, 0:NS]
                    w = [gconv[:, 4 * n + j:4 * n + j + 1] for n in range(3)]
                    dve.tensor_scalar(y, bx3[:, j, P0C:TOK], w[2], None, ALU.mult)
                    link(dve.tensor_scalar(ys, bx3[:, j, 0:NS], w[2], None, ALU.mult))
                    dve.scalar_tensor_tensor(y, bx3[:, j, P0C - 1:TOK - 1], w[1], y, ALU.mult, ALU.add)
                    link(dve.scalar_tensor_tensor(ys, cT4[:, j, :, 1], w[1], ys, ALU.mult, ALU.add))
                    dve.scalar_tensor_tensor(y, bx3[:, j, P0C - 2:TOK - 2], w[0], y, ALU.mult, ALU.add)
                    dve.scalar_tensor_tensor(ys, cT4[:, j, :, 0], w[0], ys, ALU.mult, ALU.add).then_inc(conv_sb, 1)
                if what == "proj" and a[0] == CG:
                    j = a[1]
                    dve.wait_ge(cg_ps, j + 1)
                    dve.wait_ge(conv_sb, j + 1)
                    dve.tensor_tensor(yT3[:, j, 0:NS], yT3[:, j, 0:NS], ps[:, 7, 0:NS], ALU.mult)
                    dve.tensor_tensor(yT3[:, j, P0C:TOK], yT3[:, j, P0C:TOK], ps[:, 7, P0C:TOK], ALU.mult)\
                        .then_inc(yconv_sb, 1)
                if what == "span":
                    c, l = STEPS[a]
                    dve.wait_ge(span_exp, a + 1)
                    dve.wait_ge(q_sb, HEADS)
                    dve.wait_ge(kkT_sb, 2)
                    if l == LEVELS:
                        dve.tensor_tensor(qhat3[:, c], ex3[:, a % 2], qC3[:, c], ALU.mult)
                        dve.tensor_copy(decay_all[:, 4 * c:4 * c + 4],
                                        ex3[:, a % 2].rearrange("p (h t) -> p h t", h=HEADS)[:, :, P - 1])\
                            .then_inc(ex_used, 1)
                    else:
                        h = 1 << l
                        split = lambda ap, half: ap.rearrange("p (m a i) -> p m a i", a=2, i=h)[:, :, half]
                        if a >= 2 and STEPS[a - 2][1] < LEVELS:
                            dve.wait_ge(score_ps, score_no(a - 2) + 1)
                        if a >= 3 and STEPS[a - 2][1] == LEVELS:
                            dve.wait_ge(score_ps, score_no(a - 4) + 1)
                        dve.tensor_tensor(split(wl3[:, a % 2], 0), split(ex3[:, a % 2], 0),
                                          split(kkC3[:, c], 0), ALU.mult)
                        dve.tensor_tensor(split(wl3[:, a % 2], 1), split(ex3[:, a % 2], 1),
                                          split(qC3[:, c], 1), ALU.mult).then_inc(ex_used, 1)
                if what in ("diag", "score"):
                    c = a if what == "diag" else STEPS[a][0]
                    dve.wait_ge(score_ps, scores + 1)
                    if scores:
                        dve.wait_ge(score_sb, scores)
                    got = ps[:, 2 + scores % 2, :].rearrange("p (h t) -> p h t", h=HEADS)
                    into = sc3[:, c].rearrange("p (h t) -> p h t", h=HEADS)
                    if what == "diag":
                        ins = dve.tensor_tensor(into, got, bcast(ident.unsqueeze(1), [P, HEADS, P]), ALU.mult)
                    else:
                        m = blocks3[:, STEPS[a][1]].bitcast(U32)
                        ins = dve.copy_predicated(into, bcast(m.unsqueeze(1), [P, HEADS, P]), got)
                    ins.then_inc(score_sb, 1)
                    scores += 1
                if what == "tail":
                    tails += 1
                    dve.wait_ge(tail_exp, tails)
                    dve.wait_ge(kkT_ps, 3)
                    if a == 2:
                        r = NS + NM
                        dve.scalar_tensor_tensor(kk_meta[0:r], tail3[0:r, tails % 2], meta_row[0:r], kk3[0:r, 2],
                                                 ALU.mult, ALU.mult).then_inc(khat_sb, 1)
                    else:
                        dve.tensor_tensor(kk3[:, a], kk3[:, a], tail3[:, tails % 2], ALU.mult).then_inc(khat_sb, 1)
            dve.wait_ge(state_ps, 1)
            dve.tensor_copy(srec3[:, 0], ps[:, 5, :]).then_inc(state_sb, 1)
            dve.wait_ge(ex_used, len(STEPS))
            for c in range(2):
                dve.wait_ge(state_ps, c + 2)
                dve.wait_ge(state_sb, c + 1)
                if c:
                    dve.wait_ge(o_ps, 1)
                for h in range(HEADS):
                    at = slice(h * P, (h + 1) * P)
                    last = dve.scalar_tensor_tensor(srec3[:, 1 - c, at], srec3[:, c, at],
                                                    decay_all[:, 4 * c + h:4 * c + h + 1], ps[:, 6 + c, at],
                                                    ALU.mult, ALU.add)
                last.then_inc(state_sb, 1)
            dve.tensor_copy(nconv3[:, :, 0:2], bx3[:, :, TOK - 2:TOK])
            after = nconv3[:, :, 2:].rearrange("p g (b i) -> p g b i", i=2)
            dve.tensor_copy(after[:, :, :, 0], cT4[:, :, :, 1])
            dve.tensor_copy(after[:, :, :, 1], bx3[:, :, 0:NS]).then_inc(nconv_sb, 1)
            dve.wait_ge(s0_in, 16 * HEADS)
            for h in range(HEADS):
                dve.tensor_tensor(s0[:, h], s0[:, h], bcast(fS3[:, h].unsqueeze(2), [P, NS, P]), ALU.mult)\
                    .then_inc(dve_link, 1)
                linked[0] += 1
                dve.wait_ge(dve_link, linked[0])
                dve.wait_ge(outer_ps, h + 1)
                dve.tensor_tensor(s0[:, h], s0[:, h], ps[:, 2:4, :].rearrange("p a (b v) -> p (a b) v", v=P),
                                  ALU.add).then_inc(snew_sb, 1)
                if h < 2:
                    dve.wait_ge(osq_sb, h + 1)
                    dve.tensor_reduce(ossq[:, 4 * h:4 * h + 4],
                                      ex3[:, h].rearrange("p (h v) -> p h v", h=HEADS), AX.X, ALU.add)\
                        .then_inc(oss_sb, 1)
            dve.wait_ge(ncrow_ps, 1)
            dve.tensor_copy(ncrow, ps[0:2 + 2 * NS, 5, :]).then_inc(ncrow_sb, 1)
            dve.wait_ge(os_ps, HEADS)
            dve.wait_ge(rec_out, 16)
            eye = bcast(ident.rearrange("p (h b) -> p b h", b=32)[:, 0:NS], [P, NS, HEADS])
            own = small[:, 92:92 + NS]
            link(dve.tensor_reduce(own, eye, AX.X, ALU.add))
            link(dve.tensor_tensor(ssum.rearrange("p (b v) -> p b v", b=NS),
                                   ps[:, 6:8, :].rearrange("p a (b v) -> p (a b) v", v=P),
                                   bcast(own.unsqueeze(2), [P, NS, P]), ALU.mult))
            dve.tensor_reduce(oS, ssum.rearrange("p (b v) -> p v b", b=NS), AX.X, ALU.add).then_inc(os_sb, 1)
            dve.wait_ge(ortd_sb, 1)
            link(dve.reciprocal(orstd, orstd))
            for c in range(2):
                by_head = lambda ap: ap.rearrange("p (h v) -> p h v", h=HEADS)
                link(dve.tensor_tensor(by_head(ex3[:, c]), by_head(ps[:, c, :]),
                                       bcast(orstd[:, 4 * c:4 * c + 4].unsqueeze(2), [P, HEADS, P]), ALU.mult))
                dve.tensor_tensor(sog3[:, c], ex3[:, c], sog3[:, c], ALU.mult).then_inc(yrec_sb, 1)
            dve.scalar_tensor_tensor(oS, oS, orstd[:, 8:9], sogS, ALU.mult, ALU.mult).then_inc(yrec_sb, 1)
            for c in range(2):
                dve.wait_ge(yT_ps, c + 1)
                at = TILE_COL[c]
                dve.tensor_tensor(yT3[:, 4:8, at:at + P],
                                  ps[:, (7, 0)[c], :].rearrange("p (h t) -> p h t", h=HEADS),
                                  bcast(grec.unsqueeze(2), [P, HEADS, P]), ALU.mult).then_inc(yTrec_sb, 1)
            dve.wait_ge(yT_ps, 3)
            dve.tensor_tensor(yT3[:, 4:8, 0:NS], ps[:, 1, 0:P].rearrange("p (h b) -> p h b", b=32)[:, :, 0:NS],
                              bcast(grec.unsqueeze(2), [P, HEADS, NS]), ALU.mult).then_inc(yTrec_sb, 1)
            dve.wait_ge(xres_in, 48)
            for i in range(2):
                dve.wait_ge(mix_ps, i + 1)
                dve.tensor_tensor(h3[:, i], h3[:, i], ps[:, 2 + 2 * i:4 + 2 * i, :].rearrange("p a n -> p (a n)"),
                                  ALU.add).then_inc(h_sb, 1)
            dve.wait_ge(mix_ps, 3)
            dve.tensor_tensor(h3[0:NS, 2, 0:HALF], h3[0:NS, 2, 0:HALF], ps[0:NS, 6, :], ALU.add)
            dve.wait_ge(hs_sb, 1)
            dve.tensor_tensor(h3[0:NS, 2, HALF:D], h3[0:NS, 2, HALF:D], hs_tmp, ALU.add).then_inc(h_sb, 1)
            dve.wait_ge(gffn_in, 16)
            for i in range(3):
                r = [P, P, NS][i]
                dve.wait_ge(hrstd_act, i + 1)
                link(dve.reciprocal(hrstd[0:r, i:i + 1], hrstd[0:r, i:i + 1]))
                dve.scalar_tensor_tensor(hn3[0:r, i], h3[0:r, i], hrstd[0:r, i:i + 1], gffn[0:r],
                                         ALU.mult, ALU.mult).then_inc(hn_sb, 1)
            for t in range(1, KT, 2):
                dve.wait_ge(hnT_ps, t + 1)
                dve.tensor_copy(hnT3[:, t], ps[:, t % 2, 0:NT]).then_inc(hnT_dve, 1)
            dve.wait_ge(route_const, 1)
            dve.wait_ge(logit_ps, 3)
            dve.tensor_copy(logits3[:, 0:2], ps[:, 7, 0:2 * E].rearrange("p (i e) -> p i e", e=E))
            link(dve.tensor_copy(logits3[0:NS, 2], ps[0:NS, 7, 2 * E:3 * E]))
            for i in range(3):
                last = dve.max(top8[:, i], logits3[:, i])
            link(last)
            for i in range(3):
                last = dve.max_index(idx8[:, i], top8[:, i], logits3[:, i])
            dve.tensor_tensor(gate4, top8[:, :, 0:TOPK], bcast(top8[:, :, 0:1], [P, 3, TOPK]), ALU.subtract)\
                .then_inc(gate_sub, 1)
            dve.wait_ge(gate_sub, 1)
            link(dve.tensor_copy(idxf, idx8))
            link(dve.tensor_tensor(eq_all, bcast(iota32.unsqueeze(1).unsqueeze(1), [P, 3, TOPK, E]),
                                   bcast(idxf[:, :, 0:TOPK].unsqueeze(3), [P, 3, TOPK, E]), ALU.is_equal))
            link(dve.tensor_reduce(member3, eq_all.rearrange("p i j e -> p i e j"), AX.X, ALU.add))
            dve.tensor_tensor(member3, member3, bcast(row_valid.unsqueeze(2), [P, 3, E]), ALU.mult)\
                .then_inc(member_sb, 1)
            dve.wait_ge(gate_exp, 1)
            link(dve.tensor_reduce(gsum, gate4, AX.X, ALU.add))
            link(dve.reciprocal(gsum, gsum))
            link(dve.tensor_tensor(gate4, gate4, bcast(gsum.unsqueeze(2), [P, 3, TOPK]), ALU.mult))
            link(dve.tensor_tensor(eq_all, eq_all, bcast(gate4.unsqueeze(3), [P, 3, TOPK, E]), ALU.mult))
            link(dve.tensor_reduce(comb3, eq_all.rearrange("p i j e -> p i e j"), AX.X, ALU.add))
            flat = route[:, 192:288]
            gflat = route[:, 1008:1104]
            link(dve.tensor_copy(vals[:, :, 3], flat))
            link(dve.tensor_tensor(gflat, flat, vals[:, :, 3], ALU.subtract))
            link(dve.tensor_copy(vals[:, :, 4], gflat))
            link(dve.tensor_tensor(gflat, gflat, vals[:, :, 4], ALU.subtract))
            link(dve.tensor_copy(vals[:, :, 5], gflat))
            dve.wait_ge(pos_ps, 1)
            dve.wait_ge(member_sb, 1)
            pos = ps[:, 6, 0:3 * E].rearrange("p (i e) -> p i e", e=E)
            link(dve.scalar_tensor_tensor(posm3, pos, 1.0, member3, ALU.add, ALU.mult))
            dve.tensor_scalar(posm3, posm3, -1.0, None, ALU.add)
            link(dve.tensor_reduce(maxcount, ps[:, 6, 3 * E:4 * E], AX.X, ALU.max))
            dve.tensor_copy(maxcount_i, maxcount).then_inc(max_sb, 1)

            def slot_lists(c):
                for g in range(E // ROUTE):
                    b = g % 2
                    if g < 2:
                        pass
                    else:
                        dve.wait_ge(slot_ps, c * 4 + (g - 1))
                    dve.tensor_tensor(onehot[:, b],
                                      bcast(posm3[:, :, g * ROUTE:(g + 1) * ROUTE].unsqueeze(3), [P, 3, ROUTE, CAP]),
                                      bcast(iota64.unsqueeze(1).unsqueeze(1), [P, 3, ROUTE, CAP]),
                                      ALU.is_equal).then_inc(onehot_sb, 1)
                    if g:
                        lists(c, g - 1)
                lists(c, E // ROUTE - 1)

            def lists(c, g):
                at = slice(g * ROUTE, (g + 1) * ROUTE)
                step = lambda n: c * 16 + (g * 4 + n)
                dve.wait_ge(slot_ps, c * 4 + (g + 1))
                if g:
                    dve.wait_ge(slot_sb, c * 4 + g)
                dve.tensor_copy(slotv, ps[:, 6 + g % 2, 0:6 * ROUTE].rearrange("p (e v) -> p e v", v=6))\
                    .then_inc(pass_sb, 1)
                dve.wait_ge(pass_sb, step(1))
                dve.tensor_tensor(slotf[:, at, 0], slotv[:, :, 0], slotv[:, :, 1], ALU.add)
                dve.tensor_scalar(slotf[:, at, 1], slotv[:, :, 2], unpad, pad_at, ALU.mult, ALU.add)
                dve.tensor_tensor(slot_gate[:, at], slotv[:, :, 3], slotv[:, :, 4], ALU.add).then_inc(pass_sb, 1)
                dve.wait_ge(pass_sb, step(2))
                dve.tensor_tensor(slotf[:, at, 0], slotf[:, at, 0], slotf[:, at, 1], ALU.add).then_inc(pass_sb, 1)
                dve.wait_ge(pass_sb, step(3))
                dve.tensor_copy(slot_row[:, at], slotf[:, at, 0]).then_inc(pass_sb, 1)
                dve.wait_ge(pass_sb, step(4))
                dve.tensor_tensor(slot_gate[:, at], slot_gate[:, at], slotv[:, :, 5], ALU.add).then_inc(slot_sb, 1)

            def expert(c, i, k):
                n = num(c, i, k)
                dve.wait_ge(w1_used, n * 8 + 8)
                dve.tensor_scalar(glu, psA[:, 0:D:2], LIMIT, None, ALU.min).then_inc(glu_sb, 1)
                dve.tensor_scalar(lin, psA[:, 1:D:2], -LIMIT, LIMIT, ALU.max, ALU.min).then_inc(lin_sb, 1)
                dve.wait_ge(lin_sb, n + 1)
                dve.scalar_tensor_tensor(lin, lin, 1.0, glu, ALU.add, ALU.mult).then_inc(gl_sb, 1)
                dve.wait_ge(gl_sb, n + 1)
                dve.wait_ge(sig_sb, n + 1)
                dve.tensor_tensor(act, lin, sig, ALU.mult).then_inc(act_sb, 1)
                dve.wait_ge(scattered, (n + 1) * 16)
                dve.wait_ge(w2_used, n * 4 + 4)
                dve.tensor_scalar(ysb3[:, k], ps[:, 4 + k, :], slot_gate[:, bass.ds(i * 2 + k, 1)], None,
                                  ALU.mult).then_inc(y_sb, 1)

            def sums_start():
                for i in range(2):
                    dve.wait_ge(b2_ps, i + 1)
                    b = (4, 2)[i]
                    dve.tensor_tensor(h3[:, i], h3[:, i], ps[:, b:b + 2, :].rearrange("p a n -> p (a n)"),
                                      ALU.add).then_inc(sum_sb, 1)
                dve.wait_ge(b2_ps, 3)
                dve.tensor_tensor(h3[0:NS, 2], h3[0:NS, 2], ps[0:NS, 6:8, :].rearrange("p a n -> p (a n)"),
                                  ALU.add).then_inc(sum_sb, 1)
                dve.wait_ge(hn_out, 48)
                dve.wait_ge(sum_out, 48)

            def first_pass(c):
                dve.wait_ge(max_sb, 1)
                slot_lists(c)
                sums_start()
                pairs(dve, c, expert)

            def later_pass(c):
                dve.wait_ge(scattered, c * (16 * E) + 32)
                dve.tensor_scalar(posm3, posm3, -float(CAP), None, ALU.add).then_inc(pos_moved, 1)
                dve.wait_ge(pos_moved, c)
                slot_lists(c)
                pairs(dve, c, expert)

            run_passes(dve, first_pass, later_pass)
            dve.wait_ge(gfin_in, 16)
            for i in range(3):
                r = [P, P, NS][i]
                dve.wait_ge(frstd_act, i + 1)
                link(dve.reciprocal(frstd[0:r, i:i + 1], frstd[0:r, i:i + 1]))
                dve.scalar_tensor_tensor(fin3[0:r, i], fin3[0:r, i], frstd[0:r, i:i + 1], gfin[0:r],
                                         ALU.mult, ALU.mult).then_inc(fin_sb, 1)

        @block.tensor
        def _(pe):
            mm = pe.matmul
            pe.wait_ge(pool_const, 1)
            pe.wait_ge(gain_in, 48)
            pe.transpose(ps[:, 7, 0:24], gain_rows, ident[0:24, 0:24]).then_inc(gains_ps, 1)
            pe.wait_ge(crow_in, 16)
            for g in range(4):
                last = pe.transpose(ps[:, 6, 16 * g:16 * g + 16], crow[:, g * P:(g + 1) * P],
                                    ident[0:2 * NS, 0:2 * NS])
            last.then_inc(crow_ps, 1)
            pe.wait_ge(xn_sb, 3)
            for t in range(KT):
                if t >= 2:
                    pe.wait_ge((xT_act, xT_dve)[t % 2], t // 2)
                for i in range(3):
                    r, at = TILE_ROWS[i], TILE_COL[i]
                    last = pe.transpose(ps[:, t % 2, at:at + r], xn3[0:r, i, t * P:(t + 1) * P], ident[0:r, 0:r])
                last.then_inc(xT_ps, 1)
            pe.wait_ge(xT_act, 4)
            pe.wait_ge(xT_dve, 4)

            def rows_of(g, bank, done):
                pe.wait_ge(win_in[g], 16)
                for i in range(3):
                    r, at = TILE_ROWS[i], TILE_COL[i]
                    for t in range(KT):
                        last = mm(ps[0:r, bank + i, :], xT3[:, t, at:at + r], w_sb[g][:, t, :],
                                  start=(t == 0), stop=(t == KT - 1))
                    last.then_inc(done, 1)

            def columns_of(g, j, bank, done):
                pe.wait_ge(win_in[g], 16)
                for t in range(KT):
                    last = mm(ps[:, bank, 0:TOK], w_sb[g][:, t, j * P:(j + 1) * P], xT3[:, t, :],
                              start=(t == 0), stop=(t == KT - 1))
                last.then_inc(done, 1)

            rows_of(FX, 2, fx_ps)
            pe.wait_ge(cT_sb, 1)
            rows_of(IV, 5, iv_ps)
            for h in range(HEADS):
                if h >= 2:
                    pe.wait_ge(q_sb, h - 1)
                columns_of(QG, h, h % 2, q_ps)
            pe.wait_ge(win_in[OG], 16)
            pe.wait_ge(fx_exp, 3)
            for i in range(2):
                for t in range(KT):
                    last = mm(ps[:, 2 + i, :], xT3[:, t, TILE_COL[i]:TILE_COL[i] + P], w_sb[OG][:, t, :],
                              start=(t == 0), stop=(t == KT - 1))
                last.then_inc(og_ps, 1)
            for t in range(KT):
                for h in range(HEADS):
                    last = mm(ps[32 * h:32 * h + 32, 4, 0:P], xT3[:, t, 0:32], w_sb[OG][:, t, h * P:(h + 1) * P],
                              start=(t == 0), stop=(t == KT - 1))
            last.then_inc(og_ps, 1)
            pe.wait_ge(kk_sb, 3)
            pe.wait_ge(v_sb, 3)
            pe.wait_ge(q_sb, HEADS)
            for i in range(2):
                for h in range(HEADS):
                    last = pe.transpose(ps[:, i, h * P:(h + 1) * P], kk3[:, i, h * P:(h + 1) * P], ident)
                last.then_inc(kkT_ps, 1)
            for h in range(HEADS):
                last = pe.transpose(ps[:, 5, NS * h:NS * (h + 1)], kk3[0:NS, 2, h * P:(h + 1) * P],
                                    ident[0:NS, 0:NS])
            last.then_inc(kkT_ps, 1)
            pe.wait_ge(logf_sb, 3)
            pe.wait_ge(v_sb, 3)

            scores = 0
            tails = 0
            for what, a in SCHEDULE:
                if what == "proj":
                    g, j = a
                    bank, done, used = {BG: (5, bg_ps, bg_sb), HV: (6, hv_ps, bx_sb), CG: (7, cg_ps, yconv_sb)}[g]
                    pe.wait_ge(*((used, j) if j else (kkT_sb, 3)))
                    columns_of(g, j, bank, done)
                if what == "span":
                    c, l = STEPS[a]
                    if a < 2:
                        pe.wait_ge(kkT_sb, a + 1)
                    else:
                        pe.wait_ge(span_exp, a - 1)
                    for h in range(HEADS):
                        last = mm(ps[:, a % 2, h * P:(h + 1) * P], logf3[:, c, h * P:(h + 1) * P],
                                  spans3[:, l] if l < LEVELS else prefix, start=True, stop=True)
                    last.then_inc(span_ps, 1)
                if what in ("diag", "score"):
                    if scores < 2:
                        pe.wait_ge(sog_sb, scores + 1)
                    else:
                        pe.wait_ge(score_sb, scores - 1)
                    if what == "diag":
                        pe.wait_ge(kkT_sb, 2)
                        left, right = kkC3[:, a], qC3[:, a]
                    else:
                        pe.wait_ge(ex_used, a + 1)
                        left = right = wl3[:, a % 2]
                    for h in range(HEADS):
                        at = slice(h * P, (h + 1) * P)
                        last = mm(ps[:, 2 + scores % 2, at], left[:, at], right[:, at], start=True, stop=True)
                    last.then_inc(score_ps, 1)
                    scores += 1
                if what == "tail":
                    r = TILE_ROWS[a]
                    if tails == 0:
                        pe.wait_ge(sog_sb, 3)
                        pe.wait_ge(kkT_sb, 3)
                    else:
                        pe.wait_ge(tail_exp, tails)
                    tails += 1
                    mm(ps[0:r, 4, :], suffix[0:r, 0:r], logf3[0:r, a, :], start=True, stop=True).then_inc(tail_ps, 1)
            r = NS + NM
            pe.wait_ge(khat_sb, 3)
            pe.wait_ge(bg_sb, 4)
            pe.wait_ge(bx_sb, 4)
            pe.wait_ge(yconv_sb, 4)
            for n, (keys, vals_) in enumerate([(kk_meta[0:r], vtok3[0:r, 2]), (kk3[:, 0], vtok3[:, 0]),
                                               (kk3[:, 1], vtok3[:, 1])]):
                for h in range(HEADS):
                    at = slice(h * P, (h + 1) * P)
                    last = mm(ps[:, 5 + n, at], keys[:, at], vals_[:, at], start=True, stop=True)
                last.then_inc(state_ps, 1)

            def outer(h):
                if h:
                    pe.wait_ge(snew_sb, h)
                pe.wait_ge(vdiag_sb, h + 1)
                for n in range(2):
                    last = mm(ps[:, 2 + n, :], kk3[0:NS, 2, h * P:(h + 1) * P], vdiag[:, n * 512:(n + 1) * 512],
                              start=True, stop=True)
                last.then_inc(outer_ps, 1)

            def recur(c):
                pe.wait_ge(state_sb, c + 1)
                for h in range(HEADS):
                    at = slice(h * P, (h + 1) * P)
                    mm(ps[:, c, at], sc3[:, c, at], vtok3[:, c, at], start=True, stop=False)
                    last = mm(ps[:, c, at], qhat3[:, c, at], srec3[:, c, at], start=False, stop=True)
                last.then_inc(o_ps, 1)

            pe.wait_ge(score_sb, len(SCORES))
            pe.wait_ge(ex_used, len(STEPS))
            outer(0)
            recur(0)
            outer(1)
            recur(1)
            outer(2)
            pe.wait_ge(nconv_sb, 1)
            for g in range(4):
                last = pe.transpose(ps[0:2 + 2 * NS, 5, g * P:(g + 1) * P], nconv3[:, g], ident)
            last.then_inc(ncrow_ps, 1)
            outer(3)
            pe.wait_ge(state_sb, 3)
            for h in range(HEADS):
                pe.wait_ge(snew_sb, h + 1)
                for n in range(2):
                    last = mm(ps[32 * h:32 * h + 32, 6 + n, :], qS3[:, h],
                              s0[:, h].rearrange("p b v -> p (b v)")[:, n * 512:(n + 1) * 512],
                              start=True, stop=True)
                last.then_inc(os_ps, 1)

            def mix(i, first):
                pe.wait_ge(wout_in[0 if first else 1], 16)
                for n in range(2):
                    for t in range(4):
                        k = t if first else 4 + t
                        last = mm(ps[:, 2 + 2 * i + n, :], yT3[:, k, TILE_COL[i]:TILE_COL[i] + P],
                                  wout_sb[k // 4][:, t, n * 512:(n + 1) * 512], start=(k == 0), stop=(k == KT - 1))
                return last

            mix(0, True)
            pe.wait_ge(ncrow_sb, 1)
            mix(1, True)
            for c in range(2):
                pe.wait_ge(yrec_sb, c + 1)
                for h in range(HEADS):
                    last = pe.transpose(ps[:, (7, 0)[c], h * P:(h + 1) * P], sog3[:, c, h * P:(h + 1) * P], ident)
                last.then_inc(yT_ps, 1)
            pe.wait_ge(yrec_sb, 3)
            pe.transpose(ps[:, 1, 0:P], oS, ident).then_inc(yT_ps, 1)
            for i in range(2):
                pe.wait_ge(yTrec_sb, i + 1)
                mix(i, False).then_inc(mix_ps, 1)
            pe.wait_ge(yTrec_sb, 3)
            for k in range(KT):
                for n in range(2):
                    last = mm(ps[32 * n:32 * n + NS, 6, :], yT3[:, k, 0:NS],
                              wout_sb[k // 4][:, k % 4, n * 512:(n + 1) * 512], start=(k == 0), stop=(k == KT - 1))
            last.then_inc(mix_ps, 1)
            pe.wait_ge(hn_sb, 3)
            for t in range(KT):
                if t >= 2:
                    pe.wait_ge((hnT_act, hnT_dve)[t % 2], t // 2)
                for i in range(3):
                    r = [P, P, NS][i]
                    last = pe.transpose(ps[:, t % 2, i * P:i * P + r], hn3[0:r, i, t * P:(t + 1) * P], ident[0:r, 0:r])
                last.then_inc(hnT_ps, 1)
            pe.wait_ge(hnT_act, 4)
            pe.wait_ge(hnT_dve, 4)
            pe.wait_ge(const_in, 32)
            pe.wait_ge(route_const, 1)
            for i in range(3):
                r = [P, P, NS][i]
                out = ps[0:r, 7, i * E:(i + 1) * E]
                mm(out, ones[0:1, 0:r], rbrow, start=True, stop=False)
                for t in range(KT):
                    last = mm(out, hnT3[:, t, i * P:i * P + r], router3[:, t], start=False, stop=(t == KT - 1))
                last.then_inc(logit_ps, 1)
            pe.wait_ge(member_sb, 1)
            for i in range(3):
                for m in range(i + 1):
                    mm(ps[:, 6, i * E:(i + 1) * E], strict if m == i else ones, member3[:, m],
                       start=(m == 0), stop=(m == i))
            for m in range(3):
                last = mm(ps[:, 6, 3 * E:4 * E], ones, member3[:, m], start=(m == 0), stop=(m == 2))
            last.then_inc(pos_ps, 1)

            def slot_lists(c):
                for g in range(E // ROUTE):
                    b = g % 2
                    pe.wait_ge(onehot_sb, c * 4 + (g + 1))
                    if g >= 2:
                        pe.wait_ge(slot_sb, c * 4 + (g - 1))
                    for e in range(ROUTE):
                        for i in range(3):
                            for half in range(2):
                                last = mm(ps[64 * half:64 * half + 64, 6 + b, 6 * e:6 * e + 6], onehot[:, b, i, e],
                                          vals[:, i * E + g * ROUTE + e], start=(i == 0), stop=(i == 2))
                    last.then_inc(slot_ps, 1)

            def expert(c, i, k):
                n = num(c, i, k)
                pe.wait_ge(gathered[k], use(c, i) * 16 + 16)
                for q in range(4):
                    last = pe.transpose(ps[:, 2, q * P:(q + 1) * P], xg3[:, k, q * P:(q + 1) * P], ident)
                last.then_inc(xgT_ps, 1)
                pe.wait_ge(b1_in[k], use(c, i) * 16 + 16)
                order = [(0, 0), (1, 0), (0, 1), (1, 1)]
                for half, n2 in order:
                    col = half * D + n2 * 512
                    mm(psA[64 * half:64 * half + 64, n2 * 512:(n2 + 1) * 512], ones[0:1, 0:CAP],
                       b1r3[k][:, col:col + 512], start=True, stop=False)
                pe.wait_ge(xgT_sb, n + 1)
                for t in range(KT):
                    pe.wait_ge(w1_in[t], n * 16 + 16)
                    for half, n2 in order:
                        col = half * D + n2 * 512
                        last = mm(psA[64 * half:64 * half + 64, n2 * 512:(n2 + 1) * 512],
                                  xgT4[:, k, t % 4, 64 * (t // 4):64 * (t // 4) + 64], w1r[:, t, col:col + 512],
                                  start=False, stop=(t == KT - 1))
                    last.then_inc(w1_used, 1)
                pe.wait_ge(act_sb, n + 1)
                for q in range(4):
                    last = pe.transpose(ps[:, 3, q * P:(q + 1) * P], act[:, q * P:(q + 1) * P], ident)
                last.then_inc(actT_ps, 1)
                pe.wait_ge(actT_sb, n + 1)
                for t in range(KT):
                    if t % 2 == 0:
                        pe.wait_ge(w2_in[4 * k + t // 2], use(c, i) * 16 + 16)
                    for half in range(2):
                        col = (t % 2) * D + half * HALF
                        last = mm(ps[64 * half:64 * half + 64, 4 + k, :],
                                  actT4[:, k, t % 4, 64 * (t // 4):64 * (t // 4) + 64],
                                  w2r[:, 4 * k + t // 2, col:col + HALF], start=(t == 0), stop=(t == KT - 1))
                    if t % 2:
                        last.then_inc(w2_used, 1)

            def first_pass(c):
                slot_lists(c)
                for i in range(3):
                    r = [P, P, NS][i]
                    pe.transpose(ps[0:E, 3, i * P:i * P + r], comb3[0:r, i], ident[0:r, 0:r]).then_inc(combT_ps, 1)
                pe.wait_ge(b2_in, 16)
                pe.wait_ge(combT_sb, 1)
                pe.wait_ge(slot_sb, 4)
                for i in range(3):
                    r = [P, P, NS][i]
                    b = (4, 2, 6)[i]
                    for n in range(2):
                        last = mm(ps[0:r, b + n, :], combT[:, i * P:i * P + r], b2_sb[:, n * 512:(n + 1) * 512],
                                  start=True, stop=True)
                    last.then_inc(b2_ps, 1)
                pe.wait_ge(sum_sb, 3)
                pairs(pe, c, expert)

            def later_pass(c):
                slot_lists(c)
                pairs(pe, c, expert)

            run_passes(pe, first_pass, later_pass)


INPUTS = ["x_prompt", "x_sample", "state_conv", "state_rec", "meta_tokens", "norm_mix", "w_in", "conv_w",
          "rec_lower_bound", "rec_norm", "w_out", "norm_ffn", "router_w", "router_b", "expert_w1", "expert_b1",
          "expert_w2", "expert_b2", "norm_final"]
OUTPUT_SHAPES = [(1, NP, D), (NS, 1, D), (1, 1, 2, HALF), (1, 1, HEADS, P, P), (1, NS, 2, HALF),
                 (1, NS, HEADS, P, P)]


def kernel(**inputs):
    import numpy as np
    import concourse.bacc as bacc
    from concourse.bass_utils import run_bass_kernel_spmd

    nc = bacc.Bacc("TRN2", target_bir_lowering=False, num_devices=1)
    arrays, args = {}, []
    for name in INPUTS:
        a = np.ascontiguousarray(inputs[name])
        arrays[f"in_{name}"] = a
        args.append(nc.dram_tensor(f"in_{name}", a.shape, mybir.dt.from_np(a.dtype), kind="ExternalInput").ap())
    for i, shape in enumerate(OUTPUT_SHAPES):
        args.append(nc.dram_tensor(f"out_{i}", shape, F32, kind="ExternalOutput").ap())
    build_step(nc, *args)
    r = run_bass_kernel_spmd(nc, [arrays], core_ids=[0])
    return tuple(r.results[0][f"out_{i}"] for i in range(len(OUTPUT_SHAPES)))
```

```python
import concourse.bass as bass
from concourse import mybir
from contextlib import ExitStack

F32 = mybir.dt.float32
BF16 = mybir.dt.bfloat16
U32 = mybir.dt.uint32
I32 = mybir.dt.int32
ALU = mybir.AluOpType
ACT = mybir.ActivationFunctionType
AX = mybir.AxisListType

P = 128
D = 1024
KT = D // P
HALF = D // 2
NS, NM, NP = 8, 16, 256
S0C, P0C = 0, NS + NM
TOK = NS + NM + NP
NT = NP + NS
HEADS = 4
E = 32
TOPK = 4
CAP = 64
PASSES = -(-NT // CAP)
LEVELS = 7
EPS = 1e-5
LIMIT = 7.0
ALPHA = 1.702
BG, CG, HV, QG, FX, IV, OG = range(7)
TILE_COL = [P0C, P0C + P, 0]
TILE_ROWS = [P, P, NS + NM]


def bcast(ap, shape):
    return ap.to_broadcast(shape)


def build_step(nc, x_prompt, x_sample, state_conv, state_rec, meta_tokens, norm_mix, w_in, conv_w,
               rec_lower_bound, rec_norm, w_out, norm_ffn, router_w, router_b, expert_w1, expert_b1,
               expert_w2, expert_b2, norm_final,
               y_prompt, y_sample, new_conv_prompt, new_rec_prompt, new_conv_sample, new_rec_sample):
    ctx = ExitStack()
    with ctx:
        def sem(name):
            return ctx.enter_context(nc.semaphore(name))

        w1r = ctx.enter_context(nc.sbuf_tensor("w1r", [P, 8, 2048], F32))
        w2r = ctx.enter_context(nc.sbuf_tensor("w2r", [P, 8, 2048], F32))
        ARENA = 20440
        mem = ctx.enter_context(nc.sbuf_tensor("mem", [P, ARENA], F32))
        top = [0]

        def take(n):
            a = top[0]
            top[0] += n
            assert top[0] <= ARENA, top[0]
            return mem[:, a:a + n]


        ident = take(P)
        prefix = take(P)
        suffix = take(P)
        spans = take(LEVELS * P)
        blocks = take(LEVELS * P)
        gains = take(24)
        small = take(P)
        router_sb = take(KT * E)
        lb2 = take(2 * 512)
        xT = take(KT * TOK)
        kk = take(3 * 512)
        logf = take(3 * 512)
        vtok = take(3 * 512)
        sog = take(2 * 512)
        kk_meta = take(512)
        qC = take(2 * 512)
        kkC = take(2 * 512)
        qS = take(HEADS * 32)
        kS = take(HEADS * NS)
        qhat = take(2 * 512)
        srec = take(2 * 512)
        bx = take(4 * TOK)
        ctmp = take(TOK)
        cT = take(4 * 2 * NS)
        nconv = take(4 * (2 + 2 * NS))
        yT = take(KT * TOK)

        def cut(ap, n):
            return ap.rearrange("p (a n) -> p a n", n=n)

        def from_(ap, n, at=0):
            return mem[:, ap.offset + at:ap.offset + at + n]

        spans3, blocks3 = cut(spans, P), cut(blocks, P)
        lb3, xT3, kk3, logf3, vtok3, sog3 = cut(lb2, 512), cut(xT, TOK), cut(kk, 512), cut(logf, 512), cut(vtok, 512), cut(sog, 512)
        qC3, kkC3, qS3, kS3, qhat3, srec3 = cut(qC, 512), cut(kkC, 512), cut(qS, 32), cut(kS, NS), cut(qhat, 512), cut(srec, 512)
        bx3, yT3, router3 = cut(bx, TOK), cut(yT, TOK), cut(router_sb, E)
        cT4 = cT.rearrange("p (g b i) -> p g b i", g=4, i=2)
        nconv3 = cut(nconv, 2 + 2 * NS)
        gmix, gconv, grec = gains[:, 0:8], gains[:, 8:20], gains[:, 20:24]
        ssq, rstd = small[:, 0:3], small[:, 3:6]
        ossq, orstd = small[:, 6:15], small[:, 15:24]
        hssq, hrstd = small[:, 24:27], small[:, 27:30]
        fssq, frstd = small[:, 30:33], small[:, 33:36]
        eps_col = small[:, 36:37]
        meta_row = small[:, 37:38]
        rbrow = small[0:1, 40:72]
        maxcount = small[:, 72:73]
        maxcount_i = small[:, 73:74].bitcast(I32)
        decay_all = small[:, 80:88]
        hi = w2r[:, 4:6, :].rearrange("p a n -> p (a n)")
        lo = w2r[:, 6:8, :].rearrange("p a n -> p (a n)")
        x3 = cut(hi[:, 0:3072], D)
        xn3 = cut(lo[:, 0:3072], D)
        gain_rows = lo[0:24, 3072:3200]
        ex3 = cut(hi[:, 0:1024], 512)
        wl3 = cut(hi[:, 1024:2048], 512)
        sc3 = cut(hi[:, 2048:3072], 512)
        vdiag = hi[0:NS, 3072:4096]
        s0 = lo.rearrange("p (h b v) -> p h b v", h=HEADS, b=NS)
        ftmp3 = cut(yT[:, 0:1536], 512)
        lbtmp = yT[:, 1536:2048]
        tail3 = cut(yT[:, 1120:2144], 512)
        fS3 = cut(lb2[:, 256:256 + HEADS * NS], NS)
        ssum = from_(srec, 1024)
        hs_tmp = from_(qC, 512)[0:NS, :]
        crow = qhat[0:2 * NS, 0:512]
        ncrow = lb2[0:2 + 2 * NS, 512:1024]
        sogS, oS = lb2[:, 0:128], lb2[:, 128:256]
        h3 = cut(from_(kk, 3 * D), D)
        hn3 = cut(from_(vtok, 3 * D), D)
        hnT3 = cut(xT[:, 0:KT * NT], NT)
        gffn = lb2
        b2_sb = bx[0:E, 0:D]
        route = from_(spans, 2 * LEVELS * P)
        logits3 = cut(route[:, 0:96], E)
        top8 = cut(route[:, 96:120], 8)
        idx8 = cut(route[:, 120:144].bitcast(U32), 8)
        idxf = cut(route[:, 144:168], 8)
        gate4 = cut(route[:, 168:180], TOPK)
        gsum = route[:, 180:183]
        comb3 = cut(route[:, 192:288], E)
        member3 = cut(route[:, 288:384], E)
        posm3 = cut(route[:, 384:480], E)
        iota32 = route[:, 480:512]
        iota64 = route[:, 512:576]
        row_valid = route[:, 576:579]
        member_b3 = cut(route[:, 580:628].bitcast(BF16), E)
        stack = route[:, 640:672]
        ones_b = route[:, 672:736].bitcast(BF16)
        strict_b = route[:, 736:800].bitcast(BF16)
        ones = route[:, 800:800 + P]
        combT = route[0:E, 928:928 + NT]
        logitT = route[:, 1200:1200 + NT]
        eq_all = from_(qhat, 3 * TOPK * E).rearrange("p (i j e) -> p i j e", i=3, j=TOPK)
        oh4 = from_(qhat, 2 * 3 * CAP, 384).rearrange("p (k i s) -> p k i s", k=2, i=3)
        ohg4 = from_(srec, 2 * 3 * P).rearrange("p (k i s) -> p k i s", k=2, i=3)
        ohgT = from_(kkC, NT)
        late = from_(kkC, HALF, 384)
        xg, xgT3 = from_(lb2, HALF), cut(from_(lb2, HALF, HALF), CAP)
        b1r = from_(yT, 2048)[0:1, :]
        glu, sig, lin, act = [from_(xT, 512, 512 * n) for n in range(4)]
        actT3 = cut(from_(qC, HALF), P)
        ysb = from_(qC, HALF, HALF)
        gfin = from_(bx, D)
        fsq = from_(xT, D)
        late0 = from_(xT, HALF, D)[0:NS, :]

        ps = ctx.enter_context(nc.psum_tensor("ps", [P, 8, 512], F32))
        psA = ps[:, 0:2, :].rearrange("p a n -> p (a n)")

        x_in, gain_in, lb_in, crow_in, s0_in, const_in, xres_in, gffn_in, b2_in, gfin_in = [
            sem(n) for n in ("x_in", "gain_in", "lb_in", "crow_in", "s0_in", "const_in", "xres_in",
                             "gffn_in", "b2_in", "gfin_in")]
        win_in = [sem(f"win_in{g}") for g in range(7)]
        wout_in = [sem(f"wout_in{g}") for g in range(2)]
        w1_in = [sem(f"w1_in{t}") for t in range(8)]
        w2_in = [sem(f"w2_in{t}") for t in range(8)]
        b1_in = sem("b1_in")
        out_done, state_out, rec_out, conv_out = [
            sem(n) for n in ("out_done", "state_out", "rec_out", "conv_out")]
        pool_const, pool_link, dve_link, act_link = [
            sem(n) for n in ("pool_const", "pool_link", "dve_link", "act_link")]
        gains_ps, gains_sb, x_sq, rstd_x, xn_sb, xT_ps, xT_act, xT_dve, crow_ps, cT_sb = [
            sem(n) for n in ("gains_ps", "gains_sb", "x_sq", "rstd_x", "xn_sb", "xT_ps", "xT_act", "xT_dve",
                             "crow_ps", "cT_sb")]
        lb_sub, lb_exp, lb_sb = [sem(n) for n in ("lb_sub", "lb_exp", "lb_sb")]
        fx_ps, fx_exp, f_sb, logf_sb, kk_sb, iv_ps, v_sb, q_ps, q_sb, og_ps, og_exp, sog_sb = [
            sem(n) for n in ("fx_ps", "fx_exp", "f_sb", "logf_sb", "kk_sb", "iv_ps", "v_sb", "q_ps", "q_sb",
                             "og_ps", "og_exp", "sog_sb")]
        kkT_ps, kkT_sb, span_ps, span_exp, ex_used, score_ps, score_sb, tail_ps, tail_exp, khat_sb = [
            sem(n) for n in ("kkT_ps", "kkT_sb", "span_ps", "span_exp", "ex_used", "score_ps", "score_sb",
                             "tail_ps", "tail_exp", "khat_sb")]
        bg_ps, bg_sb, hv_ps, bx_sb, cg_ps, conv_sb, yconv_sb, nconv_sb, ncrow_ps, ncrow_sb = [
            sem(n) for n in ("bg_ps", "bg_sb", "hv_ps", "bx_sb", "cg_ps", "conv_sb", "yconv_sb", "nconv_sb",
                             "ncrow_ps", "ncrow_sb")]
        state_ps, state_sb, o_ps, osq_sb, oss_sb, ortd_sb, yrec_sb, yT_ps, yTrec_sb, hs_sb = [
            sem(n) for n in ("state_ps", "state_sb", "o_ps", "osq_sb", "oss_sb", "ortd_sb", "yrec_sb", "yT_ps",
                             "yTrec_sb", "hs_sb")]
        vdiag_sb, outer_ps, snew_sb, os_ps, os_sb = [
            sem(n) for n in ("vdiag_sb", "outer_ps", "snew_sb", "os_ps", "os_sb")]
        mix_ps, h_sb, h_sq, hrstd_act, hn_sb, hnT_ps, hnT_act, hnT_dve, logit_ps, logit_sb = [
            sem(n) for n in ("mix_ps", "h_sb", "h_sq", "hrstd_act", "hn_sb", "hnT_ps", "hnT_act", "hnT_dve",
                             "logit_ps", "logit_sb")]
        logitT_ps, logitT_sb, gate_sub, gate_exp, member_sb, pos_ps, combT_ps, combT_sb, comb_sb, max_sb = [
            sem(n) for n in ("logitT_ps", "logitT_sb", "gate_sub", "gate_exp", "member_sb", "pos_ps", "combT_ps",
                             "combT_sb", "comb_sb", "max_sb")]
        pos_moved, oh_sb, ohg_sb, xg_ps, xg_sb, xgT_ps, xgT_sb, ohgT_ps, ohgT_sb = [
            sem(n) for n in ("pos_moved", "oh_sb", "ohg_sb", "xg_ps", "xg_sb", "xgT_ps", "xgT_sb", "ohgT_ps",
                             "ohgT_sb")]
        w1_used, w2_used, b1_used, glu_sb, sig_sb, lin_sb, gl_sb, act_sb, actT_ps, actT_sb, y_sb = [
            sem(n) for n in ("w1_used", "w2_used", "b1_used", "glu_sb", "sig_sb", "lin_sb", "gl_sb", "act_sb",
                             "actT_ps", "actT_sb", "y_sb")]
        rows_ps, added, late_sb, fin_sum, fin_sq, frstd_act, fin_sb, route_const = [
            sem(n) for n in ("rows_ps", "added", "late_sb", "fin_sum", "fin_sq", "frstd_act", "fin_sb",
                             "route_const")]

        STEPS = [(c, l) for c in range(2) for l in range(LEVELS + 1)]
        PIECES = []
        for s, (c, l) in enumerate(STEPS):
            PIECES.append(("span", s))
            if l == 0:
                PIECES.append(("diag", c))
            if s and STEPS[s - 1][1] < LEVELS:
                PIECES.append(("score", s - 1))
            if s < 3:
                PIECES.append(("tail", (2, 0, 1)[s]))
        PROJ = [(g, j) for j in range(4) for g in (BG, HV)] + [(CG, j) for j in range(4)]
        SCHEDULE = []
        for n, proj in enumerate(PROJ):
            SCHEDULE.append(("proj", proj))
            SCHEDULE += PIECES[3 * n:3 * n + 3]
        SCHEDULE += PIECES[3 * len(PROJ):]
        SCORES = [p for p in PIECES if p[0] in ("diag", "score")]

        def score_no(s):
            return SCORES.index(("score", s))

        def w_group(g):
            return w_in[0].rearrange("(t p) n -> p t n", p=P)[:, :, g * 512:(g + 1) * 512]

        def slots(ring, a):
            return ring[:, a:a + 2, :].rearrange("p a n -> p (a n)")

        w_sb = {g: cut(slots(ring, a), 512) for g, (ring, a) in {
            FX: (w1r, 4), IV: (w2r, 0), QG: (w1r, 6), OG: (w2r, 2), BG: (w1r, 0), HV: (w1r, 2),
            CG: (w1r, 4)}.items()}
        wout_sb = [cut(slots(w1r, 6), D), cut(slots(w2r, 0), D)]
        w1_v = expert_w1[0].rearrange("e (t p) n -> e t p n", p=P)
        w2_v = expert_w2[0].rearrange("e (r a p) n -> e r p a n", a=2, p=P)

        block = ctx.enter_context(nc.Block())

        def run_passes(eng, first, later):
            first(0)
            eng.wait_ge(max_sb, 1)
            most = eng.value_load(maxcount_i[0:1, 0:1], min_val=0, max_val=NT)
            with eng.Fori(1, PASSES) as c:
                with eng.If(most > c * CAP):
                    later(c)

        def each_expert(eng, c, body, start=0):
            with eng.Fori(start, E // 2 - 1) as i:
                for k in range(2):
                    body(c, i, k, False)
            body(c, E // 2 - 1, 0, False)
            body(c, E // 2 - 1, 1, True)

        def num(c, i, k):
            return c * E + i * 2 + k

        def use(c, i):
            return c * (E // 2) + i

        @block.sync
        def _(sp):
            for i in range(2):
                sp.dma_start(x3[:, i, :], x_prompt[0, i * P:(i + 1) * P, :]).then_inc(x_in, 16)
            sp.dma_start(x3[0:NS, 2, :], x_sample[:, 0, :]).then_inc(x_in, 16)
            sp.dma_start(x3[NS:NS + NM, 2, :], meta_tokens).then_inc(x_in, 16)
            sp.dma_start(w_sb[FX], w_group(FX)).then_inc(win_in[FX], 16)
            sp.dma_start(w_sb[IV], w_group(IV)).then_inc(win_in[IV], 16)
            sp.dma_start(w_sb[QG], w_group(QG)).then_inc(win_in[QG], 16)
            sp.dma_start(w_sb[OG], w_group(OG)).then_inc(win_in[OG], 16)
            sp.dma_start(w_sb[BG], w_group(BG)).then_inc(win_in[BG], 16)
            sp.dma_start(w_sb[HV], w_group(HV)).then_inc(win_in[HV], 16)
            sp.wait_ge(xT_ps, KT)
            for h in range(HEADS):
                sp.dma_start(s0[:, h], state_rec[0, :, h].rearrange("b k v -> k b v")).then_inc(s0_in, 16)
            sp.wait_ge(fx_ps, 3)
            sp.dma_start(w_sb[CG], w_group(CG)).then_inc(win_in[CG], 16)
            wout_v = w_out[0].rearrange("(t p) n -> p t n", p=P)
            sp.wait_ge(q_ps, HEADS)
            sp.dma_start(wout_sb[0], wout_v[:, 0:4, :]).then_inc(wout_in[0], 16)
            sp.wait_ge(iv_ps, 3)
            sp.dma_start(wout_sb[1], wout_v[:, 4:8, :]).then_inc(wout_in[1], 16)

            def load_w1(t, e):
                sp.dma_start(w1r[:, t, :], w1_v[e, t]).then_inc(w1_in[t], 16)

            def load_w2(k, r, e):
                sp.dma_start(cut(w2r[:, 4 * k + r, :], D), w2_v[e, r]).then_inc(w2_in[4 * k + r], 16)

            def load_b1(e):
                sp.dma_start(b1r, expert_b1[0, e:e + 1, :] if isinstance(e, int)
                             else expert_b1[0, bass.ds(e, 1), :]).then_inc(b1_in, 16)

            sp.wait_ge(og_ps, 3)
            load_w2(0, 2, 0)
            load_w2(0, 3, 0)
            sp.wait_ge(hv_ps, 4)
            for t in range(4):
                load_w1(t, 0)
            sp.wait_ge(cg_ps, 4)
            load_w1(4, 0)
            load_w1(5, 0)
            sp.wait_ge(snew_sb, HEADS)
            for h in range(HEADS):
                sp.dma_start(new_rec_sample[0, :, h].rearrange("b k v -> k b v"), s0[:, h]).then_inc(state_out, 16)
            sp.wait_ge(state_sb, 3)
            sp.dma_start(new_rec_prompt[0, 0].rearrange("h k v -> k h v"),
                         srec3[:, 0].rearrange("p (h v) -> p h v", h=HEADS)).then_inc(rec_out, 16)
            sp.wait_ge(yrec_sb, 3)
            sp.wait_ge(outer_ps, HEADS)
            load_w2(1, 0, 1)
            load_w2(1, 1, 1)
            sp.wait_ge(mix_ps, 3)
            load_w1(6, 0)
            load_w1(7, 0)
            load_w2(0, 0, 0)
            load_w2(0, 1, 0)
            load_b1(0)
            sp.wait_ge(state_out, 16 * HEADS)
            load_w2(1, 2, 1)
            load_w2(1, 3, 1)
            sp.wait_ge(b1_used, 1)
            load_b1(1)
            for t in range(8):
                sp.wait_ge(w1_used, t + 1)
                load_w1(t, 1)

            def load(c, i, k, last):
                n = num(c, i, k)
                e = i * 2 + k
                sp.wait_ge(b1_used, n)
                load_b1(e)
                for t in range(8):
                    sp.wait_ge(w1_used, n * 8 - 7 + t)
                    load_w1(t, e)
                for r in range(4):
                    sp.wait_ge(w2_used, n * 4 - 7 + r)
                    load_w2(k, r, e)

            run_passes(sp, lambda c: each_expert(sp, c, load, start=1), lambda c: each_expert(sp, c, load))
            for i in range(2):
                sp.wait_ge(fin_sb, i + 1)
                sp.dma_start(y_prompt[0, i * P:(i + 1) * P, :], h3[:, i]).then_inc(out_done, 16)
            sp.wait_ge(fin_sb, 3)
            sp.dma_start(y_sample[:, 0, :], h3[0:NS, 2]).then_inc(out_done, 16)
            sp.wait_ge(conv_out, 32)
            sp.wait_ge(rec_out, 16)
            sp.wait_ge(out_done, 16 * 3)


        @block.gpsimd
        def _(pool):
            linked = [0]

            def link(ins):
                linked[0] += 1
                ins.then_inc(pool_link, 1)
                pool.wait_ge(pool_link, linked[0])

            pool.memset(ident, 0.0)
            for m in (prefix, suffix, spans, blocks):
                pool.memset(m, 1.0)
            link(pool.memset(small, 0.0))
            pool.memset(eps_col, EPS)
            pool.memset(meta_row, 1.0)

            def keep(ap, op, base, chan, pattern, fill=0.0):
                return pool.affine_select(out=ap, in_=ap, compare_op=op, fill=fill, base=base,
                                          pattern=pattern, channel_multiplier=chan)

            keep(ident, ALU.not_equal, 0, 1, [[-1, P]], 1.0)
            keep(prefix, ALU.is_ge, 0, -1, [[1, P]])
            link(keep(suffix, ALU.is_ge, -1, 1, [[-1, P]]))
            keep(meta_row, ALU.is_ge, -NS, 1, [[0, 1]])
            halves = []
            for l in range(LEVELS):
                h = 1 << l
                nb = P // (2 * h)
                sp_l = spans3[:, l].rearrange("p (m a i) -> p m a i", a=2, i=h)
                bl_l = blocks3[:, l].rearrange("p (m a i) -> p m a i", a=2, i=h)
                halves.append((h, nb, sp_l, bl_l))
            for h, nb, sp_l, bl_l in halves:
                keep(sp_l[:, :, 1], ALU.is_ge, -h, 1, [[-2 * h, nb], [0, h]])
                keep(sp_l[:, :, 0], ALU.is_ge, -1, 1, [[-2 * h, nb], [-1, h]])
                keep(bl_l[:, :, 1], ALU.is_ge, 0, 1, [[-2 * h, nb], [0, h]])
                last = pool.memset(bl_l[:, :, 0], 0.0)
            link(last)
            for h, nb, sp_l, bl_l in halves:
                keep(sp_l[:, :, 1], ALU.is_ge, h, -1, [[2 * h, nb], [1, h]])
                keep(sp_l[:, :, 0], ALU.is_ge, h - 1, -1, [[2 * h, nb], [0, h]])
                last = keep(bl_l[:, :, 1], ALU.is_ge, h - 1, -1, [[2 * h, nb], [0, h]])
            last.then_inc(pool_const, 1)

            pool.wait_ge(v_sb, 3)
            for h in range(HEADS):
                if h:
                    pool.wait_ge(outer_ps, h)
                pool.tensor_tensor(vdiag.rearrange("p (b v) -> p b v", b=NS),
                                   bcast(vtok3[0:NS, 2, h * P:(h + 1) * P].unsqueeze(1), [NS, NS, P]),
                                   bcast(ident[0:NS, 0:NS].unsqueeze(2), [NS, NS, P]),
                                   ALU.mult).then_inc(vdiag_sb, 1)

            pool.wait_ge(state_ps, 3)
            pool.wait_ge(outer_ps, HEADS)
            for i in range(2):
                pool.dma_start(h3[:, i], x_prompt[0, i * P:(i + 1) * P, :]).then_inc(xres_in, 16)
            pool.dma_start(h3[0:NS, 2], x_sample[:, 0, :]).then_inc(xres_in, 16)
            pool.wait_ge(yT_ps, 3)
            pool.wait_ge(ncrow_sb, 1)
            pool.dma_start(new_conv_prompt[0, 0], ncrow[0:2, :]).then_inc(conv_out, 16)
            pool.dma_start(new_conv_sample[0].rearrange("b i n -> (b i) n"), ncrow[2:2 + 2 * NS, :])\
                .then_inc(conv_out, 16)
            pool.wait_ge(conv_out, 16 * 2)
            pool.dma_start(gffn, norm_ffn[0].unsqueeze(0).to_broadcast([P, D])).then_inc(gffn_in, 16)
            pool.wait_ge(nconv_sb, 1)
            pool.wait_ge(yconv_sb, 4)
            pool.dma_start(b2_sb, expert_b2[0]).then_inc(b2_in, 16)
            pool.wait_ge(score_sb, len(SCORES))
            pool.iota(iota32, pattern=[[1, E]], base=0, channel_multiplier=0,
                      allow_small_or_imprecise_dtypes=True)
            pool.iota(iota64, pattern=[[1, CAP]], base=0, channel_multiplier=0,
                      allow_small_or_imprecise_dtypes=True)
            pool.memset(ones, 1.0)
            pool.memset(logits3[:, 2], 0.0)
            pool.memset(row_valid, 1.0)
            pool.memset(ones_b, 1.0)
            pool.memset(strict_b, 1.0)
            link(pool.memset(stack, 0.0))
            pool.affine_select(out=row_valid[:, 2:3], in_=row_valid[:, 2:3], compare_op=ALU.is_ge, fill=0.0,
                               base=NS - 1, pattern=[[0, 1]], channel_multiplier=-1)
            keep(strict_b, ALU.is_ge, -1, -1, [[1, P]])
            for g in range(4):
                last = keep(stack, ALU.not_equal, -32 * g, 1, [[-1, E]], 1.0)
                if g < 3:
                    link(last)
            last.then_inc(route_const, 1)
            pool.wait_ge(rows_ps, 3)
            pool.dma_start(gfin, norm_final.unsqueeze(0).to_broadcast([P, D])).then_inc(gfin_in, 16)

        @block.scalar
        def _(act):
            act.dma_start(gain_rows[0:8, :], norm_mix[0].rearrange("(t p) -> t p", p=P)).then_inc(gain_in, 16)
            act.dma_start(gain_rows[8:20, :], conv_w[0].rearrange("j (g p) -> (j g) p", p=P)).then_inc(gain_in, 16)
            act.dma_start(gain_rows[20:24, :], rec_norm[0].rearrange("(g p) -> g p", p=P)).then_inc(gain_in, 16)
            act.dma_start(lb2, rec_lower_bound.rearrange("a n -> (a n)").unsqueeze(0).to_broadcast([P, D]))\
                .then_inc(lb_in, 16)
            act.dma_start(crow, state_conv[0].rearrange("b i n -> (b i) n")).then_inc(crow_in, 16)
            act.dma_start(router3, router_w[0].rearrange("(t p) n -> p t n", p=P)).then_inc(const_in, 16)
            act.wait_ge(pool_const, 1)
            act.dma_start(rbrow, router_b).then_inc(const_in, 16)
            act.wait_ge(x_in, 64)
            for i in range(3):
                r = TILE_ROWS[i]
                last = act.activation(xn3[0:r, i], x3[0:r, i], ACT.Square, accum_out=ssq[0:r, i:i + 1])
                last.then_inc(x_sq, 1)
            act.wait_ge(x_sq, 3)
            for i in range(3):
                r = TILE_ROWS[i]
                act.activation(rstd[0:r, i:i + 1], ssq[0:r, i:i + 1], ACT.Sqrt, bias=eps_col[0:r],
                               scale=1.0 / D).then_inc(rstd_x, 1)
            act.wait_ge(gains_sb, 1)
            for t in range(0, KT, 2):
                act.wait_ge(xT_ps, t + 1)
                act.activation(xT3[:, t], ps[:, t % 2, 0:TOK], ACT.Copy, scale=gmix[:, t:t + 1]).then_inc(xT_act, 1)
            act.wait_ge(lb_sub, 1)
            act.activation(lb2, lb2, ACT.Exp).then_inc(lb_exp, 1)
            for i in range(3):
                r = TILE_ROWS[i]
                act.wait_ge(fx_ps, i + 1)
                act.activation(ftmp3[0:r, i], ps[0:r, 2 + i, :], ACT.Exp, scale=-1.0).then_inc(fx_exp, 1)
            for i in range(3):
                r = TILE_ROWS[i]
                act.wait_ge(f_sb, i + 1)
                act.activation(logf3[0:r, i], ftmp3[0:r, i], ACT.Ln).then_inc(logf_sb, 1)
            for i in range(3):
                r = TILE_ROWS[i]
                act.wait_ge(iv_ps, i + 1)
                act.activation(vtok3[0:r, i], ps[0:r, 5 + i, :], ACT.Copy).then_inc(v_sb, 1)
            for h in range(HEADS):
                act.wait_ge(q_ps, h + 1)
                act.activation(qC3.rearrange("p c (h t) -> p c h t", h=HEADS)[:, :, h],
                               ps[:, h % 2, P0C:TOK].rearrange("p (c t) -> p c t", c=2), ACT.Copy)
                act.activation(qS3[:, h], ps[:, h % 2, 0:32], ACT.Copy).then_inc(q_sb, 1)
            for i in range(2):
                act.wait_ge(og_ps, i + 1)
                act.activation(sog3[:, i], ps[:, 2 + i, :], ACT.Exp, scale=-1.0).then_inc(og_exp, 1)
            act.wait_ge(og_ps, 3)
            act.wait_ge(f_sb, 3)
            act.activation(sogS, ps[:, 4, 0:P], ACT.Exp, scale=-1.0).then_inc(og_exp, 1)
            for i in range(2):
                act.wait_ge(kkT_ps, i + 1)
                act.activation(kkC3[:, i], ps[:, i, :], ACT.Copy).then_inc(kkT_sb, 1)
            act.wait_ge(kkT_ps, 3)
            act.activation(kS3, ps[:, 5, 0:HEADS * NS].rearrange("p (h b) -> p h b", h=HEADS),
                           ACT.Copy).then_inc(kkT_sb, 1)
            tails = 0
            for what, a in SCHEDULE:
                if what == "proj" and a[0] == BG:
                    j = a[1]
                    act.wait_ge(bg_ps, j + 1)
                    if j:
                        act.wait_ge(bx_sb, j)
                    act.activation(ctmp, ps[:, 5, 0:TOK], ACT.Copy).then_inc(bg_sb, 1)
                if what == "span":
                    act.wait_ge(span_ps, a + 1)
                    if a >= 2:
                        act.wait_ge(ex_used, a - 1)
                    act.activation(ex3[:, a % 2], ps[:, a % 2, :], ACT.Exp).then_inc(span_exp, 1)
                if what == "tail":
                    r = TILE_ROWS[a]
                    tails += 1
                    act.wait_ge(tail_ps, tails)
                    if tails > 2:
                        act.wait_ge(khat_sb, tails - 2)
                    act.activation(tail3[0:r, tails % 2], ps[0:r, 4, :], ACT.Exp).then_inc(tail_exp, 1)
            for c in range(2):
                act.wait_ge(o_ps, c + 1)
                act.activation(ex3[:, c], ps[:, c, :], ACT.Square).then_inc(osq_sb, 1)
            act.wait_ge(os_sb, 1)
            act.activation(tail3[:, 0, 0:P], oS, ACT.Square, accum_out=ossq[:, 8:9]).then_inc(osq_sb, 1)
            act.wait_ge(oss_sb, 2)
            act.wait_ge(osq_sb, 3)
            act.activation(orstd, ossq, ACT.Sqrt, bias=eps_col, scale=1.0 / P).then_inc(ortd_sb, 1)
            act.wait_ge(mix_ps, 3)
            act.activation(hs_tmp, ps[32:32 + NS, 6, :], ACT.Copy).then_inc(hs_sb, 1)
            for i in range(3):
                r = [P, P, NS][i]
                act.wait_ge(h_sb, i + 1)
                act.activation(hn3[0:r, i], h3[0:r, i], ACT.Square, accum_out=hssq[0:r, i:i + 1]).then_inc(h_sq, 1)
                act.wait_ge(h_sq, i + 1)
                act.activation(hrstd[0:r, i:i + 1], hssq[0:r, i:i + 1], ACT.Sqrt, bias=eps_col[0:r],
                               scale=1.0 / D).then_inc(hrstd_act, 1)
            for t in range(0, KT, 2):
                act.wait_ge(hnT_ps, t + 1)
                act.activation(hnT3[:, t], ps[:, t % 2, 0:NT], ACT.Copy).then_inc(hnT_act, 1)
            act.wait_ge(logitT_ps, 1)
            act.activation(logitT, ps[:, 2, 0:NT], ACT.Copy).then_inc(logitT_sb, 1)
            act.wait_ge(gate_sub, 1)
            act.activation(gate4, gate4, ACT.Exp).then_inc(gate_exp, 1)

            def copy_xg(n):
                act.wait_ge(xg_ps, n + 1)
                act.activation(xg, ps[:, 2, :], ACT.Copy).then_inc(xg_sb, 1)

            def copy_xgT(n):
                act.wait_ge(xgT_ps, n + 1)
                act.activation(xgT3.rearrange("p (a q) s -> p q a s", a=2),
                               ps[:, 2, :].rearrange("p (q a s) -> p q a s", q=4, a=2), ACT.Copy)\
                    .then_inc(xgT_sb, 1)

            def expert(c, i, k, last):
                n = num(c, i, k)
                act.wait_ge(glu_sb, n + 1)
                act.activation(sig, glu, ACT.Sigmoid, scale=ALPHA).then_inc(sig_sb, 1)
                act.wait_ge(ohgT_ps, n + 1)
                act.activation(ohgT, ps[:, 3, 0:NT], ACT.Copy).then_inc(ohgT_sb, 1)
                if not last:
                    copy_xg(n + 1)
                act.wait_ge(actT_ps, n + 1)
                act.activation(actT3, ps[:, 4, :].rearrange("p (c s) -> p c s", c=4), ACT.Copy)\
                    .then_inc(actT_sb, 1)
                if not last:
                    copy_xgT(n + 1)
                act.wait_ge(w2_used, n * 4 + 4)
                act.activation(ysb, ps[:, 3, :], ACT.Copy).then_inc(y_sb, 1)

            def first_pass(c):
                copy_xg(0)
                act.wait_ge(combT_ps, 1)
                act.activation(combT, ps[0:E, 5, 0:NT], ACT.Copy).then_inc(combT_sb, 1)
                copy_xgT(0)
                each_expert(act, c, expert)

            def later_pass(c):
                copy_xg(c * E)
                copy_xgT(c * E)
                each_expert(act, c, expert)

            run_passes(act, first_pass, later_pass)
            act.wait_ge(fin_sum, 1)
            act.activation(late0, late[CAP:CAP + NS, :], ACT.Copy).then_inc(late_sb, 1)
            for i in range(3):
                r = [P, P, NS][i]
                if i == 2:
                    act.wait_ge(fin_sum, 2)
                if i:
                    act.wait_ge(fin_sq, i)
                act.activation(fsq[0:r], h3[0:r, i], ACT.Square, accum_out=fssq[0:r, i:i + 1]).then_inc(fin_sq, 1)
                act.wait_ge(fin_sq, i + 1)
                act.activation(frstd[0:r, i:i + 1], fssq[0:r, i:i + 1], ACT.Sqrt, bias=eps_col[0:r],
                               scale=1.0 / D).then_inc(frstd_act, 1)

        @block.vector
        def _(dve):
            linked = [0]

            def link(ins):
                linked[0] += 1
                ins.then_inc(dve_link, 1)
                dve.wait_ge(dve_link, linked[0])

            dve.wait_ge(gains_ps, 1)
            dve.tensor_copy(gains, ps[:, 7, 0:24]).then_inc(gains_sb, 1)
            for i in range(3):
                r = TILE_ROWS[i]
                dve.wait_ge(rstd_x, i + 1)
                link(dve.reciprocal(rstd[0:r, i:i + 1], rstd[0:r, i:i + 1]))
                dve.tensor_scalar(xn3[0:r, i], x3[0:r, i], rstd[0:r, i:i + 1], None, ALU.mult).then_inc(xn_sb, 1)
            dve.wait_ge(lb_in, 16)
            link(dve.tensor_tensor(lbtmp, lb3[:, 0], lb3[:, 1], ALU.max))
            dve.tensor_tensor(lb3, lb3, bcast(lbtmp.unsqueeze(1), [P, 2, 512]), ALU.subtract).then_inc(lb_sub, 1)
            dve.wait_ge(gains_sb, 1)
            for t in range(1, KT, 2):
                dve.wait_ge(xT_ps, t + 1)
                dve.tensor_scalar(xT3[:, t], ps[:, t % 2, 0:TOK], gmix[:, t:t + 1], None, ALU.mult)\
                    .then_inc(xT_dve, 1)
            dve.wait_ge(crow_ps, 1)
            dve.tensor_copy(cT4, ps[:, 6, 0:64].rearrange("p (g b i) -> p g b i", g=4, i=2)).then_inc(cT_sb, 1)
            dve.wait_ge(lb_exp, 1)
            link(dve.tensor_tensor(lbtmp, lb3[:, 0], lb3[:, 1], ALU.add))
            link(dve.reciprocal(lbtmp, lbtmp))
            link(dve.tensor_tensor(lb3[:, 0], lb3[:, 0], lbtmp, ALU.mult))
            link(dve.tensor_scalar(lb3[:, 1], lb3[:, 0], -1.0, 1.0, ALU.mult, ALU.add))
            for i in range(3):
                r = TILE_ROWS[i]
                f = ftmp3[0:r, i]
                dve.wait_ge(fx_exp, i + 1)
                link(dve.tensor_scalar(f, f, 1.0, None, ALU.add))
                link(dve.reciprocal(f, f))
                link(dve.tensor_tensor(f, f, lb3[0:r, 1], ALU.mult))
                dve.tensor_tensor(f, f, lb3[0:r, 0], ALU.add).then_inc(f_sb, 1)
                dve.wait_ge(f_sb, i + 1)
                dve.tensor_scalar(kk3[0:r, i], f, -1.0, 1.0, ALU.mult, ALU.add).then_inc(kk_sb, 1)
            for i in range(3):
                g = sog3[:, i] if i < 2 else sogS
                o = ps[:, 2 + i, :] if i < 2 else ps[:, 4, 0:P]
                dve.wait_ge(og_exp, i + 1)
                link(dve.tensor_scalar(g, g, 1.0, None, ALU.add))
                link(dve.reciprocal(g, g))
                dve.tensor_tensor(g, g, o, ALU.mult).then_inc(sog_sb, 1)
            dve.wait_ge(kkT_sb, 3)
            dve.tensor_scalar(fS3, kS3, -1.0, 1.0, ALU.mult, ALU.add)

            tails = 0
            scores = 0
            for what, a in SCHEDULE:
                if what == "proj" and a[0] == HV:
                    j = a[1]
                    dve.wait_ge(hv_ps, j + 1)
                    dve.wait_ge(bg_sb, j + 1)
                    dve.tensor_tensor(bx3[:, j], ctmp, ps[:, 6, 0:TOK], ALU.mult).then_inc(bx_sb, 1)
                    dve.wait_ge(bx_sb, j + 1)
                    y = yT3[:, j, P0C:TOK]
                    ys = yT3[:, j, 0:NS]
                    w = [gconv[:, 4 * n + j:4 * n + j + 1] for n in range(3)]
                    dve.tensor_scalar(y, bx3[:, j, P0C:TOK], w[2], None, ALU.mult)
                    link(dve.tensor_scalar(ys, bx3[:, j, 0:NS], w[2], None, ALU.mult))
                    dve.scalar_tensor_tensor(y, bx3[:, j, P0C - 1:TOK - 1], w[1], y, ALU.mult, ALU.add)
                    link(dve.scalar_tensor_tensor(ys, cT4[:, j, :, 1], w[1], ys, ALU.mult, ALU.add))
                    dve.scalar_tensor_tensor(y, bx3[:, j, P0C - 2:TOK - 2], w[0], y, ALU.mult, ALU.add)
                    dve.scalar_tensor_tensor(ys, cT4[:, j, :, 0], w[0], ys, ALU.mult, ALU.add).then_inc(conv_sb, 1)
                if what == "proj" and a[0] == CG:
                    j = a[1]
                    dve.wait_ge(cg_ps, j + 1)
                    dve.wait_ge(conv_sb, j + 1)
                    dve.tensor_tensor(yT3[:, j, 0:NS], yT3[:, j, 0:NS], ps[:, 7, 0:NS], ALU.mult)
                    dve.tensor_tensor(yT3[:, j, P0C:TOK], yT3[:, j, P0C:TOK], ps[:, 7, P0C:TOK], ALU.mult)\
                        .then_inc(yconv_sb, 1)
                if what == "span":
                    c, l = STEPS[a]
                    dve.wait_ge(span_exp, a + 1)
                    dve.wait_ge(q_sb, HEADS)
                    dve.wait_ge(kkT_sb, 2)
                    if l == LEVELS:
                        dve.tensor_tensor(qhat3[:, c], ex3[:, a % 2], qC3[:, c], ALU.mult)
                        dve.tensor_copy(decay_all[:, 4 * c:4 * c + 4],
                                        ex3[:, a % 2].rearrange("p (h t) -> p h t", h=HEADS)[:, :, P - 1])\
                            .then_inc(ex_used, 1)
                    else:
                        h = 1 << l
                        split = lambda ap, half: ap.rearrange("p (m a i) -> p m a i", a=2, i=h)[:, :, half]
                        if a >= 2 and STEPS[a - 2][1] < LEVELS:
                            dve.wait_ge(score_ps, score_no(a - 2) + 1)
                        if a >= 3 and STEPS[a - 2][1] == LEVELS:
                            dve.wait_ge(score_ps, score_no(a - 4) + 1)
                        dve.tensor_tensor(split(wl3[:, a % 2], 0), split(ex3[:, a % 2], 0),
                                          split(kkC3[:, c], 0), ALU.mult)
                        dve.tensor_tensor(split(wl3[:, a % 2], 1), split(ex3[:, a % 2], 1),
                                          split(qC3[:, c], 1), ALU.mult).then_inc(ex_used, 1)
                if what in ("diag", "score"):
                    c = a if what == "diag" else STEPS[a][0]
                    dve.wait_ge(score_ps, scores + 1)
                    if scores:
                        dve.wait_ge(score_sb, scores)
                    got = ps[:, 2 + scores % 2, :].rearrange("p (h t) -> p h t", h=HEADS)
                    into = sc3[:, c].rearrange("p (h t) -> p h t", h=HEADS)
                    if what == "diag":
                        ins = dve.tensor_tensor(into, got, bcast(ident.unsqueeze(1), [P, HEADS, P]), ALU.mult)
                    else:
                        m = blocks3[:, STEPS[a][1]].bitcast(U32)
                        ins = dve.copy_predicated(into, bcast(m.unsqueeze(1), [P, HEADS, P]), got)
                    ins.then_inc(score_sb, 1)
                    scores += 1
                if what == "tail":
                    tails += 1
                    dve.wait_ge(tail_exp, tails)
                    dve.wait_ge(kkT_ps, 3)
                    if a == 2:
                        r = NS + NM
                        dve.scalar_tensor_tensor(kk_meta[0:r], tail3[0:r, tails % 2], meta_row[0:r], kk3[0:r, 2],
                                                 ALU.mult, ALU.mult).then_inc(khat_sb, 1)
                    else:
                        dve.tensor_tensor(kk3[:, a], kk3[:, a], tail3[:, tails % 2], ALU.mult).then_inc(khat_sb, 1)
            dve.wait_ge(state_ps, 1)
            dve.tensor_copy(srec3[:, 0], ps[:, 5, :]).then_inc(state_sb, 1)
            dve.wait_ge(ex_used, len(STEPS))
            for c in range(2):
                dve.wait_ge(state_ps, c + 2)
                dve.wait_ge(state_sb, c + 1)
                if c:
                    dve.wait_ge(o_ps, 1)
                for h in range(HEADS):
                    at = slice(h * P, (h + 1) * P)
                    last = dve.scalar_tensor_tensor(srec3[:, 1 - c, at], srec3[:, c, at],
                                                    decay_all[:, 4 * c + h:4 * c + h + 1], ps[:, 6 + c, at],
                                                    ALU.mult, ALU.add)
                last.then_inc(state_sb, 1)
            dve.tensor_copy(nconv3[:, :, 0:2], bx3[:, :, TOK - 2:TOK])
            after = nconv3[:, :, 2:].rearrange("p g (b i) -> p g b i", i=2)
            dve.tensor_copy(after[:, :, :, 0], cT4[:, :, :, 1])
            dve.tensor_copy(after[:, :, :, 1], bx3[:, :, 0:NS]).then_inc(nconv_sb, 1)
            dve.wait_ge(s0_in, 16 * HEADS)
            for h in range(HEADS):
                dve.tensor_tensor(s0[:, h], s0[:, h], bcast(fS3[:, h].unsqueeze(2), [P, NS, P]), ALU.mult)\
                    .then_inc(dve_link, 1)
                linked[0] += 1
                dve.wait_ge(dve_link, linked[0])
                dve.wait_ge(outer_ps, h + 1)
                dve.tensor_tensor(s0[:, h], s0[:, h], ps[:, 2:4, :].rearrange("p a (b v) -> p (a b) v", v=P),
                                  ALU.add).then_inc(snew_sb, 1)
                if h < 2:
                    dve.wait_ge(osq_sb, h + 1)
                    dve.tensor_reduce(ossq[:, 4 * h:4 * h + 4],
                                      ex3[:, h].rearrange("p (h v) -> p h v", h=HEADS), AX.X, ALU.add)\
                        .then_inc(oss_sb, 1)
            dve.wait_ge(ncrow_ps, 1)
            dve.tensor_copy(ncrow, ps[0:2 + 2 * NS, 5, :]).then_inc(ncrow_sb, 1)
            dve.wait_ge(os_ps, HEADS)
            dve.wait_ge(rec_out, 16)
            eye = bcast(ident.rearrange("p (h b) -> p b h", b=32)[:, 0:NS], [P, NS, HEADS])
            own = small[:, 92:92 + NS]
            link(dve.tensor_reduce(own, eye, AX.X, ALU.add))
            link(dve.tensor_tensor(ssum.rearrange("p (b v) -> p b v", b=NS),
                                   ps[:, 6:8, :].rearrange("p a (b v) -> p (a b) v", v=P),
                                   bcast(own.unsqueeze(2), [P, NS, P]), ALU.mult))
            dve.tensor_reduce(oS, ssum.rearrange("p (b v) -> p v b", b=NS), AX.X, ALU.add).then_inc(os_sb, 1)
            dve.wait_ge(ortd_sb, 1)
            link(dve.reciprocal(orstd, orstd))
            for c in range(2):
                by_head = lambda ap: ap.rearrange("p (h v) -> p h v", h=HEADS)
                link(dve.tensor_tensor(by_head(ex3[:, c]), by_head(ps[:, c, :]),
                                       bcast(orstd[:, 4 * c:4 * c + 4].unsqueeze(2), [P, HEADS, P]), ALU.mult))
                dve.tensor_tensor(sog3[:, c], ex3[:, c], sog3[:, c], ALU.mult).then_inc(yrec_sb, 1)
            dve.scalar_tensor_tensor(oS, oS, orstd[:, 8:9], sogS, ALU.mult, ALU.mult).then_inc(yrec_sb, 1)
            for c in range(2):
                dve.wait_ge(yT_ps, c + 1)
                at = TILE_COL[c]
                dve.tensor_tensor(yT3[:, 4:8, at:at + P],
                                  ps[:, (7, 0)[c], :].rearrange("p (h t) -> p h t", h=HEADS),
                                  bcast(grec.unsqueeze(2), [P, HEADS, P]), ALU.mult).then_inc(yTrec_sb, 1)
            dve.wait_ge(yT_ps, 3)
            dve.tensor_tensor(yT3[:, 4:8, 0:NS], ps[:, 1, 0:P].rearrange("p (h b) -> p h b", b=32)[:, :, 0:NS],
                              bcast(grec.unsqueeze(2), [P, HEADS, NS]), ALU.mult).then_inc(yTrec_sb, 1)
            dve.wait_ge(xres_in, 48)
            for i in range(2):
                dve.wait_ge(mix_ps, i + 1)
                dve.tensor_tensor(h3[:, i], h3[:, i], ps[:, 2 + 2 * i:4 + 2 * i, :].rearrange("p a n -> p (a n)"),
                                  ALU.add).then_inc(h_sb, 1)
            dve.wait_ge(mix_ps, 3)
            dve.tensor_tensor(h3[0:NS, 2, 0:HALF], h3[0:NS, 2, 0:HALF], ps[0:NS, 6, :], ALU.add)
            dve.wait_ge(hs_sb, 1)
            dve.tensor_tensor(h3[0:NS, 2, HALF:D], h3[0:NS, 2, HALF:D], hs_tmp, ALU.add).then_inc(h_sb, 1)
            dve.wait_ge(gffn_in, 16)
            for i in range(3):
                r = [P, P, NS][i]
                dve.wait_ge(hrstd_act, i + 1)
                link(dve.reciprocal(hrstd[0:r, i:i + 1], hrstd[0:r, i:i + 1]))
                dve.scalar_tensor_tensor(hn3[0:r, i], h3[0:r, i], hrstd[0:r, i:i + 1], gffn[0:r],
                                         ALU.mult, ALU.mult).then_inc(hn_sb, 1)
            for t in range(1, KT, 2):
                dve.wait_ge(hnT_ps, t + 1)
                dve.tensor_copy(hnT3[:, t], ps[:, t % 2, 0:NT]).then_inc(hnT_dve, 1)
            dve.wait_ge(route_const, 1)
            dve.wait_ge(logit_ps, 3)
            dve.tensor_copy(logits3[:, 0:2], ps[:, 7, 0:2 * E].rearrange("p (i e) -> p i e", e=E))
            link(dve.tensor_copy(logits3[0:NS, 2], ps[0:NS, 7, 2 * E:3 * E]))
            for i in range(3):
                last = dve.max(top8[:, i], logits3[:, i])
            link(last)
            for i in range(3):
                last = dve.max_index(idx8[:, i], top8[:, i], logits3[:, i])
            dve.tensor_tensor(gate4, top8[:, :, 0:TOPK], bcast(top8[:, :, 0:1], [P, 3, TOPK]), ALU.subtract)\
                .then_inc(gate_sub, 1)
            dve.wait_ge(gate_sub, 1)
            link(dve.tensor_copy(idxf, idx8))
            link(dve.tensor_tensor(eq_all, bcast(iota32.unsqueeze(1).unsqueeze(1), [P, 3, TOPK, E]),
                                   bcast(idxf[:, :, 0:TOPK].unsqueeze(3), [P, 3, TOPK, E]), ALU.is_equal))
            link(dve.tensor_reduce(member3, eq_all.rearrange("p i j e -> p i e j"), AX.X, ALU.add))
            link(dve.tensor_tensor(member3, member3, bcast(row_valid.unsqueeze(2), [P, 3, E]), ALU.mult))
            dve.tensor_copy(member_b3, member3).then_inc(member_sb, 1)
            dve.wait_ge(gate_exp, 1)
            link(dve.tensor_reduce(gsum, gate4, AX.X, ALU.add))
            link(dve.reciprocal(gsum, gsum))
            link(dve.tensor_tensor(gate4, gate4, bcast(gsum.unsqueeze(2), [P, 3, TOPK]), ALU.mult))
            link(dve.tensor_tensor(eq_all, eq_all, bcast(gate4.unsqueeze(3), [P, 3, TOPK, E]), ALU.mult))
            dve.tensor_reduce(comb3, eq_all.rearrange("p i j e -> p i e j"), AX.X, ALU.add).then_inc(comb_sb, 1)
            dve.wait_ge(pos_ps, 1)
            pos = ps[:, 6, 0:3 * E].rearrange("p (i e) -> p i e", e=E)
            link(dve.scalar_tensor_tensor(posm3, pos, 1.0, member3, ALU.add, ALU.mult))
            link(dve.tensor_scalar(posm3, posm3, -1.0, None, ALU.add))

            def one_hots(n, k, e):
                col = bass.ds(e, 1)
                dve.tensor_tensor(oh4[:, k], bcast(posm3[:, :, col], [P, 3, CAP]),
                                  bcast(iota64.unsqueeze(1), [P, 3, CAP]), ALU.is_equal).then_inc(oh_sb, 1)
                dve.wait_ge(oh_sb, n + 1)
                for half in range(2):
                    last = dve.tensor_tensor(ohg4[:, k, :, CAP * half:CAP * half + CAP], oh4[:, k],
                                             bcast(comb3[:, :, col], [P, 3, CAP]), ALU.mult)
                last.then_inc(ohg_sb, 1)

            def add_rows(nth):
                dve.wait_ge(rows_ps, nth * 3 + 1)
                dve.tensor_tensor(h3[:, 0], h3[:, 0], ps[:, 6:8, :].rearrange("p a n -> p (a n)"), ALU.add)\
                    .then_inc(added, 1)
                dve.wait_ge(rows_ps, nth * 3 + 2)
                dve.tensor_tensor(h3[:, 1], h3[:, 1], ps[:, 4:6, :].rearrange("p a n -> p (a n)"), ALU.add)\
                    .then_inc(added, 1)
                dve.wait_ge(rows_ps, nth * 3 + 3)
                dve.tensor_tensor(h3[0:NS, 2, 0:HALF], h3[0:NS, 2, 0:HALF], ps[0:NS, 3, :], ALU.add)
                dve.tensor_tensor(late[CAP:CAP + NS, :], late[CAP:CAP + NS, :], ps[CAP:CAP + NS, 3, :], ALU.add)\
                    .then_inc(added, 1)

            def expert(c, i, k, last, adds=None):
                n = num(c, i, k)
                if not last:
                    if adds != "biases":
                        dve.wait_ge(ohgT_ps, n)
                    one_hots(n + 1, 1 - k, i * 2 + k + 1)
                if adds != "none":
                    add_rows(n)
                dve.wait_ge(w1_used, n * 8 + 8)
                dve.tensor_scalar(glu, psA[:, 0:D:2], LIMIT, None, ALU.min).then_inc(glu_sb, 1)
                dve.tensor_scalar(lin, psA[:, 1:D:2], -LIMIT, LIMIT, ALU.max, ALU.min).then_inc(lin_sb, 1)
                dve.wait_ge(lin_sb, n + 1)
                dve.scalar_tensor_tensor(lin, lin, 1.0, glu, ALU.add, ALU.mult).then_inc(gl_sb, 1)
                dve.wait_ge(gl_sb, n + 1)
                dve.wait_ge(sig_sb, n + 1)
                dve.tensor_tensor(act, lin, sig, ALU.mult).then_inc(act_sb, 1)

            def first_pass(c):
                one_hots(0, 0, 0)
                link(dve.tensor_reduce(maxcount, ps[:, 6, 3 * E:4 * E], AX.X, ALU.max))
                dve.tensor_copy(maxcount_i, maxcount).then_inc(max_sb, 1)
                link(dve.memset(late[CAP:CAP + NS, :], 0.0))
                expert(c, 0, 0, False, adds="biases")
                expert(c, 0, 1, False)
                each_expert(dve, c, expert, start=1)
                add_rows(E)

            def later_pass(c):
                dve.wait_ge(ohgT_ps, c * E)
                dve.tensor_scalar(posm3, posm3, -float(CAP), None, ALU.add).then_inc(pos_moved, 1)
                dve.wait_ge(pos_moved, c)
                one_hots(c * E, 0, 0)
                expert(c, 0, 0, False, adds="none")
                expert(c, 0, 1, False)
                each_expert(dve, c, expert, start=1)
                add_rows(c * E + E)

            run_passes(dve, first_pass, later_pass)
            dve.memset(small[:, 91:92], 0.0).then_inc(fin_sum, 1)
            dve.wait_ge(late_sb, 1)
            dve.tensor_tensor(h3[0:NS, 2, HALF:D], h3[0:NS, 2, HALF:D], late0, ALU.add).then_inc(fin_sum, 1)
            dve.wait_ge(gfin_in, 16)
            for i in range(3):
                r = [P, P, NS][i]
                dve.wait_ge(frstd_act, i + 1)
                link(dve.reciprocal(frstd[0:r, i:i + 1], frstd[0:r, i:i + 1]))
                dve.scalar_tensor_tensor(h3[0:r, i], h3[0:r, i], frstd[0:r, i:i + 1], gfin[0:r],
                                         ALU.mult, ALU.mult).then_inc(fin_sb, 1)

        @block.tensor
        def _(pe):
            mm = pe.matmul
            pe.wait_ge(pool_const, 1)
            pe.wait_ge(gain_in, 48)
            pe.transpose(ps[:, 7, 0:24], gain_rows, ident[0:24, 0:24]).then_inc(gains_ps, 1)
            pe.wait_ge(crow_in, 16)
            for g in range(4):
                last = pe.transpose(ps[:, 6, 16 * g:16 * g + 16], crow[:, g * P:(g + 1) * P],
                                    ident[0:2 * NS, 0:2 * NS])
            last.then_inc(crow_ps, 1)
            pe.wait_ge(xn_sb, 3)
            for t in range(KT):
                if t >= 2:
                    pe.wait_ge((xT_act, xT_dve)[t % 2], t // 2)
                for i in range(3):
                    r, at = TILE_ROWS[i], TILE_COL[i]
                    last = pe.transpose(ps[:, t % 2, at:at + r], xn3[0:r, i, t * P:(t + 1) * P], ident[0:r, 0:r])
                last.then_inc(xT_ps, 1)
            pe.wait_ge(xT_act, 4)
            pe.wait_ge(xT_dve, 4)

            def rows_of(g, bank, done):
                pe.wait_ge(win_in[g], 16)
                for i in range(3):
                    r, at = TILE_ROWS[i], TILE_COL[i]
                    for t in range(KT):
                        last = mm(ps[0:r, bank + i, :], xT3[:, t, at:at + r], w_sb[g][:, t, :],
                                  start=(t == 0), stop=(t == KT - 1))
                    last.then_inc(done, 1)

            def columns_of(g, j, bank, done):
                pe.wait_ge(win_in[g], 16)
                for t in range(KT):
                    last = mm(ps[:, bank, 0:TOK], w_sb[g][:, t, j * P:(j + 1) * P], xT3[:, t, :],
                              start=(t == 0), stop=(t == KT - 1))
                last.then_inc(done, 1)

            rows_of(FX, 2, fx_ps)
            pe.wait_ge(cT_sb, 1)
            rows_of(IV, 5, iv_ps)
            for h in range(HEADS):
                if h >= 2:
                    pe.wait_ge(q_sb, h - 1)
                columns_of(QG, h, h % 2, q_ps)
            pe.wait_ge(win_in[OG], 16)
            pe.wait_ge(fx_exp, 3)
            for i in range(2):
                for t in range(KT):
                    last = mm(ps[:, 2 + i, :], xT3[:, t, TILE_COL[i]:TILE_COL[i] + P], w_sb[OG][:, t, :],
                              start=(t == 0), stop=(t == KT - 1))
                last.then_inc(og_ps, 1)
            for t in range(KT):
                for h in range(HEADS):
                    last = mm(ps[32 * h:32 * h + 32, 4, 0:P], xT3[:, t, 0:32], w_sb[OG][:, t, h * P:(h + 1) * P],
                              start=(t == 0), stop=(t == KT - 1))
            last.then_inc(og_ps, 1)
            pe.wait_ge(kk_sb, 3)
            pe.wait_ge(v_sb, 3)
            pe.wait_ge(q_sb, HEADS)
            for i in range(2):
                for h in range(HEADS):
                    last = pe.transpose(ps[:, i, h * P:(h + 1) * P], kk3[:, i, h * P:(h + 1) * P], ident)
                last.then_inc(kkT_ps, 1)
            for h in range(HEADS):
                last = pe.transpose(ps[:, 5, NS * h:NS * (h + 1)], kk3[0:NS, 2, h * P:(h + 1) * P],
                                    ident[0:NS, 0:NS])
            last.then_inc(kkT_ps, 1)
            pe.wait_ge(logf_sb, 3)
            pe.wait_ge(v_sb, 3)

            scores = 0
            tails = 0
            for what, a in SCHEDULE:
                if what == "proj":
                    g, j = a
                    bank, done, used = {BG: (5, bg_ps, bg_sb), HV: (6, hv_ps, bx_sb), CG: (7, cg_ps, yconv_sb)}[g]
                    pe.wait_ge(*((used, j) if j else (kkT_sb, 3)))
                    columns_of(g, j, bank, done)
                if what == "span":
                    c, l = STEPS[a]
                    if a < 2:
                        pe.wait_ge(kkT_sb, a + 1)
                    else:
                        pe.wait_ge(span_exp, a - 1)
                    for h in range(HEADS):
                        last = mm(ps[:, a % 2, h * P:(h + 1) * P], logf3[:, c, h * P:(h + 1) * P],
                                  spans3[:, l] if l < LEVELS else prefix, start=True, stop=True)
                    last.then_inc(span_ps, 1)
                if what in ("diag", "score"):
                    if scores < 2:
                        pe.wait_ge(sog_sb, scores + 1)
                    else:
                        pe.wait_ge(score_sb, scores - 1)
                    if what == "diag":
                        pe.wait_ge(kkT_sb, 2)
                        left, right = kkC3[:, a], qC3[:, a]
                    else:
                        pe.wait_ge(ex_used, a + 1)
                        left = right = wl3[:, a % 2]
                    for h in range(HEADS):
                        at = slice(h * P, (h + 1) * P)
                        last = mm(ps[:, 2 + scores % 2, at], left[:, at], right[:, at], start=True, stop=True)
                    last.then_inc(score_ps, 1)
                    scores += 1
                if what == "tail":
                    r = TILE_ROWS[a]
                    if tails == 0:
                        pe.wait_ge(sog_sb, 3)
                        pe.wait_ge(kkT_sb, 3)
                    else:
                        pe.wait_ge(tail_exp, tails)
                    tails += 1
                    mm(ps[0:r, 4, :], suffix[0:r, 0:r], logf3[0:r, a, :], start=True, stop=True).then_inc(tail_ps, 1)
            r = NS + NM
            pe.wait_ge(khat_sb, 3)
            pe.wait_ge(bg_sb, 4)
            pe.wait_ge(bx_sb, 4)
            pe.wait_ge(yconv_sb, 4)
            for n, (keys, vals_) in enumerate([(kk_meta[0:r], vtok3[0:r, 2]), (kk3[:, 0], vtok3[:, 0]),
                                               (kk3[:, 1], vtok3[:, 1])]):
                for h in range(HEADS):
                    at = slice(h * P, (h + 1) * P)
                    last = mm(ps[:, 5 + n, at], keys[:, at], vals_[:, at], start=True, stop=True)
                last.then_inc(state_ps, 1)

            def outer(h):
                if h:
                    pe.wait_ge(snew_sb, h)
                pe.wait_ge(vdiag_sb, h + 1)
                for n in range(2):
                    last = mm(ps[:, 2 + n, :], kk3[0:NS, 2, h * P:(h + 1) * P], vdiag[:, n * 512:(n + 1) * 512],
                              start=True, stop=True)
                last.then_inc(outer_ps, 1)

            def recur(c):
                pe.wait_ge(state_sb, c + 1)
                for h in range(HEADS):
                    at = slice(h * P, (h + 1) * P)
                    mm(ps[:, c, at], sc3[:, c, at], vtok3[:, c, at], start=True, stop=False)
                    last = mm(ps[:, c, at], qhat3[:, c, at], srec3[:, c, at], start=False, stop=True)
                last.then_inc(o_ps, 1)

            pe.wait_ge(score_sb, len(SCORES))
            pe.wait_ge(ex_used, len(STEPS))
            outer(0)
            recur(0)
            outer(1)
            recur(1)
            outer(2)
            pe.wait_ge(nconv_sb, 1)
            for g in range(4):
                last = pe.transpose(ps[0:2 + 2 * NS, 5, g * P:(g + 1) * P], nconv3[:, g], ident)
            last.then_inc(ncrow_ps, 1)
            outer(3)
            pe.wait_ge(state_sb, 3)
            for h in range(HEADS):
                pe.wait_ge(snew_sb, h + 1)
                for n in range(2):
                    last = mm(ps[32 * h:32 * h + 32, 6 + n, :], qS3[:, h],
                              s0[:, h].rearrange("p b v -> p (b v)")[:, n * 512:(n + 1) * 512],
                              start=True, stop=True)
                last.then_inc(os_ps, 1)

            def mix(i, first):
                pe.wait_ge(wout_in[0 if first else 1], 16)
                for n in range(2):
                    for t in range(4):
                        k = t if first else 4 + t
                        last = mm(ps[:, 2 + 2 * i + n, :], yT3[:, k, TILE_COL[i]:TILE_COL[i] + P],
                                  wout_sb[k // 4][:, t, n * 512:(n + 1) * 512], start=(k == 0), stop=(k == KT - 1))
                return last

            mix(0, True)
            pe.wait_ge(ncrow_sb, 1)
            mix(1, True)
            for c in range(2):
                pe.wait_ge(yrec_sb, c + 1)
                for h in range(HEADS):
                    last = pe.transpose(ps[:, (7, 0)[c], h * P:(h + 1) * P], sog3[:, c, h * P:(h + 1) * P], ident)
                last.then_inc(yT_ps, 1)
            pe.wait_ge(yrec_sb, 3)
            pe.transpose(ps[:, 1, 0:P], oS, ident).then_inc(yT_ps, 1)
            for i in range(2):
                pe.wait_ge(yTrec_sb, i + 1)
                mix(i, False).then_inc(mix_ps, 1)
            pe.wait_ge(yTrec_sb, 3)
            for k in range(KT):
                for n in range(2):
                    last = mm(ps[32 * n:32 * n + NS, 6, :], yT3[:, k, 0:NS],
                              wout_sb[k // 4][:, k % 4, n * 512:(n + 1) * 512], start=(k == 0), stop=(k == KT - 1))
            last.then_inc(mix_ps, 1)
            pe.wait_ge(hn_sb, 3)
            for t in range(KT):
                if t >= 2:
                    pe.wait_ge((hnT_act, hnT_dve)[t % 2], t // 2)
                for i in range(3):
                    r = [P, P, NS][i]
                    last = pe.transpose(ps[:, t % 2, i * P:i * P + r], hn3[0:r, i, t * P:(t + 1) * P], ident[0:r, 0:r])
                last.then_inc(hnT_ps, 1)
            pe.wait_ge(hnT_act, 4)
            pe.wait_ge(hnT_dve, 4)
            pe.wait_ge(const_in, 32)
            pe.wait_ge(route_const, 1)
            for t in range(KT):
                g = t % 4
                last = mm(ps[32 * g:32 * g + 32, 2, 0:NT], router3[:, t], hnT3[:, t], start=(t < 4), stop=(t >= 4))
            last.then_inc(logitT_ps, 1)
            pe.wait_ge(logitT_sb, 1)
            for i in range(3):
                r = [P, P, NS][i]
                out = ps[0:r, 7, i * E:(i + 1) * E]
                mm(out, ones[0:1, 0:r], rbrow, start=True, stop=False)
                mm(out, logitT[:, i * P:i * P + r], stack, start=False, stop=True).then_inc(logit_ps, 1)
            pe.wait_ge(member_sb, 1)
            for i in range(3):
                for m in range(i + 1):
                    mm(ps[:, 6, i * E:(i + 1) * E], strict_b if m == i else ones_b, member_b3[:, m],
                       start=(m == 0), stop=(m == i))
            for m in range(3):
                last = mm(ps[:, 6, 3 * E:4 * E], ones_b, member_b3[:, m], start=(m == 0), stop=(m == 2))
            last.then_inc(pos_ps, 1)

            def pick(n, k):
                pe.wait_ge(oh_sb, n + 1)
                for i in range(3):
                    r = [P, P, NS][i]
                    for half in range(2):
                        last = mm(ps[64 * half:64 * half + 64, 2, :], oh4[0:r, k, i],
                                  hn3[0:r, i, half * HALF:(half + 1) * HALF], start=(i == 0), stop=(i == 2))
                last.then_inc(xg_ps, 1)

            def turn(n):
                pe.wait_ge(xg_sb, n + 1)
                for q in range(4):
                    last = pe.transpose(ps[:, 2, q * P:(q + 1) * P], xg[:, q * P:(q + 1) * P], ident)
                last.then_inc(xgT_ps, 1)

            order = [(0, 0), (1, 0), (0, 1), (1, 1)]

            def bias(half, n2):
                col = half * D + n2 * 512
                return mm(psA[64 * half:64 * half + 64, n2 * 512:(n2 + 1) * 512], ones[0:1, 0:CAP],
                          b1r[:, col:col + 512], start=True, stop=False)

            def biases(n):
                pe.wait_ge(b1_in, n * 16 + 16)
                for half, n2 in order:
                    last = bias(half, n2)
                last.then_inc(b1_used, 1)

            def expert(c, i, k, last, adds=None):
                n = num(c, i, k)
                pe.wait_ge(xgT_sb, n + 1)
                for t in range(KT):
                    pe.wait_ge(w1_in[t], n * 16 + 16)
                    for half, n2 in order:
                        col = half * D + n2 * 512
                        done = mm(psA[64 * half:64 * half + 64, n2 * 512:(n2 + 1) * 512],
                                  xgT3[:, t], w1r[:, t, col:col + 512], start=False, stop=(t == KT - 1))
                    done.then_inc(w1_used, 1)
                    if t < 3 and adds != "none":
                        if adds == "biases":
                            rows(0, t, lambda half: combT, lambda half: b2_sb[:, half * HALF:(half + 1) * HALF])
                        else:
                            y_rows(n, t)
                pe.wait_ge(ohg_sb, n + 1)
                pe.wait_ge(added, n * 3 + 3)
                for m in range(3):
                    r = [P, P, NS][m]
                    done = pe.transpose(ps[:, 3, m * P:m * P + r], ohg4[0:r, k, m], ident[0:r, 0:r])
                done.then_inc(ohgT_ps, 1)
                if not last:
                    pick(n + 1, 1 - k)
                pe.wait_ge(act_sb, n + 1)
                for q in range(4):
                    done = pe.transpose(ps[:, 4, q * P:(q + 1) * P], act[:, q * P:(q + 1) * P], ident)
                done.then_inc(actT_ps, 1)
                pe.wait_ge(actT_sb, n + 1)
                pe.wait_ge(ohgT_sb, n + 1)
                if not last:
                    pe.wait_ge(b1_in, n * 16 + 32)
                for t in range(KT):
                    if t % 2 == 0:
                        pe.wait_ge(w2_in[4 * k + t // 2], use(c, i) * 16 + 16)
                    for half in range(2):
                        col = (t % 2) * D + half * HALF
                        done = mm(ps[64 * half:64 * half + 64, 3, :],
                                  actT3[:, t % 4, 64 * (t // 4):64 * (t // 4) + 64],
                                  w2r[:, 4 * k + t // 2, col:col + HALF], start=(t == 0), stop=(t == KT - 1))
                    if t % 2:
                        done.then_inc(w2_used, 1)
                    if t < 4 and not last:
                        done = bias(*order[t])
                        if t == 3:
                            done.then_inc(b1_used, 1)
                if not last:
                    turn(n + 1)

            def rows(nth, m, left, right):
                r = [P, P, NS][m]
                out = [ps[:, 6:8, :], ps[:, 4:6, :]][m] if m < 2 else None
                for half in range(2):
                    to = out[:, half] if m < 2 else ps[CAP * half:CAP * half + NS, 3, :]
                    last = mm(to, left(half)[:, m * P:m * P + r], right(half), start=True, stop=True)
                last.then_inc(rows_ps, 1)

            def y_rows(nth, m):
                if m == 0:
                    pe.wait_ge(y_sb, nth)
                    pe.wait_ge(added, nth * 3 - 2)
                if m == 1:
                    pe.wait_ge(added, nth * 3)
                rows(nth, m, lambda half: ohgT[64 * half:64 * half + 64], lambda half: ysb[64 * half:64 * half + 64])

            def rows_after(nth):
                for m in range(3):
                    y_rows(nth, m)

            def first_pass(c):
                pick(0, 0)
                biases(0)
                pe.wait_ge(comb_sb, 1)
                for i in range(3):
                    r = [P, P, NS][i]
                    last = pe.transpose(ps[0:E, 5, i * P:i * P + r], comb3[0:r, i], ident[0:r, 0:r])
                last.then_inc(combT_ps, 1)
                turn(0)
                pe.wait_ge(b2_in, 16)
                pe.wait_ge(combT_sb, 1)
                pe.wait_ge(max_sb, 1)
                expert(c, 0, 0, False, adds="biases")
                expert(c, 0, 1, False)
                each_expert(pe, c, expert, start=1)
                rows_after(E)

            def later_pass(c):
                pick(c * E, 0)
                turn(c * E)
                biases(c * E)
                expert(c, 0, 0, False, adds="none")
                expert(c, 0, 1, False)
                each_expert(pe, c, expert, start=1)
                rows_after(c * E + E)

            run_passes(pe, first_pass, later_pass)


INPUTS = ["x_prompt", "x_sample", "state_conv", "state_rec", "meta_tokens", "norm_mix", "w_in", "conv_w",
          "rec_lower_bound", "rec_norm", "w_out", "norm_ffn", "router_w", "router_b", "expert_w1", "expert_b1",
          "expert_w2", "expert_b2", "norm_final"]
OUTPUT_SHAPES = [(1, NP, D), (NS, 1, D), (1, 1, 2, HALF), (1, 1, HEADS, P, P), (1, NS, 2, HALF),
                 (1, NS, HEADS, P, P)]


def kernel(**inputs):
    import numpy as np
    import concourse.bacc as bacc
    from concourse.bass_utils import run_bass_kernel_spmd

    nc = bacc.Bacc("TRN2", target_bir_lowering=False, num_devices=1)
    arrays, args = {}, []
    for name in INPUTS:
        a = np.ascontiguousarray(inputs[name])
        arrays[f"in_{name}"] = a
        args.append(nc.dram_tensor(f"in_{name}", a.shape, mybir.dt.from_np(a.dtype), kind="ExternalInput").ap())
    for i, shape in enumerate(OUTPUT_SHAPES):
        args.append(nc.dram_tensor(f"out_{i}", shape, F32, kind="ExternalOutput").ap())
    build_step(nc, *args)
    r = run_bass_kernel_spmd(nc, [arrays], core_ids=[0])
    return tuple(r.results[0][f"out_{i}"] for i in range(len(OUTPUT_SHAPES)))
```

```python
import concourse.bass as bass
from concourse import mybir
from contextlib import ExitStack

F32 = mybir.dt.float32
BF16 = mybir.dt.bfloat16
U32 = mybir.dt.uint32
I32 = mybir.dt.int32
ALU = mybir.AluOpType
ACT = mybir.ActivationFunctionType
AX = mybir.AxisListType

P = 128
D = 1024
KT = D // P
HALF = D // 2
NS, NM, NP = 8, 16, 256
S0C, P0C = 0, NS + NM
TOK = NS + NM + NP
NT = NP + NS
HEADS = 4
E = 32
TOPK = 4
CAP = 64
PASSES = -(-NT // CAP)
LEVELS = 7
EPS = 1e-5
LIMIT = 7.0
ALPHA = 1.702
BG, CG, HV, QG, FX, IV, OG = range(7)
ORDER = [2, 0, 1]
TILE_COL = [P0C, P0C + P, 0]
TILE_ROWS = [P, P, NS + NM]
WIDE = [4 * P, 4 * P, P]


def bcast(ap, shape):
    return ap.to_broadcast(shape)


def build_step(nc, x_prompt, x_sample, state_conv, state_rec, meta_tokens, norm_mix, w_in, conv_w,
               rec_lower_bound, rec_norm, w_out, norm_ffn, router_w, router_b, expert_w1, expert_b1,
               expert_w2, expert_b2, norm_final,
               y_prompt, y_sample, new_conv_prompt, new_rec_prompt, new_conv_sample, new_rec_sample):
    ctx = ExitStack()
    with ctx:
        def sem(name):
            return ctx.enter_context(nc.semaphore(name))

        w1r = ctx.enter_context(nc.sbuf_tensor("w1r", [P, 8, 2048], F32))
        w2r = ctx.enter_context(nc.sbuf_tensor("w2r", [P, 8, 2048], F32))
        ARENA = 20440
        mem = ctx.enter_context(nc.sbuf_tensor("mem", [P, ARENA], F32))
        top = [0]

        def take(n):
            a = top[0]
            top[0] += n
            assert top[0] <= ARENA, top[0]
            return mem[:, a:a + n]


        ident = take(P)
        prefix = take(P)
        suffix = take(P)
        suffix_s = take(P)
        spans = take(LEVELS * P)
        blocks = take(LEVELS * P)
        gains = take(24)
        small = take(P)
        router_sb = take(KT * E)
        lb2 = take(2 * 512)
        xT = take(KT * TOK)
        kk = take(3 * 512)
        logf = take(3 * 512)
        vtok = take(3 * 512)
        sog = take(2 * 512)
        kk_meta = take(512)
        qC = take(2 * 512)
        kkC = take(2 * 512)
        qS = take(HEADS * 32)
        kS = take(HEADS * NS)
        qhat = take(2 * 512)
        srec = take(2 * 512)
        bx = take(4 * TOK)
        ctmp = take(TOK)
        cT = take(4 * 2 * NS)
        nconv = take(4 * (2 + 2 * NS))
        yT = take(KT * TOK)

        def cut(ap, n):
            return ap.rearrange("p (a n) -> p a n", n=n)

        def from_(ap, n, at=0):
            return mem[:, ap.offset + at:ap.offset + at + n]

        spans3, blocks3 = cut(spans, P), cut(blocks, P)
        lb3, xT3, kk3, logf3, vtok3, sog3 = cut(lb2, 512), cut(xT, TOK), cut(kk, 512), cut(logf, 512), cut(vtok, 512), cut(sog, 512)
        qC3, kkC3, qS3, kS3, qhat3, srec3 = cut(qC, 512), cut(kkC, 512), cut(qS, 32), cut(kS, NS), cut(qhat, 512), cut(srec, 512)
        bx3, yT3, router3 = cut(bx, TOK), cut(yT, TOK), cut(router_sb, E)
        cT4 = cT.rearrange("p (g b i) -> p g b i", g=4, i=2)
        nconv3 = cut(nconv, 2 + 2 * NS)
        gmix, gconv, grec = gains[:, 0:8], gains[:, 8:20], gains[:, 20:24]
        ssq, rstd = small[:, 0:3], small[:, 3:6]
        ossq, orstd = small[:, 6:15], small[:, 15:24]
        hssq, hrstd = small[:, 24:27], small[:, 27:30]
        fssq, frstd = small[:, 30:33], small[:, 33:36]
        eps_col = small[:, 36:37]
        meta_row = small[:, 37:38]
        head = small[:, 100:100 + HEADS]
        meta_of = small[:, 104:104 + HEADS]
        own = small[:, 92:92 + NS]
        rbrow = small[0:1, 40:72]
        maxcount = small[:, 72:73]
        maxcount_i = small[:, 73:74].bitcast(I32)
        decay_all = small[:, 80:88]
        hi = w2r[:, 4:6, :].rearrange("p a n -> p (a n)")
        lo = w2r[:, 6:8, :].rearrange("p a n -> p (a n)")
        x3 = cut(hi[:, 0:3072], D)
        xn3 = cut(lo[:, 0:3072], D)
        gain_rows = lo[0:24, 3072:3200]
        ex3 = cut(hi[:, 0:1024], 512)
        wl3 = cut(hi[:, 1024:2048], 512)
        sc3 = cut(hi[:, 2048:3072], 512)
        vdiag = hi[:, 3072:4096]
        s0 = lo.rearrange("p (h b v) -> p h b v", h=HEADS, b=NS)
        ftmp3 = cut(yT[:, 0:1536], 512)
        lbtmp = yT[:, 1536:2048]
        v_heads = lb2[:, 512:1024]
        lb_s3 = cut(from_(ctmp, 2 * P), P)
        tail3 = cut(yT[:, 1120:2144], 512)
        fS3 = cut(lb2[:, 256:256 + HEADS * NS], NS)
        ssum = from_(kkC, 1024)
        hs_parts = [from_(qC, 512, 512 * g)[0:NS, :] for g in range(3)]
        crow = qhat[0:2 * NS, 0:512]
        ncrow = lb2[0:2 + 2 * NS, 512:1024]
        sogS, oS = lb2[:, 0:128], lb2[:, 128:256]
        h3 = cut(from_(kk, 3 * D), D)
        hn3 = cut(from_(vtok, 3 * D), D)
        hnT3 = cut(xT[:, 0:KT * NT], NT)
        gffn = qhat
        b2_sb = bx[0:E, 0:D]
        route = from_(spans, 2 * LEVELS * P)
        logits3 = cut(route[:, 0:96], E)
        top8 = cut(route[:, 96:120], 8)
        idx8 = cut(route[:, 120:144].bitcast(U32), 8)
        idxf = cut(route[:, 144:168], 8)
        gate4 = cut(route[:, 168:180], TOPK)
        gsum = route[:, 180:183]
        comb3 = cut(route[:, 192:288], E)
        member3 = cut(route[:, 288:384], E)
        posm3 = cut(route[:, 384:480], E)
        iota32 = route[:, 480:512]
        iota64 = route[:, 512:576]
        row_valid = route[:, 576:579]
        member_b3 = cut(route[:, 580:628].bitcast(BF16), E)
        stack = route[:, 640:672]
        ones_b = route[:, 672:736].bitcast(BF16)
        strict_b = route[:, 736:800].bitcast(BF16)
        ones = route[:, 800:800 + P]
        combT = route[0:E, 928:928 + NT]
        logitT = route[:, 1200:1200 + NT]
        eq_all = from_(qhat, 3 * TOPK * E).rearrange("p (i j e) -> p i j e", i=3, j=TOPK)
        oh4 = from_(qhat, 2 * 3 * CAP, 384).rearrange("p (k i s) -> p k i s", k=2, i=3)
        ohg4 = from_(srec, 2 * 3 * P).rearrange("p (k i s) -> p k i s", k=2, i=3)
        ohgT = from_(kkC, NT)
        late = from_(kkC, HALF, 384)
        xg, xgT3 = from_(lb2, HALF), cut(from_(lb2, HALF, HALF), CAP)
        b1r = from_(yT, 2048)[0:1, :]
        glu, sig, lin, act = [from_(xT, 512, 512 * n) for n in range(4)]
        actT3 = cut(from_(qC, HALF), P)
        ysb = from_(qC, HALF, HALF)
        gfin = from_(bx, D)
        fsq = from_(xT, D)
        late0 = from_(xT, HALF, D)[0:NS, :]

        ps = ctx.enter_context(nc.psum_tensor("ps", [P, 8, 512], F32))
        psA = ps[:, 0:2, :].rearrange("p a n -> p (a n)")

        x_in = [sem(f"x_in{i}") for i in range(3)]
        gain_in, lb_in, crow_in, s0_in, const_in, xres_in, gffn_in, b2_in, gfin_in = [
            sem(n) for n in ("gain_in", "lb_in", "crow_in", "s0_in", "const_in", "xres_in",
                             "gffn_in", "b2_in", "gfin_in")]
        win_in = [sem(f"win_in{g}") for g in range(7)]
        wout_in = [sem(f"wout_in{g}") for g in range(2)]
        w1_in = [sem(f"w1_in{t}") for t in range(8)]
        w2_in = [sem(f"w2_in{t}") for t in range(8)]
        b1_in = sem("b1_in")
        out_done, state_out, rec_out, conv_out = [
            sem(n) for n in ("out_done", "state_out", "rec_out", "conv_out")]
        pool_const, pool_link, dve_link = [sem(n) for n in ("pool_const", "pool_link", "dve_link")]
        ident_sb, own_sb, fS_sb, s0f_sb, mixc_ps = [
            sem(n) for n in ("ident_sb", "own_sb", "fS_sb", "s0f_sb", "mixc_ps")]
        gains_ps, gains_sb, x_sq, rstd_x, xn_sb, xT_ps, xT_act, xT_dve, crow_ps, cT_sb = [
            sem(n) for n in ("gains_ps", "gains_sb", "x_sq", "rstd_x", "xn_sb", "xT_ps", "xT_act", "xT_dve",
                             "crow_ps", "cT_sb")]
        lb_sub, lb_exp = [sem(n) for n in ("lb_sub", "lb_exp")]
        fx_ps, fx_exp, f_sb, logf_sb, kk_sb, iv_ps, v_sb, q_ps, q_sb, og_ps, og_exp, sog_sb = [
            sem(n) for n in ("fx_ps", "fx_exp", "f_sb", "logf_sb", "kk_sb", "iv_ps", "v_sb", "q_ps", "q_sb",
                             "og_ps", "og_exp", "sog_sb")]
        kkT_ps, kkT_sb, span_ps, span_exp, ex_used, score_ps, score_sb, tail_ps, tail_exp, khat_sb = [
            sem(n) for n in ("kkT_ps", "kkT_sb", "span_ps", "span_exp", "ex_used", "score_ps", "score_sb",
                             "tail_ps", "tail_exp", "khat_sb")]
        bg_ps, bg_sb, hv_ps, bx_sb, cg_ps, conv_sb, yconv_sb, nconv_sb, ncrow_ps, ncrow_sb = [
            sem(n) for n in ("bg_ps", "bg_sb", "hv_ps", "bx_sb", "cg_ps", "conv_sb", "yconv_sb", "nconv_sb",
                             "ncrow_ps", "ncrow_sb")]
        state_ps, state_sb, o_ps, osq_sb, oss_sb, ortd_sb, yrec_sb, yT_ps, yTrec_sb, hs_sb = [
            sem(n) for n in ("state_ps", "state_sb", "o_ps", "osq_sb", "oss_sb", "ortd_sb", "yrec_sb", "yT_ps",
                             "yTrec_sb", "hs_sb")]
        vdiag_sb, outer_ps, snew_sb, os_ps, os_sb = [
            sem(n) for n in ("vdiag_sb", "outer_ps", "snew_sb", "os_ps", "os_sb")]
        mix_ps, h_sb, h_sq, hrstd_act, hn_sb, hnT_ps, hnT_act, hnT_dve, logit_ps = [
            sem(n) for n in ("mix_ps", "h_sb", "h_sq", "hrstd_act", "hn_sb", "hnT_ps", "hnT_act", "hnT_dve",
                             "logit_ps")]
        logitT_ps, logitT_sb, gate_sub, gate_exp, member_sb, pos_ps, combT_ps, combT_sb, comb_sb, max_sb = [
            sem(n) for n in ("logitT_ps", "logitT_sb", "gate_sub", "gate_exp", "member_sb", "pos_ps", "combT_ps",
                             "combT_sb", "comb_sb", "max_sb")]
        pos_moved, oh_sb, ohg_sb, xg_ps, xg_sb, xgT_ps, xgT_sb, ohgT_ps, ohgT_sb = [
            sem(n) for n in ("pos_moved", "oh_sb", "ohg_sb", "xg_ps", "xg_sb", "xgT_ps", "xgT_sb", "ohgT_ps",
                             "ohgT_sb")]
        w1_used, w2_used, b1_used, glu_sb, sig_sb, lin_sb, gl_sb, act_sb, actT_ps, actT_sb, y_sb = [
            sem(n) for n in ("w1_used", "w2_used", "b1_used", "glu_sb", "sig_sb", "lin_sb", "gl_sb", "act_sb",
                             "actT_ps", "actT_sb", "y_sb")]
        rows_ps, added, late_sb, fin_sum, fin_sb, route_const = [
            sem(n) for n in ("rows_ps", "added", "late_sb", "fin_sum", "fin_sb", "route_const")]

        STEPS = [(c, l) for c in range(2) for l in range(LEVELS + 1)]
        PIECES = []
        for s, (c, l) in enumerate(STEPS):
            PIECES.append(("span", s))
            if l == 0:
                PIECES.append(("diag", c))
            if s and STEPS[s - 1][1] < LEVELS:
                PIECES.append(("score", s - 1))
            if s < 3:
                PIECES.append(("tail", (2, 0, 1)[s]))
            elif s < 3 + 2 * HEADS:
                PIECES.append(("outer", s - 3))
        PROJ = [(g, j) for j in range(4) for g in (BG, HV)] + [(CG, j) for j in range(4)]
        SCHEDULE = []
        for n, proj in enumerate(PROJ):
            SCHEDULE.append(("proj", proj))
            SCHEDULE += PIECES[4 * n:4 * n + 4]
        SCHEDULE += PIECES[4 * len(PROJ):]
        SCORES = [p for p in PIECES if p[0] in ("diag", "score")]

        def score_no(s):
            return SCORES.index(("score", s))

        def w_group(g):
            return w_in[0].rearrange("(t p) n -> p t n", p=P)[:, :, g * 512:(g + 1) * 512]

        def slots(ring, a):
            return ring[:, a:a + 2, :].rearrange("p a n -> p (a n)")

        w_sb = {g: cut(slots(ring, a), 512) for g, (ring, a) in {
            FX: (w1r, 4), IV: (w2r, 0), QG: (w1r, 6), OG: (w2r, 2), BG: (w1r, 0), HV: (w1r, 2),
            CG: (w1r, 4)}.items()}
        wout_sb = [cut(slots(w1r, 6), D), cut(slots(w2r, 0), D)]
        w1_v = expert_w1[0].rearrange("e (t p) n -> e t p n", p=P)
        w2_v = expert_w2[0].rearrange("e (r a p) n -> e r p a n", a=2, p=P)

        block = ctx.enter_context(nc.Block())

        def run_passes(eng, first, later):
            first(0)
            eng.wait_ge(max_sb, 1)
            most = eng.value_load(maxcount_i[0:1, 0:1], min_val=0, max_val=NT)
            with eng.If(most > CAP):
                with eng.Fori(1, PASSES) as c:
                    with eng.If(most > c * CAP):
                        later(c)

        def each_expert(eng, c, body, start=0):
            with eng.Fori(start, E // 2 - 1) as i:
                for k in range(2):
                    body(c, i, k, False)
            body(c, E // 2 - 1, 0, False)
            body(c, E // 2 - 1, 1, True)

        def num(c, i, k):
            return c * E + i * 2 + k

        def use(c, i):
            return c * (E // 2) + i

        @block.sync
        def _(sp):
            for i in range(2):
                sp.dma_start(x3[:, i, :], x_prompt[0, i * P:(i + 1) * P, :]).then_inc(x_in[i], 16)
            sp.dma_start(x3[0:NS, 2, :], x_sample[:, 0, :]).then_inc(x_in[2], 16)
            sp.dma_start(x3[NS:NS + NM, 2, :], meta_tokens).then_inc(x_in[2], 16)
            sp.dma_start(w_sb[FX], w_group(FX)).then_inc(win_in[FX], 16)
            sp.dma_start(w_sb[IV], w_group(IV)).then_inc(win_in[IV], 16)
            sp.dma_start(w_sb[QG], w_group(QG)).then_inc(win_in[QG], 16)
            sp.dma_start(w_sb[OG], w_group(OG)).then_inc(win_in[OG], 16)
            sp.dma_start(w_sb[BG], w_group(BG)).then_inc(win_in[BG], 16)
            sp.dma_start(w_sb[HV], w_group(HV)).then_inc(win_in[HV], 16)
            sp.wait_ge(xT_ps, KT)
            for h in range(HEADS):
                sp.dma_start(s0[:, h], state_rec[0, :, h].rearrange("b k v -> k b v")).then_inc(s0_in, 16)
            sp.wait_ge(fx_ps, 3)
            sp.dma_start(w_sb[CG], w_group(CG)).then_inc(win_in[CG], 16)
            wout_v = w_out[0].rearrange("(t p) n -> p t n", p=P)
            sp.wait_ge(q_ps, HEADS)
            sp.dma_start(wout_sb[0], wout_v[:, 0:4, :]).then_inc(wout_in[0], 16)
            sp.wait_ge(iv_ps, 3)
            sp.dma_start(wout_sb[1], wout_v[:, 4:8, :]).then_inc(wout_in[1], 16)

            def load_w1(t, e):
                sp.dma_start(w1r[:, t, :], w1_v[e, t]).then_inc(w1_in[t], 16)

            def load_w2(k, r, e):
                sp.dma_start(cut(w2r[:, 4 * k + r, :], D), w2_v[e, r]).then_inc(w2_in[4 * k + r], 16)

            def load_b1(e):
                sp.dma_start(b1r, expert_b1[0, e:e + 1, :] if isinstance(e, int)
                             else expert_b1[0, bass.ds(e, 1), :]).then_inc(b1_in, 16)

            sp.wait_ge(og_ps, 3)
            load_w2(0, 2, 0)
            load_w2(0, 3, 0)
            sp.wait_ge(hv_ps, 4)
            for t in range(4):
                load_w1(t, 0)
            sp.wait_ge(cg_ps, 4)
            load_w1(4, 0)
            load_w1(5, 0)
            sp.wait_ge(snew_sb, 2 * HEADS)
            for h in range(HEADS):
                sp.dma_start(new_rec_sample[0, :, h].rearrange("b k v -> k b v"), s0[:, h]).then_inc(state_out, 16)
            sp.wait_ge(state_sb, 3)
            sp.dma_start(new_rec_prompt[0, 0].rearrange("h k v -> k h v"),
                         srec3[:, 0].rearrange("p (h v) -> p h v", h=HEADS)).then_inc(rec_out, 16)
            sp.wait_ge(os_ps, HEADS)
            sp.wait_ge(state_out, 16 * HEADS)
            load_w2(1, 2, 1)
            load_w2(1, 3, 1)
            sp.wait_ge(mixc_ps, 3)
            load_w1(6, 0)
            load_w1(7, 0)
            sp.wait_ge(yrec_sb, 3)
            load_w2(1, 0, 1)
            load_w2(1, 1, 1)
            sp.wait_ge(mix_ps, 3)
            load_w2(0, 0, 0)
            load_w2(0, 1, 0)
            load_b1(0)
            sp.wait_ge(b1_used, 1)
            load_b1(1)
            for t in range(8):
                sp.wait_ge(w1_used, t + 1)
                load_w1(t, 1)

            def load(c, i, k, last):
                n = num(c, i, k)
                e = i * 2 + k
                sp.wait_ge(b1_used, n)
                load_b1(e)
                for t in range(8):
                    sp.wait_ge(w1_used, n * 8 - 7 + t)
                    load_w1(t, e)
                for r in range(4):
                    sp.wait_ge(w2_used, n * 4 - 7 + r)
                    load_w2(k, r, e)

            run_passes(sp, lambda c: each_expert(sp, c, load, start=1), lambda c: each_expert(sp, c, load))
            for i in range(2):
                sp.wait_ge(fin_sb, i + 1)
                sp.dma_start(y_prompt[0, i * P:(i + 1) * P, :], h3[:, i]).then_inc(out_done, 16)
            sp.wait_ge(fin_sb, 3)
            sp.dma_start(y_sample[:, 0, :], h3[0:NS, 2]).then_inc(out_done, 16)
            sp.wait_ge(conv_out, 32)
            sp.wait_ge(rec_out, 16)
            sp.wait_ge(out_done, 16 * 3)


        @block.gpsimd
        def _(pool):
            linked = [0]

            def link(ins):
                linked[0] += 1
                ins.then_inc(pool_link, 1)
                pool.wait_ge(pool_link, linked[0])

            def keep(ap, op, base, chan, pattern, fill=0.0):
                return pool.affine_select(out=ap, in_=ap, compare_op=op, fill=fill, base=base,
                                          pattern=pattern, channel_multiplier=chan)

            pool.memset(ident, 0.0)
            link(pool.memset(small, 0.0))
            pool.memset(eps_col, EPS)
            keep(ident, ALU.not_equal, 0, 1, [[-1, P]], 1.0).then_inc(ident_sb, 1)
            for m in (prefix, suffix, suffix_s, spans, blocks):
                last = pool.memset(m, 1.0)
            link(last)
            keep(prefix, ALU.is_ge, 0, -1, [[1, P]])
            keep(suffix, ALU.is_ge, -1, 1, [[-1, P]])
            link(keep(cut(suffix_s, 32), ALU.is_ge, -1, 1, [[-32, HEADS], [-1, 32]]))
            link(keep(cut(suffix_s, 32), ALU.is_ge, NS + NM - 1, -1, [[32, HEADS], [0, 32]]))
            halves = []
            for l in range(LEVELS):
                h = 1 << l
                nb = P // (2 * h)
                sp_l = spans3[:, l].rearrange("p (m a i) -> p m a i", a=2, i=h)
                bl_l = blocks3[:, l].rearrange("p (m a i) -> p m a i", a=2, i=h)
                halves.append((h, nb, sp_l, bl_l))
            for h, nb, sp_l, bl_l in halves:
                keep(sp_l[:, :, 1], ALU.is_ge, -h, 1, [[-2 * h, nb], [0, h]])
                keep(sp_l[:, :, 0], ALU.is_ge, -1, 1, [[-2 * h, nb], [-1, h]])
                keep(bl_l[:, :, 1], ALU.is_ge, 0, 1, [[-2 * h, nb], [0, h]])
                last = pool.memset(bl_l[:, :, 0], 0.0)
            link(last)
            for h, nb, sp_l, bl_l in halves:
                keep(sp_l[:, :, 1], ALU.is_ge, h, -1, [[2 * h, nb], [1, h]])
                keep(sp_l[:, :, 0], ALU.is_ge, h - 1, -1, [[2 * h, nb], [0, h]])
                last = keep(bl_l[:, :, 1], ALU.is_ge, h - 1, -1, [[2 * h, nb], [0, h]])
            last.then_inc(pool_const, 1)

            pool.wait_ge(v_sb, 3)
            pool.wait_ge(own_sb, 1)
            pool.tensor_tensor(vdiag.rearrange("p (b v) -> p b v", b=NS),
                               bcast(vtok3[:, 2, 0:P].unsqueeze(1), [P, NS, P]),
                               bcast(own.unsqueeze(2), [P, NS, P]), ALU.mult).then_inc(vdiag_sb, 1)
            pool.wait_ge(s0_in, 16 * HEADS)
            pool.wait_ge(fS_sb, 1)
            for h in range(HEADS):
                pool.tensor_tensor(s0[:, h], s0[:, h], bcast(fS3[:, h].unsqueeze(2), [P, NS, P]), ALU.mult)\
                    .then_inc(s0f_sb, 1)

            pool.wait_ge(state_ps, 3)
            pool.wait_ge(outer_ps, 2 * HEADS)
            for i in range(2):
                pool.dma_start(h3[:, i], x_prompt[0, i * P:(i + 1) * P, :]).then_inc(xres_in, 16)
            pool.dma_start(h3[0:NS, 2], x_sample[:, 0, :]).then_inc(xres_in, 16)
            pool.wait_ge(o_ps, 2)
            pool.dma_start(gffn, norm_ffn[0].unsqueeze(0).to_broadcast([P, D])).then_inc(gffn_in, 16)
            pool.wait_ge(nconv_sb, 1)
            pool.wait_ge(yconv_sb, 4)
            pool.dma_start(b2_sb, expert_b2[0]).then_inc(b2_in, 16)
            pool.wait_ge(ncrow_sb, 1)
            pool.dma_start(new_conv_prompt[0, 0], ncrow[0:2, :]).then_inc(conv_out, 16)
            pool.dma_start(new_conv_sample[0].rearrange("b i n -> (b i) n"), ncrow[2:2 + 2 * NS, :])\
                .then_inc(conv_out, 16)
            pool.wait_ge(score_sb, len(SCORES))
            pool.iota(iota32, pattern=[[1, E]], base=0, channel_multiplier=0,
                      allow_small_or_imprecise_dtypes=True)
            pool.iota(iota64, pattern=[[1, CAP]], base=0, channel_multiplier=0,
                      allow_small_or_imprecise_dtypes=True)
            pool.memset(ones, 1.0)
            pool.memset(logits3[:, 2], 0.0)
            pool.memset(row_valid, 1.0)
            pool.memset(ones_b, 1.0)
            pool.memset(strict_b, 1.0)
            link(pool.memset(stack, 0.0))
            pool.affine_select(out=row_valid[:, 2:3], in_=row_valid[:, 2:3], compare_op=ALU.is_ge, fill=0.0,
                               base=NS - 1, pattern=[[0, 1]], channel_multiplier=-1)
            keep(strict_b, ALU.is_ge, -1, -1, [[1, P]])
            for g in range(4):
                last = keep(stack, ALU.not_equal, -32 * g, 1, [[-1, E]], 1.0)
                if g < 3:
                    link(last)
            last.then_inc(route_const, 1)
            pool.wait_ge(rows_ps, 6)
            pool.dma_start(gfin, norm_final.unsqueeze(0).to_broadcast([P, D])).then_inc(gfin_in, 16)

        @block.scalar
        def _(act):
            act.dma_start(gain_rows[0:8, :], norm_mix[0].rearrange("(t p) -> t p", p=P)).then_inc(gain_in, 16)
            act.dma_start(gain_rows[8:20, :], conv_w[0].rearrange("j (g p) -> (j g) p", p=P)).then_inc(gain_in, 16)
            act.dma_start(gain_rows[20:24, :], rec_norm[0].rearrange("(g p) -> g p", p=P)).then_inc(gain_in, 16)
            act.dma_start(crow, state_conv[0].rearrange("b i n -> (b i) n")).then_inc(crow_in, 16)
            act.dma_start(lb2, rec_lower_bound.rearrange("a n -> (a n)").unsqueeze(0).to_broadcast([P, D]))\
                .then_inc(lb_in, 16)
            act.wait_ge(ident_sb, 1)
            act.activation(small[:, 110:111], small[:, 111:112], ACT.Square)
            for i in range(3):
                r = TILE_ROWS[i]
                act.wait_ge(x_in[i], 32 if i == 2 else 16)
                last = act.activation(xn3[0:r, i], x3[0:r, i], ACT.Square, accum_out=ssq[0:r, i:i + 1])
                last.then_inc(x_sq, 1)
            act.wait_ge(x_sq, 3)
            for i in range(3):
                r = TILE_ROWS[i]
                act.activation(rstd[0:r, i:i + 1], ssq[0:r, i:i + 1], ACT.Sqrt, bias=eps_col[0:r],
                               scale=1.0 / D).then_inc(rstd_x, 1)
            act.dma_start(router3, router_w[0].rearrange("(t p) n -> p t n", p=P)).then_inc(const_in, 16)
            act.dma_start(rbrow, router_b).then_inc(const_in, 16)
            act.wait_ge(gains_sb, 1)
            for t in range(0, KT, 2):
                act.wait_ge(xT_ps, t + 1)
                act.activation(xT3[:, t], ps[:, t, 0:TOK], ACT.Copy, scale=gmix[:, t:t + 1]).then_inc(xT_act, 1)
            act.wait_ge(lb_sub, 1)
            act.activation(lb2, lb2, ACT.Exp).then_inc(lb_exp, 1)
            for i in range(3):
                act.wait_ge(fx_ps, i + 1)
                act.activation(ftmp3[:, i, 0:WIDE[i]], ps[:, 2 + i, 0:WIDE[i]], ACT.Exp, scale=-1.0)\
                    .then_inc(fx_exp, 1)
            for i in range(3):
                act.wait_ge(f_sb, i + 1)
                act.activation(logf3[:, i, 0:WIDE[i]], ftmp3[:, i, 0:WIDE[i]], ACT.Ln).then_inc(logf_sb, 1)
            for i in range(3):
                act.wait_ge(iv_ps, i + 1)
                act.activation(vtok3[:, i, 0:WIDE[i]], ps[:, 5 + i, 0:WIDE[i]], ACT.Copy).then_inc(v_sb, 1)
            for h in range(HEADS):
                act.wait_ge(q_ps, h + 1)
                act.activation(qC3.rearrange("p c (h t) -> p c h t", h=HEADS)[:, :, h],
                               ps[:, h % 2, P0C:TOK].rearrange("p (c t) -> p c t", c=2), ACT.Copy)
                act.activation(qS3[:, h], ps[:, h % 2, 0:32], ACT.Copy).then_inc(q_sb, 1)
            for i in range(2):
                act.wait_ge(og_ps, i + 1)
                act.activation(sog3[:, i], ps[:, 2 + i, :], ACT.Exp, scale=-1.0).then_inc(og_exp, 1)
            act.wait_ge(og_ps, 3)
            act.wait_ge(f_sb, 3)
            act.activation(sogS, ps[:, 4, 0:P], ACT.Exp, scale=-1.0).then_inc(og_exp, 1)
            for i in range(2):
                act.wait_ge(kkT_ps, i + 1)
                act.activation(kkC3[:, i], ps[:, i, :], ACT.Copy).then_inc(kkT_sb, 1)
            act.wait_ge(kkT_ps, 3)
            act.activation(kS3, ps[:, 5, 0:P].rearrange("p (h b) -> p h b", h=HEADS)[:, :, 0:NS],
                           ACT.Copy).then_inc(kkT_sb, 1)
            tails = 0
            for what, a in SCHEDULE:
                if what == "proj" and a[0] == BG:
                    j = a[1]
                    act.wait_ge(bg_ps, j + 1)
                    if j:
                        act.wait_ge(bx_sb, j)
                    act.activation(ctmp, ps[:, 5, 0:TOK], ACT.Copy).then_inc(bg_sb, 1)
                if what == "span":
                    act.wait_ge(span_ps, a + 1)
                    if a >= 2:
                        act.wait_ge(ex_used, a - 1)
                    act.activation(ex3[:, a % 2], ps[:, a % 2, :], ACT.Exp).then_inc(span_exp, 1)
                if what == "tail":
                    tails += 1
                    act.wait_ge(tail_ps, tails)
                    if tails > 2:
                        act.wait_ge(khat_sb, tails - 2)
                    act.activation(tail3[:, tails % 2, 0:WIDE[a]], ps[:, 4, 0:WIDE[a]], ACT.Exp)\
                        .then_inc(tail_exp, 1)
            for c in range(2):
                act.wait_ge(o_ps, c + 1)
                act.activation(ex3[:, c], ps[:, c, :], ACT.Square).then_inc(osq_sb, 1)
            act.wait_ge(os_sb, 1)
            act.activation(tail3[:, 0, 0:P], oS, ACT.Square, accum_out=ossq[:, 8:9]).then_inc(osq_sb, 1)
            act.wait_ge(oss_sb, 2)
            act.wait_ge(osq_sb, 3)
            act.activation(orstd, ossq, ACT.Sqrt, bias=eps_col, scale=1.0 / P).then_inc(ortd_sb, 1)
            act.wait_ge(mix_ps, 1)
            for g in range(1, 4):
                act.activation(hs_parts[g - 1], ps[32 * g:32 * g + NS, 2, :], ACT.Copy).then_inc(hs_sb, 1)
            for n, i in enumerate(ORDER):
                r = [P, P, NS][i]
                act.wait_ge(h_sb, n + 1)
                act.activation(hn3[0:r, i], h3[0:r, i], ACT.Square, accum_out=hssq[0:r, i:i + 1]).then_inc(h_sq, 1)
                act.wait_ge(h_sq, n + 1)
                act.activation(hrstd[0:r, i:i + 1], hssq[0:r, i:i + 1], ACT.Sqrt, bias=eps_col[0:r],
                               scale=1.0 / D).then_inc(hrstd_act, 1)
            act.wait_ge(hnT_ps, 1)
            act.activation(hnT3[:, :, 2 * P:NT], ps[:, 3, 0:KT * NS].rearrange("p (t b) -> p t b", t=KT), ACT.Copy)
            for i in range(2):
                act.wait_ge(hnT_ps, i + 2)
                act.activation(hnT3[:, 0:4, i * P:(i + 1) * P],
                               ps[:, (0, 6)[i], :].rearrange("p (t b) -> p t b", t=4), ACT.Copy).then_inc(hnT_act, 1)
            act.wait_ge(logitT_ps, 1)
            act.activation(logitT, ps[:, 2, 0:NT], ACT.Copy).then_inc(logitT_sb, 1)
            act.wait_ge(gate_sub, 1)
            act.activation(gate4, gate4, ACT.Exp).then_inc(gate_exp, 1)

            def copy_xg(n):
                act.wait_ge(xg_ps, n + 1)
                act.activation(xg, ps[:, 2, :], ACT.Copy).then_inc(xg_sb, 1)

            def copy_xgT(n):
                act.wait_ge(xgT_ps, n + 1)
                act.activation(xgT3.rearrange("p (a q) s -> p q a s", a=2),
                               ps[:, 2, :].rearrange("p (q a s) -> p q a s", q=4, a=2), ACT.Copy)\
                    .then_inc(xgT_sb, 1)

            def expert(c, i, k, last):
                n = num(c, i, k)
                act.wait_ge(glu_sb, n + 1)
                act.activation(sig, glu, ACT.Sigmoid, scale=ALPHA).then_inc(sig_sb, 1)
                act.wait_ge(ohgT_ps, n + 1)
                act.activation(ohgT, ps[:, 3, 0:NT], ACT.Copy).then_inc(ohgT_sb, 1)
                if not last:
                    copy_xg(n + 1)
                act.wait_ge(actT_ps, n + 1)
                act.activation(actT3, ps[:, 4, :].rearrange("p (c s) -> p c s", c=4), ACT.Copy)\
                    .then_inc(actT_sb, 1)
                if not last:
                    copy_xgT(n + 1)
                act.wait_ge(w2_used, n * 4 + 4)
                act.activation(ysb, ps[:, 3, :], ACT.Copy).then_inc(y_sb, 1)

            def first_pass(c):
                act.wait_ge(conv_out, 32)
                copy_xg(0)
                copy_xgT(0)
                act.wait_ge(combT_ps, 1)
                act.activation(combT, ps[0:E, 5, 0:NT], ACT.Copy).then_inc(combT_sb, 1)
                each_expert(act, c, expert)

            def later_pass(c):
                copy_xg(c * E)
                copy_xgT(c * E)
                each_expert(act, c, expert)

            run_passes(act, first_pass, later_pass)
            act.wait_ge(fin_sum, 1)
            act.activation(late0, late[CAP:CAP + NS, :], ACT.Copy).then_inc(late_sb, 1)
            for i in range(3):
                r = [P, P, NS][i]
                if i == 2:
                    act.wait_ge(fin_sum, 2)
                act.activation(fsq[0:r], h3[0:r, i], ACT.Square, accum_out=fssq[0:r, i:i + 1]).then_inc(h_sq, 1)
                act.wait_ge(h_sq, 3 + i + 1)
                act.activation(frstd[0:r, i:i + 1], fssq[0:r, i:i + 1], ACT.Sqrt, bias=eps_col[0:r],
                               scale=1.0 / D).then_inc(hrstd_act, 1)

        @block.vector
        def _(dve):
            linked = [0]

            def link(ins):
                linked[0] += 1
                ins.then_inc(dve_link, 1)
                dve.wait_ge(dve_link, linked[0])

            dve.wait_ge(ident_sb, 1)
            eye = ident.rearrange("p (h b) -> p b h", b=32)[:, 0:NS]
            dve.tensor_reduce(own, eye, AX.X, ALU.add).then_inc(own_sb, 1)
            dve.tensor_reduce(head, cut(ident, 32), AX.X, ALU.add)
            link(dve.tensor_reduce(meta_of, cut(ident, 32)[:, :, NS:NS + NM], AX.X, ALU.add))
            dve.tensor_reduce(meta_row, meta_of, AX.X, ALU.add).then_inc(own_sb, 1)
            dve.wait_ge(gains_ps, 1)
            dve.tensor_copy(gains, ps[:, 7, 0:24]).then_inc(gains_sb, 1)
            dve.wait_ge(crow_ps, 1)
            dve.tensor_copy(cT4, ps[:, 6, 0:64].rearrange("p (g b i) -> p g b i", g=4, i=2)).then_inc(cT_sb, 1)
            for i in range(3):
                r = TILE_ROWS[i]
                dve.wait_ge(rstd_x, i + 1)
                link(dve.reciprocal(rstd[0:r, i:i + 1], rstd[0:r, i:i + 1]))
                dve.tensor_scalar(xn3[0:r, i], x3[0:r, i], rstd[0:r, i:i + 1], None, ALU.mult).then_inc(xn_sb, 1)
            dve.wait_ge(lb_in, 16)
            link(dve.tensor_tensor(lbtmp, lb3[:, 0], lb3[:, 1], ALU.max))
            dve.tensor_tensor(lb3, lb3, bcast(lbtmp.unsqueeze(1), [P, 2, 512]), ALU.subtract).then_inc(lb_sub, 1)
            dve.wait_ge(gains_sb, 1)
            for t in range(1, KT, 2):
                dve.wait_ge(xT_ps, t + 1)
                dve.tensor_scalar(xT3[:, t], ps[:, t, 0:TOK], gmix[:, t:t + 1], None, ALU.mult)\
                    .then_inc(xT_dve, 1)
            dve.wait_ge(lb_exp, 1)
            link(dve.tensor_tensor(lbtmp, lb3[:, 0], lb3[:, 1], ALU.add))
            link(dve.reciprocal(lbtmp, lbtmp))
            link(dve.tensor_tensor(lb3[:, 0], lb3[:, 0], lbtmp, ALU.mult))
            link(dve.tensor_scalar(lb3[:, 1], lb3[:, 0], -1.0, 1.0, ALU.mult, ALU.add))
            for h in range(HEADS):
                rows = slice(32 * h, 32 * h + 32)
                last = dve.tensor_copy(lb_s3[rows], lb3[rows, :, h * P:(h + 1) * P])
            link(last)
            for i in range(3):
                f = ftmp3[:, i, 0:WIDE[i]]
                bound = lb3 if i < 2 else lb_s3
                dve.wait_ge(fx_exp, i + 1)
                link(dve.tensor_scalar(f, f, 1.0, None, ALU.add))
                link(dve.reciprocal(f, f))
                link(dve.tensor_tensor(f, f, bound[:, 1], ALU.mult))
                dve.tensor_tensor(f, f, bound[:, 0], ALU.add).then_inc(f_sb, 1)
                dve.wait_ge(f_sb, i + 1)
                dve.tensor_scalar(kk3[:, i, 0:WIDE[i]], f, -1.0, 1.0, ALU.mult, ALU.add).then_inc(kk_sb, 1)
            for i in range(3):
                g = sog3[:, i] if i < 2 else sogS
                o = ps[:, 2 + i, :] if i < 2 else ps[:, 4, 0:P]
                dve.wait_ge(og_exp, i + 1)
                link(dve.tensor_scalar(g, g, 1.0, None, ALU.add))
                link(dve.reciprocal(g, g))
                dve.tensor_tensor(g, g, o, ALU.mult).then_inc(sog_sb, 1)
            dve.wait_ge(kkT_sb, 3)
            dve.tensor_scalar(fS3, kS3, -1.0, 1.0, ALU.mult, ALU.add).then_inc(fS_sb, 1)
            dve.wait_ge(v_sb, 3)
            dve.tensor_tensor(cut(v_heads, P), bcast(vtok3[:, 2, 0:P].unsqueeze(1), [P, HEADS, P]),
                              bcast(head.unsqueeze(2), [P, HEADS, P]), ALU.mult)

            tails = 0
            scores = 0
            dve.wait_ge(pool_const, 1)
            for what, a in SCHEDULE:
                if what == "proj" and a[0] == HV:
                    j = a[1]
                    dve.wait_ge(hv_ps, j + 1)
                    dve.wait_ge(bg_sb, j + 1)
                    dve.tensor_tensor(bx3[:, j], ctmp, ps[:, 6, 0:TOK], ALU.mult).then_inc(bx_sb, 1)
                    dve.wait_ge(bx_sb, j + 1)
                    y = yT3[:, j, P0C:TOK]
                    ys = yT3[:, j, 0:NS]
                    w = [gconv[:, 4 * n + j:4 * n + j + 1] for n in range(3)]
                    dve.tensor_scalar(y, bx3[:, j, P0C:TOK], w[2], None, ALU.mult)
                    link(dve.tensor_scalar(ys, bx3[:, j, 0:NS], w[2], None, ALU.mult))
                    dve.scalar_tensor_tensor(y, bx3[:, j, P0C - 1:TOK - 1], w[1], y, ALU.mult, ALU.add)
                    link(dve.scalar_tensor_tensor(ys, cT4[:, j, :, 1], w[1], ys, ALU.mult, ALU.add))
                    dve.scalar_tensor_tensor(y, bx3[:, j, P0C - 2:TOK - 2], w[0], y, ALU.mult, ALU.add)
                    dve.scalar_tensor_tensor(ys, cT4[:, j, :, 0], w[0], ys, ALU.mult, ALU.add).then_inc(conv_sb, 1)
                if what == "proj" and a[0] == CG:
                    j = a[1]
                    dve.wait_ge(cg_ps, j + 1)
                    dve.wait_ge(conv_sb, j + 1)
                    dve.tensor_tensor(yT3[:, j, 0:NS], yT3[:, j, 0:NS], ps[:, 7, 0:NS], ALU.mult)
                    dve.tensor_tensor(yT3[:, j, P0C:TOK], yT3[:, j, P0C:TOK], ps[:, 7, P0C:TOK], ALU.mult)\
                        .then_inc(yconv_sb, 1)
                if what == "span":
                    c, l = STEPS[a]
                    dve.wait_ge(span_exp, a + 1)
                    dve.wait_ge(q_sb, HEADS)
                    dve.wait_ge(kkT_sb, 2)
                    if l == LEVELS:
                        dve.tensor_tensor(qhat3[:, c], ex3[:, a % 2], qC3[:, c], ALU.mult)
                        dve.tensor_copy(decay_all[:, 4 * c:4 * c + 4],
                                        ex3[:, a % 2].rearrange("p (h t) -> p h t", h=HEADS)[:, :, P - 1])\
                            .then_inc(ex_used, 1)
                    else:
                        h = 1 << l
                        split = lambda ap, half: ap.rearrange("p (m a i) -> p m a i", a=2, i=h)[:, :, half]
                        if a >= 2 and STEPS[a - 2][1] < LEVELS:
                            dve.wait_ge(score_ps, score_no(a - 2) + 1)
                        if a >= 3 and STEPS[a - 2][1] == LEVELS:
                            dve.wait_ge(score_ps, score_no(a - 4) + 1)
                        dve.tensor_tensor(split(wl3[:, a % 2], 0), split(ex3[:, a % 2], 0),
                                          split(kkC3[:, c], 0), ALU.mult)
                        dve.tensor_tensor(split(wl3[:, a % 2], 1), split(ex3[:, a % 2], 1),
                                          split(qC3[:, c], 1), ALU.mult).then_inc(ex_used, 1)
                if what in ("diag", "score"):
                    c = a if what == "diag" else STEPS[a][0]
                    dve.wait_ge(score_ps, scores + 1)
                    if scores:
                        dve.wait_ge(score_sb, scores)
                    got = ps[:, 2 + scores % 2, :].rearrange("p (h t) -> p h t", h=HEADS)
                    into = sc3[:, c].rearrange("p (h t) -> p h t", h=HEADS)
                    if what == "diag":
                        ins = dve.tensor_tensor(into, got, bcast(ident.unsqueeze(1), [P, HEADS, P]), ALU.mult)
                    else:
                        m = blocks3[:, STEPS[a][1]].bitcast(U32)
                        ins = dve.copy_predicated(into, bcast(m.unsqueeze(1), [P, HEADS, P]), got)
                    ins.then_inc(score_sb, 1)
                    scores += 1
                if what == "tail":
                    tails += 1
                    dve.wait_ge(tail_exp, tails)
                    dve.wait_ge(kkT_ps, 3)
                    if a == 2:
                        dve.scalar_tensor_tensor(kk_meta[:, 0:P], tail3[:, tails % 2, 0:P], meta_row,
                                                 kk3[:, 2, 0:P], ALU.mult, ALU.mult).then_inc(khat_sb, 1)
                    else:
                        dve.tensor_tensor(kk3[:, a], kk3[:, a], tail3[:, tails % 2], ALU.mult).then_inc(khat_sb, 1)
                if what == "outer":
                    h, n = a // 2, a % 2
                    dve.wait_ge(outer_ps, a + 1)
                    dve.wait_ge(s0f_sb, h + 1)
                    half = s0[:, h, 4 * n:4 * n + 4]
                    dve.tensor_tensor(half, half, ps[:, 4, :].rearrange("p (b v) -> p b v", v=P), ALU.add)\
                        .then_inc(snew_sb, 1)
            dve.wait_ge(state_ps, 1)
            dve.tensor_copy(srec3[:, 0], ps[:, 5, :]).then_inc(state_sb, 1)
            dve.wait_ge(ex_used, len(STEPS))
            for c in range(2):
                dve.wait_ge(state_ps, c + 2)
                dve.wait_ge(state_sb, c + 1)
                if c:
                    dve.wait_ge(o_ps, 1)
                for h in range(HEADS):
                    at = slice(h * P, (h + 1) * P)
                    last = dve.scalar_tensor_tensor(srec3[:, 1 - c, at], srec3[:, c, at],
                                                    decay_all[:, 4 * c + h:4 * c + h + 1], ps[:, 6 + c, at],
                                                    ALU.mult, ALU.add)
                last.then_inc(state_sb, 1)
                if c == 0:
                    dve.tensor_copy(nconv3[:, :, 0:2], bx3[:, :, TOK - 2:TOK])
                    after = nconv3[:, :, 2:].rearrange("p g (b i) -> p g b i", i=2)
                    dve.tensor_copy(after[:, :, :, 0], cT4[:, :, :, 1])
                    dve.tensor_copy(after[:, :, :, 1], bx3[:, :, 0:NS]).then_inc(nconv_sb, 1)
            dve.wait_ge(os_ps, HEADS)
            link(dve.tensor_tensor(ssum.rearrange("p (b v) -> p b v", b=NS),
                                   ps[:, 2:4, :].rearrange("p a (b v) -> p (a b) v", v=P),
                                   bcast(own.unsqueeze(2), [P, NS, P]), ALU.mult))
            dve.tensor_reduce(oS, ssum.rearrange("p (b v) -> p v b", b=NS), AX.X, ALU.add).then_inc(os_sb, 1)
            for c in range(2):
                dve.wait_ge(osq_sb, c + 1)
                dve.tensor_reduce(ossq[:, 4 * c:4 * c + 4],
                                  ex3[:, c].rearrange("p (h v) -> p h v", h=HEADS), AX.X, ALU.add)\
                    .then_inc(oss_sb, 1)
            dve.wait_ge(ncrow_ps, 1)
            dve.tensor_copy(ncrow, ps[0:2 + 2 * NS, 5, :]).then_inc(ncrow_sb, 1)
            dve.wait_ge(ortd_sb, 1)
            link(dve.reciprocal(orstd, orstd))
            for c in range(2):
                by_head = lambda ap: ap.rearrange("p (h v) -> p h v", h=HEADS)
                link(dve.tensor_tensor(by_head(ex3[:, c]), by_head(ps[:, c, :]),
                                       bcast(orstd[:, 4 * c:4 * c + 4].unsqueeze(2), [P, HEADS, P]), ALU.mult))
                dve.tensor_tensor(sog3[:, c], ex3[:, c], sog3[:, c], ALU.mult).then_inc(yrec_sb, 1)
            dve.scalar_tensor_tensor(oS, oS, orstd[:, 8:9], sogS, ALU.mult, ALU.mult).then_inc(yrec_sb, 1)
            for c in range(2):
                dve.wait_ge(yT_ps, c + 1)
                at = TILE_COL[c]
                dve.tensor_tensor(yT3[:, 4:8, at:at + P],
                                  ps[:, (3, 0)[c], :].rearrange("p (h t) -> p h t", h=HEADS),
                                  bcast(grec.unsqueeze(2), [P, HEADS, P]), ALU.mult).then_inc(yTrec_sb, 1)
            dve.wait_ge(yT_ps, 3)
            dve.tensor_tensor(yT3[:, 4:8, 0:NS], ps[:, 1, 0:P].rearrange("p (h b) -> p h b", b=32)[:, :, 0:NS],
                              bcast(grec.unsqueeze(2), [P, HEADS, NS]), ALU.mult).then_inc(yTrec_sb, 1)
            dve.wait_ge(xres_in, 48)
            dve.wait_ge(gffn_in, 16)
            for n, i in enumerate(ORDER):
                r = [P, P, NS][i]
                dve.wait_ge(mix_ps, n + 1)
                if i < 2:
                    b = (6, 4)[i]
                    dve.tensor_tensor(h3[:, i], h3[:, i], ps[:, b:b + 2, :].rearrange("p a n -> p (a n)"),
                                      ALU.add).then_inc(h_sb, 1)
                else:
                    left, right = h3[0:NS, 2, 0:HALF], h3[0:NS, 2, HALF:D]
                    dve.tensor_tensor(left, left, ps[0:NS, 2, :], ALU.add)
                    dve.wait_ge(hs_sb, 1)
                    link(dve.tensor_tensor(right, right, hs_parts[0], ALU.add))
                    dve.wait_ge(hs_sb, 3)
                    dve.tensor_tensor(left, left, hs_parts[1], ALU.add)
                    dve.tensor_tensor(right, right, hs_parts[2], ALU.add).then_inc(h_sb, 1)
                dve.wait_ge(hrstd_act, n + 1)
                link(dve.reciprocal(hrstd[0:r, i:i + 1], hrstd[0:r, i:i + 1]))
                dve.scalar_tensor_tensor(hn3[0:r, i], h3[0:r, i], hrstd[0:r, i:i + 1], gffn[0:r],
                                         ALU.mult, ALU.mult).then_inc(hn_sb, 1)
            for i in range(2):
                dve.wait_ge(hnT_ps, i + 2)
                dve.tensor_copy(hnT3[:, 4:8, i * P:(i + 1) * P],
                                ps[:, (1, 7)[i], :].rearrange("p (t b) -> p t b", t=4)).then_inc(hnT_dve, 1)
            dve.wait_ge(route_const, 1)
            dve.wait_ge(logit_ps, 3)
            dve.tensor_copy(logits3[:, 0:2], ps[:, 7, 0:2 * E].rearrange("p (i e) -> p i e", e=E))
            link(dve.tensor_copy(logits3[0:NS, 2], ps[0:NS, 7, 2 * E:3 * E]))
            for i in range(3):
                last = dve.max(top8[:, i], logits3[:, i])
            link(last)
            for i in range(3):
                last = dve.max_index(idx8[:, i], top8[:, i], logits3[:, i])
            dve.tensor_tensor(gate4, top8[:, :, 0:TOPK], bcast(top8[:, :, 0:1], [P, 3, TOPK]), ALU.subtract)\
                .then_inc(gate_sub, 1)
            dve.wait_ge(gate_sub, 1)
            link(dve.tensor_copy(idxf, idx8))
            link(dve.tensor_tensor(eq_all, bcast(iota32.unsqueeze(1).unsqueeze(1), [P, 3, TOPK, E]),
                                   bcast(idxf[:, :, 0:TOPK].unsqueeze(3), [P, 3, TOPK, E]), ALU.is_equal))
            link(dve.tensor_reduce(member3, eq_all.rearrange("p i j e -> p i e j"), AX.X, ALU.add))
            link(dve.tensor_tensor(member3, member3, bcast(row_valid.unsqueeze(2), [P, 3, E]), ALU.mult))
            dve.tensor_copy(member_b3, member3).then_inc(member_sb, 1)
            dve.wait_ge(gate_exp, 1)
            link(dve.tensor_reduce(gsum, gate4, AX.X, ALU.add))
            link(dve.reciprocal(gsum, gsum))
            link(dve.tensor_tensor(gate4, gate4, bcast(gsum.unsqueeze(2), [P, 3, TOPK]), ALU.mult))
            link(dve.tensor_tensor(eq_all, eq_all, bcast(gate4.unsqueeze(3), [P, 3, TOPK, E]), ALU.mult))
            dve.tensor_reduce(comb3, eq_all.rearrange("p i j e -> p i e j"), AX.X, ALU.add).then_inc(comb_sb, 1)
            dve.wait_ge(pos_ps, 1)
            pos = ps[:, 6, 0:3 * E].rearrange("p (i e) -> p i e", e=E)
            link(dve.scalar_tensor_tensor(posm3, pos, 1.0, member3, ALU.add, ALU.mult))
            link(dve.tensor_scalar(posm3, posm3, -1.0, None, ALU.add))

            def one_hots(n, k, e):
                col = bass.ds(e, 1)
                dve.tensor_tensor(oh4[:, k], bcast(posm3[:, :, col], [P, 3, CAP]),
                                  bcast(iota64.unsqueeze(1), [P, 3, CAP]), ALU.is_equal).then_inc(oh_sb, 1)
                dve.wait_ge(oh_sb, n + 1)
                for half in range(2):
                    last = dve.tensor_tensor(ohg4[:, k, :, CAP * half:CAP * half + CAP], oh4[:, k],
                                             bcast(comb3[:, :, col], [P, 3, CAP]), ALU.mult)
                last.then_inc(ohg_sb, 1)

            def add_rows(nth):
                dve.wait_ge(rows_ps, nth * 3 + 1)
                dve.tensor_tensor(h3[:, 0], h3[:, 0], ps[:, 6:8, :].rearrange("p a n -> p (a n)"), ALU.add)\
                    .then_inc(added, 1)
                dve.wait_ge(rows_ps, nth * 3 + 2)
                dve.tensor_tensor(h3[:, 1], h3[:, 1], ps[:, 4:6, :].rearrange("p a n -> p (a n)"), ALU.add)\
                    .then_inc(added, 1)
                dve.wait_ge(rows_ps, nth * 3 + 3)
                dve.tensor_tensor(h3[0:NS, 2, 0:HALF], h3[0:NS, 2, 0:HALF], ps[0:NS, 3, :], ALU.add)
                dve.tensor_tensor(late[CAP:CAP + NS, :], late[CAP:CAP + NS, :], ps[CAP:CAP + NS, 3, :], ALU.add)\
                    .then_inc(added, 1)

            def expert(c, i, k, last, adds="before"):
                n = num(c, i, k)
                if not last:
                    if adds != "first":
                        dve.wait_ge(ohgT_ps, n)
                    one_hots(n + 1, 1 - k, i * 2 + k + 1)
                if adds == "before":
                    add_rows(n)
                if adds == "two":
                    add_rows(0)
                    dve.wait_ge(added, 3)
                    add_rows(1)
                dve.wait_ge(w1_used, n * 8 + 8)
                dve.tensor_scalar(glu, psA[:, 0:D:2], LIMIT, None, ALU.min).then_inc(glu_sb, 1)
                dve.tensor_scalar(lin, psA[:, 1:D:2], -LIMIT, LIMIT, ALU.max, ALU.min).then_inc(lin_sb, 1)
                dve.wait_ge(lin_sb, n + 1)
                dve.scalar_tensor_tensor(lin, lin, 1.0, glu, ALU.add, ALU.mult).then_inc(gl_sb, 1)
                dve.wait_ge(gl_sb, n + 1)
                dve.wait_ge(sig_sb, n + 1)
                dve.tensor_tensor(act, lin, sig, ALU.mult).then_inc(act_sb, 1)

            def first_pass(c):
                dve.wait_ge(rec_out, 16)
                one_hots(0, 0, 0)
                link(dve.tensor_reduce(maxcount, ps[:, 6, 3 * E:4 * E], AX.X, ALU.max))
                dve.tensor_copy(maxcount_i, maxcount).then_inc(max_sb, 1)
                link(dve.memset(late[CAP:CAP + NS, :], 0.0))
                expert(c, 0, 0, False, adds="first")
                expert(c, 0, 1, False, adds="two")
                each_expert(dve, c, expert, start=1)
                add_rows(E)

            def later_pass(c):
                dve.wait_ge(ohgT_ps, c * E)
                dve.tensor_scalar(posm3, posm3, -float(CAP), None, ALU.add).then_inc(pos_moved, 1)
                dve.wait_ge(pos_moved, c)
                one_hots(c * E, 0, 0)
                expert(c, 0, 0, False, adds="none")
                expert(c, 0, 1, False)
                each_expert(dve, c, expert, start=1)
                add_rows(c * E + E)

            run_passes(dve, first_pass, later_pass)
            dve.memset(small[:, 91:92], 0.0).then_inc(fin_sum, 1)
            dve.wait_ge(late_sb, 1)
            dve.tensor_tensor(h3[0:NS, 2, HALF:D], h3[0:NS, 2, HALF:D], late0, ALU.add).then_inc(fin_sum, 1)
            dve.wait_ge(gfin_in, 16)
            for i in range(3):
                r = [P, P, NS][i]
                dve.wait_ge(hrstd_act, 3 + i + 1)
                link(dve.reciprocal(frstd[0:r, i:i + 1], frstd[0:r, i:i + 1]))
                dve.scalar_tensor_tensor(h3[0:r, i], h3[0:r, i], frstd[0:r, i:i + 1], gfin[0:r],
                                         ALU.mult, ALU.mult).then_inc(fin_sb, 1)

        @block.tensor
        def _(pe):
            mm = pe.matmul
            pe.wait_ge(ident_sb, 1)
            pe.wait_ge(gain_in, 48)
            pe.transpose(ps[:, 7, 0:24], gain_rows, ident[0:24, 0:24]).then_inc(gains_ps, 1)
            pe.wait_ge(crow_in, 16)
            for g in range(4):
                last = pe.transpose(ps[:, 6, 16 * g:16 * g + 16], crow[:, g * P:(g + 1) * P],
                                    ident[0:2 * NS, 0:2 * NS])
            last.then_inc(crow_ps, 1)
            for i in range(3):
                pe.wait_ge(xn_sb, i + 1)
                if i == 0:
                    pe.wait_ge(gains_sb, 1)
                    pe.wait_ge(cT_sb, 1)
                for t in range(KT):
                    r, at = TILE_ROWS[i], TILE_COL[i]
                    last = pe.transpose(ps[:, t, at:at + r], xn3[0:r, i, t * P:(t + 1) * P], ident[0:r, 0:r])
                    if i == 2:
                        last.then_inc(xT_ps, 1)

            def rows_of(g, i, bank, done, first=False):
                at = TILE_COL[i]
                for t in range(KT):
                    if first:
                        pe.wait_ge((xT_act, xT_dve)[t % 2], max(t // 2 + 1, 2 - t % 2))
                    last = mm(ps[:, bank, :], xT3[:, t, at:at + P], w_sb[g][:, t, :],
                              start=(t == 0), stop=(t == KT - 1))
                last.then_inc(done, 1)

            def stacked(g, bank, done):
                for t in range(KT):
                    for h in range(HEADS):
                        last = mm(ps[32 * h:32 * h + 32, bank, 0:P], xT3[:, t, 0:32],
                                  w_sb[g][:, t, h * P:(h + 1) * P], start=(t == 0), stop=(t == KT - 1))
                last.then_inc(done, 1)

            def columns_of(g, j, bank, done):
                pe.wait_ge(win_in[g], 16)
                for t in range(KT):
                    last = mm(ps[:, bank, 0:TOK], w_sb[g][:, t, j * P:(j + 1) * P], xT3[:, t, :],
                              start=(t == 0), stop=(t == KT - 1))
                last.then_inc(done, 1)

            pe.wait_ge(win_in[FX], 16)
            for i in range(2):
                rows_of(FX, i, 2 + i, fx_ps, first=(i == 0))
            stacked(FX, 4, fx_ps)
            pe.wait_ge(win_in[IV], 16)
            for i in range(2):
                rows_of(IV, i, 5 + i, iv_ps)
            stacked(IV, 7, iv_ps)
            for h in range(HEADS):
                if h >= 2:
                    pe.wait_ge(q_sb, h - 1)
                columns_of(QG, h, h % 2, q_ps)
            pe.wait_ge(win_in[OG], 16)
            pe.wait_ge(fx_exp, 3)
            for i in range(2):
                rows_of(OG, i, 2 + i, og_ps)
            stacked(OG, 4, og_ps)
            pe.wait_ge(kk_sb, 3)
            pe.wait_ge(v_sb, 3)
            pe.wait_ge(q_sb, HEADS)
            for i in range(2):
                for h in range(HEADS):
                    last = pe.transpose(ps[:, i, h * P:(h + 1) * P], kk3[:, i, h * P:(h + 1) * P], ident)
                last.then_inc(kkT_ps, 1)
            pe.transpose(ps[:, 5, 0:P], kk3[:, 2, 0:P], ident).then_inc(kkT_ps, 1)
            pe.wait_ge(logf_sb, 3)
            pe.wait_ge(v_sb, 3)
            pe.wait_ge(pool_const, 1)

            scores = 0
            tails = 0
            for what, a in SCHEDULE:
                if what == "proj":
                    g, j = a
                    bank, done, used = {BG: (5, bg_ps, bg_sb), HV: (6, hv_ps, bx_sb), CG: (7, cg_ps, yconv_sb)}[g]
                    pe.wait_ge(*((used, j) if j else (kkT_sb, 3)))
                    columns_of(g, j, bank, done)
                if what == "span":
                    c, l = STEPS[a]
                    if a < 2:
                        pe.wait_ge(kkT_sb, a + 1)
                    else:
                        pe.wait_ge(span_exp, a - 1)
                    for h in range(HEADS):
                        last = mm(ps[:, a % 2, h * P:(h + 1) * P], logf3[:, c, h * P:(h + 1) * P],
                                  spans3[:, l] if l < LEVELS else prefix, start=True, stop=True)
                    last.then_inc(span_ps, 1)
                if what in ("diag", "score"):
                    if scores < 2:
                        pe.wait_ge(sog_sb, scores + 1)
                    else:
                        pe.wait_ge(score_sb, scores - 1)
                    if what == "diag":
                        pe.wait_ge(kkT_sb, 2)
                        left, right = kkC3[:, a], qC3[:, a]
                    else:
                        pe.wait_ge(ex_used, a + 1)
                        left = right = wl3[:, a % 2]
                    for h in range(HEADS):
                        at = slice(h * P, (h + 1) * P)
                        last = mm(ps[:, 2 + scores % 2, at], left[:, at], right[:, at], start=True, stop=True)
                    last.then_inc(score_ps, 1)
                    scores += 1
                if what == "tail":
                    if tails == 0:
                        pe.wait_ge(sog_sb, 3)
                        pe.wait_ge(kkT_sb, 3)
                    else:
                        pe.wait_ge(tail_exp, tails)
                    tails += 1
                    mm(ps[:, 4, 0:WIDE[a]], suffix if a < 2 else suffix_s, logf3[:, a, 0:WIDE[a]],
                       start=True, stop=True).then_inc(tail_ps, 1)
                if what == "outer":
                    h, n = a // 2, a % 2
                    rows_h = slice(32 * h, 32 * h + 32)
                    if a:
                        pe.wait_ge(snew_sb, a)
                    else:
                        pe.wait_ge(tail_exp, 3)
                        pe.wait_ge(vdiag_sb, 1)
                    mm(ps[:, 4, :], kk3[rows_h, 2, 0:P], vdiag[rows_h, n * 512:(n + 1) * 512],
                       start=True, stop=True).then_inc(outer_ps, 1)
            pe.wait_ge(khat_sb, 3)
            pe.wait_ge(bg_sb, 4)
            pe.wait_ge(bx_sb, 4)
            pe.wait_ge(yconv_sb, 4)
            for n in range(3):
                for h in range(HEADS):
                    at = slice(h * P, (h + 1) * P)
                    if n == 0:
                        last = mm(ps[:, 5, at], kk_meta[:, 0:P], v_heads[:, at], start=True, stop=True)
                    else:
                        last = mm(ps[:, 5 + n, at], kk3[:, n - 1, at], vtok3[:, n - 1, at], start=True, stop=True)
                last.then_inc(state_ps, 1)

            def recur(c):
                pe.wait_ge(state_sb, c + 1)
                for h in range(HEADS):
                    at = slice(h * P, (h + 1) * P)
                    mm(ps[:, c, at], sc3[:, c, at], vtok3[:, c, at], start=True, stop=False)
                    last = mm(ps[:, c, at], qhat3[:, c, at], srec3[:, c, at], start=False, stop=True)
                last.then_inc(o_ps, 1)

            pe.wait_ge(score_sb, len(SCORES))
            pe.wait_ge(snew_sb, 2 * HEADS)
            for h in range(HEADS):
                for n in range(2):
                    last = mm(ps[32 * h:32 * h + 32, 2 + n, :], qS3[:, h],
                              s0[:, h].rearrange("p b v -> p (b v)")[:, n * 512:(n + 1) * 512],
                              start=True, stop=True)
                last.then_inc(os_ps, 1)
            pe.wait_ge(ex_used, len(STEPS))
            recur(0)
            recur(1)
            pe.wait_ge(nconv_sb, 1)
            for g in range(4):
                last = pe.transpose(ps[0:2 + 2 * NS, 5, g * P:(g + 1) * P], nconv3[:, g], ident)
            last.then_inc(ncrow_ps, 1)

            def mix(i, first):
                for n in range(2):
                    for t in range(4):
                        k = t if first else 4 + t
                        last = mm(ps[:, (6, 4)[i] + n, :], yT3[:, k, TILE_COL[i]:TILE_COL[i] + P],
                                  wout_sb[k // 4][:, t, n * 512:(n + 1) * 512], start=(k == 0), stop=(k == KT - 1))
                return last

            def mix_samples(first):
                for t in range(4):
                    for n in range(2):
                        k = t if first else 4 + t
                        at = 64 * (t % 2) + 32 * n
                        last = mm(ps[at:at + NS, 2, :], yT3[:, k, 0:NS],
                                  wout_sb[k // 4][:, t, n * 512:(n + 1) * 512], start=(k < 2), stop=(k >= KT - 2))
                return last

            pe.wait_ge(wout_in[0], 16)
            pe.wait_ge(state_sb, 3)
            mix(0, True).then_inc(mixc_ps, 1)
            pe.wait_ge(ncrow_sb, 1)
            mix(1, True).then_inc(mixc_ps, 1)
            pe.wait_ge(os_sb, 1)
            mix_samples(True).then_inc(mixc_ps, 1)
            for c in range(2):
                pe.wait_ge(yrec_sb, c + 1)
                for h in range(HEADS):
                    last = pe.transpose(ps[:, (3, 0)[c], h * P:(h + 1) * P], sog3[:, c, h * P:(h + 1) * P], ident)
                last.then_inc(yT_ps, 1)
            pe.wait_ge(yrec_sb, 3)
            pe.transpose(ps[:, 1, 0:P], oS, ident).then_inc(yT_ps, 1)
            pe.wait_ge(wout_in[1], 16)
            pe.wait_ge(yTrec_sb, 3)
            mix_samples(False).then_inc(mix_ps, 1)
            mix(0, False).then_inc(mix_ps, 1)

            def turn_rows(n, i, bank):
                r = [P, P, NS][i]
                out = ps[:, bank:bank + 2, :].rearrange("p a n -> p (a n)")
                pe.wait_ge(hn_sb, n + 1)
                for t in range(KT):
                    last = pe.transpose(out[:, t * r:(t + 1) * r], hn3[0:r, i, t * P:(t + 1) * P], ident[0:r, 0:r])
                last.then_inc(hnT_ps, 1)

            turn_rows(0, 2, 3)
            mix(1, False).then_inc(mix_ps, 1)
            turn_rows(1, 0, 0)
            turn_rows(2, 1, 6)
            pe.wait_ge(hnT_act, 2)
            pe.wait_ge(hnT_dve, 2)
            pe.wait_ge(const_in, 32)
            pe.wait_ge(route_const, 1)
            order = [(0, 0), (1, 0), (0, 1), (1, 1)]

            def bias(half, n2):
                col = half * D + n2 * 512
                return mm(psA[64 * half:64 * half + 64, n2 * 512:(n2 + 1) * 512], ones[0:1, 0:CAP],
                          b1r[:, col:col + 512], start=True, stop=False)

            def biases(n):
                pe.wait_ge(b1_in, n * 16 + 16)
                for half, n2 in order:
                    last = bias(half, n2)
                last.then_inc(b1_used, 1)

            for t in range(KT):
                g = t % 4
                last = mm(ps[32 * g:32 * g + 32, 2, 0:NT], router3[:, t], hnT3[:, t], start=(t < 4), stop=(t >= 4))
            last.then_inc(logitT_ps, 1)
            pe.wait_ge(logitT_sb, 1)
            for i in range(3):
                r = [P, P, NS][i]
                out = ps[0:r, 7, i * E:(i + 1) * E]
                mm(out, ones[0:1, 0:r], rbrow, start=True, stop=False)
                mm(out, logitT[:, i * P:i * P + r], stack, start=False, stop=True).then_inc(logit_ps, 1)
            biases(0)
            pe.wait_ge(member_sb, 1)
            for i in range(3):
                for m in range(i + 1):
                    mm(ps[:, 6, i * E:(i + 1) * E], strict_b if m == i else ones_b, member_b3[:, m],
                       start=(m == 0), stop=(m == i))
            for m in range(3):
                last = mm(ps[:, 6, 3 * E:4 * E], ones_b, member_b3[:, m], start=(m == 0), stop=(m == 2))
            last.then_inc(pos_ps, 1)

            def pick(n, k):
                pe.wait_ge(oh_sb, n + 1)
                for i in range(3):
                    r = [P, P, NS][i]
                    for half in range(2):
                        last = mm(ps[64 * half:64 * half + 64, 2, :], oh4[0:r, k, i],
                                  hn3[0:r, i, half * HALF:(half + 1) * HALF], start=(i == 0), stop=(i == 2))
                last.then_inc(xg_ps, 1)

            def turn(n):
                pe.wait_ge(xg_sb, n + 1)
                for q in range(4):
                    last = pe.transpose(ps[:, 2, q * P:(q + 1) * P], xg[:, q * P:(q + 1) * P], ident)
                last.then_inc(xgT_ps, 1)

            def expert(c, i, k, last, adds="before"):
                n = num(c, i, k)
                pe.wait_ge(xgT_sb, n + 1)
                for t in range(KT):
                    pe.wait_ge(w1_in[t], n * 16 + 16)
                    for half, n2 in order:
                        col = half * D + n2 * 512
                        done = mm(psA[64 * half:64 * half + 64, n2 * 512:(n2 + 1) * 512],
                                  xgT3[:, t], w1r[:, t, col:col + 512], start=False, stop=(t == KT - 1))
                    done.then_inc(w1_used, 1)
                    if t < 3 and adds == "before":
                        y_rows(n, t, n)
                    if t < 3 and adds == "two":
                        y_rows(0, t, n)
                    if 3 <= t < 6 and adds == "two":
                        if t == 3:
                            pe.wait_ge(added, 3)
                        rows(1, t - 3, lambda half: combT, lambda half: b2_sb[:, half * HALF:(half + 1) * HALF])
                pe.wait_ge(ohg_sb, n + 1)
                if adds != "first":
                    pe.wait_ge(added, n * 3 + 3)
                for m in range(3):
                    r = [P, P, NS][m]
                    done = pe.transpose(ps[:, 3, m * P:m * P + r], ohg4[0:r, k, m], ident[0:r, 0:r])
                done.then_inc(ohgT_ps, 1)
                if not last:
                    pick(n + 1, 1 - k)
                pe.wait_ge(act_sb, n + 1)
                for q in range(4):
                    done = pe.transpose(ps[:, 4, q * P:(q + 1) * P], act[:, q * P:(q + 1) * P], ident)
                done.then_inc(actT_ps, 1)
                pe.wait_ge(actT_sb, n + 1)
                pe.wait_ge(ohgT_sb, n + 1)
                if not last:
                    pe.wait_ge(b1_in, n * 16 + 32)
                for t in range(KT):
                    if t % 2 == 0:
                        pe.wait_ge(w2_in[4 * k + t // 2], use(c, i) * 16 + 16)
                    for half in range(2):
                        col = (t % 2) * D + half * HALF
                        done = mm(ps[64 * half:64 * half + 64, 3, :],
                                  actT3[:, t % 4, 64 * (t // 4):64 * (t // 4) + 64],
                                  w2r[:, 4 * k + t // 2, col:col + HALF], start=(t == 0), stop=(t == KT - 1))
                    if t % 2:
                        done.then_inc(w2_used, 1)
                    if t < 4 and not last:
                        done = bias(*order[t])
                        if t == 3:
                            done.then_inc(b1_used, 1)
                if not last:
                    turn(n + 1)

            def rows(nth, m, left, right):
                r = [P, P, NS][m]
                out = [ps[:, 6:8, :], ps[:, 4:6, :]][m] if m < 2 else None
                for half in range(2):
                    to = out[:, half] if m < 2 else ps[CAP * half:CAP * half + NS, 3, :]
                    last = mm(to, left(half)[:, m * P:m * P + r], right(half), start=True, stop=True)
                last.then_inc(rows_ps, 1)

            def y_rows(nth, m, before):
                if m == 0:
                    pe.wait_ge(y_sb, before)
                if adds_before(nth):
                    if m == 0:
                        pe.wait_ge(added, nth * 3 - 2)
                    if m == 1:
                        pe.wait_ge(added, nth * 3)
                rows(nth, m, lambda half: ohgT[64 * half:64 * half + 64], lambda half: ysb[64 * half:64 * half + 64])

            def adds_before(nth):
                return not isinstance(nth, int) or nth > 0

            def rows_after(nth):
                for m in range(3):
                    y_rows(nth, m, nth)

            def first_pass(c):
                pick(0, 0)
                turn(0)
                pe.wait_ge(comb_sb, 1)
                for i in range(3):
                    r = [P, P, NS][i]
                    last = pe.transpose(ps[0:E, 5, i * P:i * P + r], comb3[0:r, i], ident[0:r, 0:r])
                last.then_inc(combT_ps, 1)
                expert(c, 0, 0, False, adds="first")
                pe.wait_ge(b2_in, 16)
                pe.wait_ge(combT_sb, 1)
                pe.wait_ge(max_sb, 1)
                expert(c, 0, 1, False, adds="two")
                each_expert(pe, c, expert, start=1)
                rows_after(E)

            def later_pass(c):
                pick(c * E, 0)
                turn(c * E)
                biases(c * E)
                expert(c, 0, 0, False, adds="none")
                expert(c, 0, 1, False)
                each_expert(pe, c, expert, start=1)
                rows_after(c * E + E)

            run_passes(pe, first_pass, later_pass)


INPUTS = ["x_prompt", "x_sample", "state_conv", "state_rec", "meta_tokens", "norm_mix", "w_in", "conv_w",
          "rec_lower_bound", "rec_norm", "w_out", "norm_ffn", "router_w", "router_b", "expert_w1", "expert_b1",
          "expert_w2", "expert_b2", "norm_final"]
OUTPUT_SHAPES = [(1, NP, D), (NS, 1, D), (1, 1, 2, HALF), (1, 1, HEADS, P, P), (1, NS, 2, HALF),
                 (1, NS, HEADS, P, P)]


def kernel(**inputs):
    import numpy as np
    import concourse.bacc as bacc
    from concourse.bass_utils import run_bass_kernel_spmd

    nc = bacc.Bacc("TRN2", target_bir_lowering=False, num_devices=1)
    arrays, args = {}, []
    for name in INPUTS:
        a = np.ascontiguousarray(inputs[name])
        arrays[f"in_{name}"] = a
        args.append(nc.dram_tensor(f"in_{name}", a.shape, mybir.dt.from_np(a.dtype), kind="ExternalInput").ap())
    for i, shape in enumerate(OUTPUT_SHAPES):
        args.append(nc.dram_tensor(f"out_{i}", shape, F32, kind="ExternalOutput").ap())
    build_step(nc, *args)
    r = run_bass_kernel_spmd(nc, [arrays], core_ids=[0])
    return tuple(r.results[0][f"out_{i}"] for i in range(len(OUTPUT_SHAPES)))
```
